# Optimizing a Trainium2 kernel written in Bass

```python
import math
import jax, jax.numpy as jnp
from jax import lax
import numpy as np

D_MODEL = 1024
BATCH = 1
SEQ = 256
DEPTH = 2

HEAD_DIM = 64
N_RET = 6
N_NSA = 6
N_KV = 2
HPG = N_NSA // N_KV
N_GM = 4
GM_DIM = 64
RET_W = N_RET * HEAD_DIM
NSA_W = N_NSA * HEAD_DIM
GM_W = N_GM * GM_DIM
MIX_W = RET_W + NSA_W + GM_W
RET_CHUNK = 128
CMP_LEN = 32
CMP_STRIDE = 16
SEL_BLOCK = 64
N_SEL = 16
WINDOW = 512
Q_BLOCK = 128
GM_CHUNK = 128
N_BUCKETS = 32
MAX_DISTANCE = 128
ROPE_THETA = 10000.0
D_FF = -(-8 * D_MODEL // (3 * 256)) * 256
SPLIT_SIZES = (RET_W, RET_W, RET_W, RET_W, NSA_W, 3 * 2 * N_KV * HEAD_DIM, 3 * N_NSA, 2 * GM_W)
IN_W = sum(SPLIT_SIZES)
EPS = 1e-6
BIG = 1e9
NEG = -1e30


def rms_norm(x, gain=None):
    xf = x.astype(jnp.float32)
    y = xf * lax.rsqrt(jnp.mean(xf * xf, axis=-1, keepdims=True) + EPS)
    if gain is not None:
        y = y * gain.astype(jnp.float32)
    return y.astype(x.dtype)

def rope(x, pos):
    half = x.shape[-1] // 2
    inv = ROPE_THETA ** (-jnp.arange(half, dtype=jnp.float32) / half)
    ang = pos.astype(jnp.float32)[:, None] * inv[None, :]
    cos = jnp.cos(ang)[None, :, None, :]
    sin = jnp.sin(ang)[None, :, None, :]
    x1 = x[..., :half].astype(jnp.float32)
    x2 = x[..., half:].astype(jnp.float32)
    return jnp.concatenate([x1 * cos - x2 * sin, x2 * cos + x1 * sin], axis=-1).astype(x.dtype)

def t5_bucket(dist):
    n = jnp.maximum(dist, 0)
    max_exact = N_BUCKETS // 2
    nf = jnp.maximum(n, 1).astype(jnp.float32)
    large = max_exact + (jnp.log(nf / max_exact) / math.log(MAX_DISTANCE / max_exact)
                         * (N_BUCKETS - max_exact)).astype(jnp.int32)
    large = jnp.minimum(large, N_BUCKETS - 1)
    return jnp.where(n < max_exact, n, large)

def masked_softmax(logits, mask):
    s = jnp.where(mask, logits.astype(jnp.float32), NEG)
    return jax.nn.softmax(s, axis=-1) * mask

def retention(q, k, v, g):
    B, T, H, d = q.shape
    C = RET_CHUNK
    nc = T // C
    f32 = jnp.float32
    to_chunks = lambda a: a.astype(f32).reshape(B, nc, C, H, d).transpose(0, 3, 1, 2, 4)
    qc, kc, vc = to_chunks(q), to_chunks(k * d ** -0.5), to_chunks(v)
    log_gamma = jnp.log(1.0 - 2.0 ** (-5.0 - jnp.arange(H, dtype=f32)))
    idx = jnp.arange(C, dtype=f32)
    diff = idx[:, None] - idx[None, :]
    decay = jnp.where(diff >= 0, jnp.exp(jnp.maximum(diff, 0.0)[None] * log_gamma[:, None, None]), 0.0)
    scores = jnp.einsum('bhcnd,bhcmd->bhcnm', qc, kc) * decay[:, None]
    inner = jnp.einsum('bhcnm,bhcme->bhcne', scores, vc)
    zeta = jnp.exp((C - 1 - idx)[None, :] * log_gamma[:, None])
    xi = jnp.exp((idx + 1)[None, :] * log_gamma[:, None])
    chunk_decay = jnp.exp(C * log_gamma)

    def step(R, kv):
        kt, vt = kv
        R_new = chunk_decay[None, :, None, None] * R + jnp.einsum('bhmd,bhme->bhde', kt * zeta[None, :, :, None], vt)
        return R_new, R

    R0 = jnp.zeros((B, H, d, d), f32)
    _, R_prev = lax.scan(step, R0, (kc.transpose(2, 0, 1, 3, 4), vc.transpose(2, 0, 1, 3, 4)))
    cross = jnp.einsum('bhcnd,cbhde->bhcne', qc, R_prev) * xi[None, :, None, :, None]
    o = (inner + cross).transpose(0, 2, 3, 1, 4).reshape(B, T, H, d)
    o = rms_norm(o) * jax.nn.silu(g.astype(f32))
    return o.reshape(B, T, H * d).astype(q.dtype)

def nsa(q, kv, gates, q_gain, k_gain, cmp_pe, cmp_w1, cmp_w2, rel_bias):
    B, T, _, d = q.shape
    out_dtype = q.dtype
    q = rms_norm(q, q_gain) * d ** -0.5
    q = q.reshape(B, T, N_KV, HPG, d).transpose(0, 2, 3, 1, 4)
    kv = kv.transpose(2, 3, 0, 4, 1, 5)

    n_cmp = (T - CMP_LEN) // CMP_STRIDE + 1
    blk_idx = np.arange(n_cmp)[:, None] * CMP_STRIDE + np.arange(CMP_LEN)[None, :]

    def compress(a, j):
        blocks = a[:, :, blk_idx] + cmp_pe[j]
        flat = blocks.reshape(B, N_KV, n_cmp, CMP_LEN * d)
        return jax.nn.gelu(flat @ cmp_w1[j]) @ cmp_w2[j]

    k_cmp = rms_norm(compress(kv[0, 0], 0), k_gain[0])
    v_cmp = compress(kv[0, 1], 1)
    cmp_end = jnp.asarray(blk_idx[:, -1], jnp.int32)

    n_slc = T // SEL_BLOCK
    n_sel = min(N_SEL, n_slc)
    k_sel = rms_norm(kv[1, 0], k_gain[1]).reshape(B, N_KV, n_slc, SEL_BLOCK, d)
    v_sel = kv[1, 1].reshape(B, N_KV, n_slc, SEL_BLOCK, d)
    cs = np.arange(n_cmp)[:, None] * CMP_STRIDE
    ss = np.arange(n_slc)[None, :] * SEL_BLOCK
    overlap = np.clip(np.minimum(cs + CMP_LEN, ss + SEL_BLOCK) - np.maximum(cs, ss), 0, None) // CMP_STRIDE
    overlap = jnp.asarray(overlap, jnp.float32)

    pad = ((0, 0), (0, 0), (WINDOW, 0), (0, 0))
    k_win = jnp.pad(rms_norm(kv[2, 0], k_gain[2]), pad)
    v_win = jnp.pad(kv[2, 1], pad)

    gates_t = jax.nn.sigmoid(gates.astype(jnp.float32)).reshape(B, T, N_KV, HPG, 3).transpose(0, 2, 3, 1, 4)
    bias_tab = rel_bias.reshape(N_BUCKETS, N_KV, HPG)
    bi = jnp.arange(B)[:, None, None, None]
    gi = jnp.arange(N_KV)[None, :, None, None]
    K_SEL = n_sel * SEL_BLOCK

    def block(i):
        q0 = i * Q_BLOCK
        qb = lax.dynamic_slice_in_dim(q, q0, Q_BLOCK, axis=3)
        t = q0 + jnp.arange(Q_BLOCK, dtype=jnp.int32)

        dist_c = t[:, None] - cmp_end[None, :]
        bias_c = bias_tab[t5_bucket(dist_c)].transpose(2, 3, 0, 1)
        s_c = jnp.einsum('bghqd,bgnd->bghqn', qb, k_cmp) + bias_c
        p_c = masked_softmax(s_c, dist_c >= 0)
        o_c = jnp.einsum('bghqn,bgnd->bghqd', p_c, v_cmp)

        imp = jnp.einsum('bghqn,nj->bgqj', p_c, overlap)
        cur = (t // SEL_BLOCK)[:, None]
        j = jnp.arange(n_slc)[None, :]
        imp = jnp.where((j == 0) | (j == cur) | (j == cur - 1), BIG, imp)
        imp = jnp.where(j > cur, -BIG, imp)
        _, sel = lax.top_k(imp, n_sel)
        ks = k_sel[bi, gi, sel].reshape(B, N_KV, Q_BLOCK, K_SEL, d)
        vs = v_sel[bi, gi, sel].reshape(B, N_KV, Q_BLOCK, K_SEL, d)
        pos = sel[..., None] * SEL_BLOCK + jnp.arange(SEL_BLOCK, dtype=jnp.int32)
        dist_s = (t[None, None, :, None, None] - pos).reshape(B, N_KV, Q_BLOCK, K_SEL)
        bias_s = bias_tab[t5_bucket(dist_s), gi].transpose(0, 1, 4, 2, 3)
        s_s = jnp.einsum('bghqd,bgqkd->bghqk', qb, ks) + bias_s
        p_s = masked_softmax(s_s, (dist_s >= 0)[:, :, None])
        o_s = jnp.einsum('bghqk,bgqkd->bghqd', p_s, vs)

        kw = lax.dynamic_slice_in_dim(k_win, q0, WINDOW + Q_BLOCK, axis=2)
        vw = lax.dynamic_slice_in_dim(v_win, q0, WINDOW + Q_BLOCK, axis=2)
        s_pos = q0 - WINDOW + jnp.arange(WINDOW + Q_BLOCK, dtype=jnp.int32)
        dist_w = t[:, None] - s_pos[None, :]
        mask_w = (dist_w >= 0) & (dist_w < WINDOW) & (s_pos[None, :] >= 0)
        bias_w = bias_tab[t5_bucket(dist_w)].transpose(2, 3, 0, 1)
        s_w = jnp.einsum('bghqd,bgkd->bghqk', qb, kw) + bias_w
        p_w = masked_softmax(s_w, mask_w)
        o_w = jnp.einsum('bghqk,bgkd->bghqd', p_w, vw)

        g = lax.dynamic_slice_in_dim(gates_t, q0, Q_BLOCK, axis=3)
        return g[..., 0:1] * o_c + g[..., 1:2] * o_s + g[..., 2:3] * o_w

    out = lax.map(block, jnp.arange(T // Q_BLOCK, dtype=jnp.int32))
    return out.transpose(1, 0, 4, 2, 3, 5).reshape(B, T, N_NSA * d).astype(out_dtype)

def spatial_gating(z, ws, b):
    B, T, _ = z.shape
    nch = T // GM_CHUNK
    z = jax.nn.gelu(z)
    u, v = jnp.split(z, 2, axis=-1)
    v = rms_norm(v.reshape(B, nch, GM_CHUNK, N_GM, GM_DIM))
    causal = jnp.tril(jnp.ones((GM_CHUNK, GM_CHUNK), ws.dtype))
    sv = jnp.einsum('gts,bcsgd->bctgd', ws * causal, v) + b.T[None, None, :, :, None]
    return (u.reshape(B, nch, GM_CHUNK, N_GM, GM_DIM) * sv).reshape(B, T, GM_W)

def first_inputs(seed: int = 0) -> dict:
    key = jax.random.key(seed)
    ks = jax.random.split(key, 16)
    f32 = jnp.float32
    nrm = lambda k, shape, scale: jax.random.normal(k, shape, f32) * scale
    return {
        "x": nrm(ks[0], (BATCH, SEQ, D_MODEL), 1.0),
        "attn_norm": 1.0 + nrm(ks[1], (DEPTH, D_MODEL), 0.02),
        "w_in": nrm(ks[2], (DEPTH, D_MODEL, IN_W), D_MODEL ** -0.5),
        "w_out": nrm(ks[3], (DEPTH, MIX_W, D_MODEL), MIX_W ** -0.5),
        "nsa_q_gain": 1.0 + nrm(ks[4], (DEPTH, HEAD_DIM), 0.02),
        "nsa_k_gain": 1.0 + nrm(ks[5], (DEPTH, 3, HEAD_DIM), 0.02),
        "cmp_pe": nrm(ks[6], (DEPTH, 2, CMP_LEN, HEAD_DIM), 0.1),
        "cmp_w1": nrm(ks[7], (DEPTH, 2, CMP_LEN * HEAD_DIM, HEAD_DIM), (CMP_LEN * HEAD_DIM) ** -0.5),
        "cmp_w2": nrm(ks[8], (DEPTH, 2, HEAD_DIM, HEAD_DIM), HEAD_DIM ** -0.5),
        "gm_ws": nrm(ks[9], (DEPTH, N_GM, GM_CHUNK, GM_CHUNK), GM_CHUNK ** -0.5),
        "gm_b": 1.0 + nrm(ks[10], (DEPTH, N_GM, GM_CHUNK), 0.02),
        "ffn_norm": 1.0 + nrm(ks[11], (DEPTH, D_MODEL), 0.02),
        "w_gate_up": nrm(ks[12], (DEPTH, D_MODEL, 2 * D_FF), D_MODEL ** -0.5),
        "w_down": nrm(ks[13], (DEPTH, D_FF, D_MODEL), D_FF ** -0.5),
        "rel_bias": nrm(ks[14], (N_BUCKETS, N_NSA), 0.5),
    }

def first_block(x, attn_norm, w_in, w_out, nsa_q_gain, nsa_k_gain, cmp_pe, cmp_w1, cmp_w2,
              gm_ws, gm_b, ffn_norm, w_gate_up, w_down, rel_bias):
    B, T, _ = x.shape
    pos = jnp.arange(T, dtype=jnp.int32)
    split_points = [int(s) for s in np.cumsum(SPLIT_SIZES)[:-1]]
    for l in range(DEPTH):
        h = rms_norm(x, attn_norm[l])
        proj = h @ w_in[l]
        r_q, r_k, r_v, r_g, n_q, n_kv, n_g, gm_z = jnp.split(proj, split_points, axis=-1)
        hs = (B, T, N_RET, HEAD_DIM)
        ret_o = retention(rope(r_q.reshape(hs), pos), rope(r_k.reshape(hs), pos),
                          r_v.reshape(hs), r_g.reshape(hs))
        nsa_o = nsa(n_q.reshape(B, T, N_NSA, HEAD_DIM),
                    n_kv.reshape(B, T, 3, 2, N_KV, HEAD_DIM),
                    n_g.reshape(B, T, N_NSA, 3),
                    nsa_q_gain[l], nsa_k_gain[l], cmp_pe[l], cmp_w1[l], cmp_w2[l], rel_bias)
        gm_o = spatial_gating(gm_z, gm_ws[l], gm_b[l])
        mix = jnp.concatenate([ret_o, nsa_o.astype(ret_o.dtype), gm_o.astype(ret_o.dtype)], axis=-1)
        x = x + (mix @ w_out[l]).astype(x.dtype)
        h = rms_norm(x, ffn_norm[l])
        gate, up = jnp.split(h @ w_gate_up[l], 2, axis=-1)
        x = x + ((jax.nn.silu(gate) * up) @ w_down[l]).astype(x.dtype)
    return x


N_EVEN = (DEPTH + 1) // 2
N_ODD = DEPTH // 2

HGRN_DIM = D_MODEL // 2
HGRN_HEAD_DIM = 128
HGRN_HEADS = HGRN_DIM // HGRN_HEAD_DIM
HGRN_CHUNK = 64

S5_DIM = D_MODEL - HGRN_DIM
S5_GROUP = 16
S5_GROUPS = S5_DIM // S5_GROUP
S5_STATE = 64
S5_DT_MIN = 1e-3
S5_DT_MAX = 1e-1

EVEN_IN = 4 * HGRN_DIM + S5_DIM

MLA_HEADS = 8
MLA_Q_RANK = 384
MLA_KV_RANK = 256
MLA_NOPE = 128
MLA_ROPE = 64
MLA_V = 128
MLA_QK = MLA_NOPE + MLA_ROPE
ODD_IN = MLA_Q_RANK + MLA_KV_RANK + MLA_ROPE

D_FF_2 = 2816
CONV_W = 3


def rmsnorm(x, g):
    xf = x.astype(jnp.float32)
    y = xf * lax.rsqrt(jnp.mean(xf * xf, axis=-1, keepdims=True) + EPS)
    return (y * g.astype(jnp.float32)).astype(x.dtype)

def hgrn2(q, f, i, g, lb, norm_g):
    f32 = jnp.float32
    B_, S_, _ = q.shape
    H, Dh, C = HGRN_HEADS, HGRN_HEAD_DIM, HGRN_CHUNK
    N = S_ // C
    lb = lb.astype(f32)
    forget = lb + (1.0 - lb) * jax.nn.sigmoid(f.astype(f32))
    key_in = 1.0 - forget

    def heads(t):
        return t.astype(f32).reshape(B_, N, C, H, Dh).transpose(0, 3, 1, 2, 4)

    qh, kh, vh = heads(q), heads(key_in), heads(i)
    b = jnp.cumsum(heads(jnp.log(forget)), axis=3)
    b_last = b[:, :, :, -1:, :]
    qd = qh * jnp.exp(b)
    kd = kh * jnp.exp(-b)
    causal = jnp.tril(jnp.ones((C, C), dtype=bool))
    att = jnp.where(causal, jnp.einsum('bhntd,bhnsd->bhnts', qd, kd), 0.0)
    o_intra = jnp.einsum('bhnts,bhnsv->bhntv', att, vh)
    d_state = jnp.einsum('bhnsd,bhnsv->bhndv', kh * jnp.exp(b_last - b), vh)
    decay = jnp.exp(b_last[:, :, :, 0, :])

    def step(state, inp):
        ds_n, dec_n = inp
        return dec_n[..., None] * state + ds_n, state

    s0 = jnp.zeros((B_, H, Dh, Dh), f32)
    _, s_start = lax.scan(step, s0, (d_state.transpose(2, 0, 1, 3, 4), decay.transpose(2, 0, 1, 3)))
    s_start = s_start.transpose(1, 2, 0, 3, 4)
    o = o_intra + jnp.einsum('bhntd,bhndv->bhntv', qd, s_start)
    o = o.transpose(0, 2, 3, 1, 4).reshape(B_, S_, H, Dh)
    o = o * lax.rsqrt(jnp.mean(o * o, axis=-1, keepdims=True) + EPS) * norm_g.astype(f32).reshape(H, Dh)
    return o.reshape(B_, S_, HGRN_DIM) * jax.nn.silu(g.astype(f32))

def s5(u, a_re, a_im, log_dt, b_re, b_im, c_re, c_im, d_skip, w_glu, b_glu):
    f32 = jnp.float32
    B_, S_, _ = u.shape
    G, P, Hc = S5_GROUPS, S5_STATE, S5_GROUP
    uf = u.astype(f32).reshape(B_, S_, G, Hc)
    ar, ai = a_re.astype(f32), a_im.astype(f32)
    dt = jnp.exp(log_dt.astype(f32))[:, None]
    mag = jnp.exp(ar * dt)
    abar_re, abar_im = mag * jnp.cos(ai * dt), mag * jnp.sin(ai * dt)
    den = ar * ar + ai * ai
    xr, xi = abar_re - 1.0, abar_im
    coef_re = ((xr * ar + xi * ai) / den)[..., None]
    coef_im = ((xi * ar - xr * ai) / den)[..., None]
    br, bi = b_re.astype(f32), b_im.astype(f32)
    bb_re = coef_re * br - coef_im * bi
    bb_im = coef_re * bi + coef_im * br
    bu_re = jnp.einsum('bsgh,gph->bsgp', uf, bb_re)
    bu_im = jnp.einsum('bsgh,gph->bsgp', uf, bb_im)
    a_seq_re = jnp.broadcast_to(abar_re, (1, S_, G, P))
    a_seq_im = jnp.broadcast_to(abar_im, (1, S_, G, P))

    def combine(left, right):
        a1r, a1i, b1r, b1i = left
        a2r, a2i, b2r, b2i = right
        return (a2r * a1r - a2i * a1i, a2r * a1i + a2i * a1r,
                a2r * b1r - a2i * b1i + b2r, a2r * b1i + a2i * b1r + b2i)

    _, _, s_re, s_im = lax.associative_scan(combine, (a_seq_re, a_seq_im, bu_re, bu_im), axis=1)
    y = (jnp.einsum('bsgp,ghp->bsgh', s_re, c_re.astype(f32))
         - jnp.einsum('bsgp,ghp->bsgh', s_im, c_im.astype(f32))
         + d_skip.astype(f32).reshape(G, Hc) * uf)
    z = jax.nn.gelu(y.reshape(B_, S_, S5_DIM))
    return z * jax.nn.sigmoid(z @ w_glu.astype(f32) + b_glu.astype(f32))

def even_mixer(hn, w_in, lb, hgrn_norm_g, a_re, a_im, log_dt, b_re, b_im, c_re, c_im,
               d_skip, w_glu, b_glu, w_out):
    proj = hn @ w_in
    q, f, i, g, u = jnp.split(proj, [HGRN_DIM, 2 * HGRN_DIM, 3 * HGRN_DIM, 4 * HGRN_DIM], axis=-1)
    y_a = hgrn2(q, f, i, g, lb, hgrn_norm_g).astype(hn.dtype)
    y_b = s5(u, a_re, a_im, log_dt, b_re, b_im, c_re, c_im, d_skip, w_glu, b_glu).astype(hn.dtype)
    return jnp.concatenate([y_a, y_b], axis=-1) @ w_out

def rotate(x, cos, sin):
    x1, x2 = jnp.split(x, 2, axis=-1)
    return jnp.concatenate([x1 * cos - x2 * sin, x1 * sin + x2 * cos], axis=-1)

def mla(hn, positions, w_in, q_norm_g, w_uq, kv_norm_g, w_ukv, w_out):
    B_, S_, _ = hn.shape
    H = MLA_HEADS
    proj = hn @ w_in
    cq, ckv, k_rope = jnp.split(proj, [MLA_Q_RANK, MLA_Q_RANK + MLA_KV_RANK], axis=-1)
    q = (rmsnorm(cq, q_norm_g) @ w_uq).reshape(B_, S_, H, MLA_QK)
    kv = (rmsnorm(ckv, kv_norm_g) @ w_ukv).reshape(B_, S_, H, MLA_NOPE + MLA_V)
    q_nope, q_rope = jnp.split(q, [MLA_NOPE], axis=-1)
    k_nope, v = jnp.split(kv, [MLA_NOPE], axis=-1)
    freqs = ROPE_THETA ** (-jnp.arange(0, MLA_ROPE, 2, dtype=jnp.float32) / MLA_ROPE)
    ang = positions.astype(jnp.float32)[..., None] * freqs
    cos = jnp.cos(ang)[:, :, None, :].astype(hn.dtype)
    sin = jnp.sin(ang)[:, :, None, :].astype(hn.dtype)
    q_rope = rotate(q_rope, cos, sin)
    k_rope = rotate(k_rope[:, :, None, :], cos, sin)
    q = jnp.concatenate([q_nope, q_rope], axis=-1)
    k = jnp.concatenate([k_nope, jnp.broadcast_to(k_rope, (B_, S_, H, MLA_ROPE))], axis=-1)
    scale = MLA_QK ** -0.5
    nb = S_ // Q_BLOCK
    qb = q.reshape(B_, nb, Q_BLOCK, H, MLA_QK).transpose(1, 0, 2, 3, 4)
    kpos = jnp.arange(S_)

    def attend(args):
        q_blk, blk = args
        s = jnp.einsum('bqhd,bkhd->bhqk', q_blk, k).astype(jnp.float32) * scale
        qpos = blk * Q_BLOCK + jnp.arange(Q_BLOCK)
        s = jnp.where(kpos[None, :] <= qpos[:, None], s, -jnp.inf)
        p = jax.nn.softmax(s, axis=-1).astype(v.dtype)
        return jnp.einsum('bhqk,bkhd->bqhd', p, v)

    o = lax.map(attend, (qb, jnp.arange(nb)))
    o = o.transpose(1, 0, 2, 3, 4).reshape(B_, S_, H * MLA_V)
    return o @ w_out

def conv_ffn(hn, w_in, conv_w, conv_b, w_out):
    a, u = jnp.split(hn @ w_in, 2, axis=-1)
    a = lax.conv_general_dilated(a, conv_w[:, None, :], window_strides=(1,),
                                 padding=[(CONV_W - 1, 0)],
                                 dimension_numbers=('NWC', 'WIO', 'NWC'),
                                 feature_group_count=D_FF_2) + conv_b
    return (jax.nn.silu(a) * u) @ w_out

def second_inputs(seed: int = 0) -> dict:
    key = jax.random.key(seed)
    ks = iter(jax.random.split(key, 40))
    nrm = lambda shape, s: jax.random.normal(next(ks), shape, jnp.float32) * s
    D = D_MODEL
    G, P, Hc = S5_GROUPS, S5_STATE, S5_GROUP
    x = nrm((BATCH, SEQ, D), 1.0)
    offset = jax.random.randint(next(ks), (BATCH, 1), 0, SEQ)
    positions = (offset + jnp.arange(SEQ)[None, :]).astype(jnp.int32)
    return {
        "x": x,
        "positions": positions,
        "norm_mix_g": 1.0 + nrm((DEPTH, D), 0.02),
        "norm_ffn_g": 1.0 + nrm((DEPTH, D), 0.02),
        "final_norm_g": 1.0 + nrm((D,), 0.02),
        "even_w_in": nrm((N_EVEN, D, EVEN_IN), D ** -0.5),
        "hgrn_lb_logits": nrm((N_EVEN + 1, HGRN_DIM), 0.1),
        "hgrn_norm_g": 1.0 + nrm((N_EVEN, HGRN_DIM), 0.02),
        "s5_a_re": -0.5 + nrm((N_EVEN, G, P), 0.01),
        "s5_a_im": jnp.pi * jnp.arange(P, dtype=jnp.float32) + nrm((N_EVEN, G, P), 0.01),
        "s5_log_dt": jax.random.uniform(next(ks), (N_EVEN, G), jnp.float32,
                                        math.log(S5_DT_MIN), math.log(S5_DT_MAX)),
        "s5_b_re": nrm((N_EVEN, G, P, Hc), (2 * Hc) ** -0.5),
        "s5_b_im": nrm((N_EVEN, G, P, Hc), (2 * Hc) ** -0.5),
        "s5_c_re": nrm((N_EVEN, G, Hc, P), (2 * P) ** -0.5),
        "s5_c_im": nrm((N_EVEN, G, Hc, P), (2 * P) ** -0.5),
        "s5_d": nrm((N_EVEN, S5_DIM), 1.0),
        "s5_w_glu": nrm((N_EVEN, S5_DIM, S5_DIM), S5_DIM ** -0.5),
        "s5_b_glu": nrm((N_EVEN, S5_DIM), 0.02),
        "even_w_out": nrm((N_EVEN, HGRN_DIM + S5_DIM, D), (HGRN_DIM + S5_DIM) ** -0.5),
        "odd_w_in": nrm((N_ODD, D, ODD_IN), D ** -0.5),
        "mla_q_norm_g": 1.0 + nrm((N_ODD, MLA_Q_RANK), 0.02),
        "mla_w_uq": nrm((N_ODD, MLA_Q_RANK, MLA_HEADS * MLA_QK), MLA_Q_RANK ** -0.5),
        "mla_kv_norm_g": 1.0 + nrm((N_ODD, MLA_KV_RANK), 0.02),
        "mla_w_ukv": nrm((N_ODD, MLA_KV_RANK, MLA_HEADS * (MLA_NOPE + MLA_V)), MLA_KV_RANK ** -0.5),
        "odd_w_out": nrm((N_ODD, MLA_HEADS * MLA_V, D), (MLA_HEADS * MLA_V) ** -0.5),
        "ffn_w_in": nrm((DEPTH, D, 2 * D_FF_2), D ** -0.5),
        "ffn_conv_w": nrm((DEPTH, CONV_W, D_FF_2), CONV_W ** -0.5),
        "ffn_conv_b": nrm((DEPTH, D_FF_2), 0.02),
        "ffn_w_out": nrm((DEPTH, D_FF_2, D), D_FF_2 ** -0.5),
    }

def second_block(x, positions, norm_mix_g, norm_ffn_g, final_norm_g,
              even_w_in, hgrn_lb_logits, hgrn_norm_g,
              s5_a_re, s5_a_im, s5_log_dt, s5_b_re, s5_b_im, s5_c_re, s5_c_im,
              s5_d, s5_w_glu, s5_b_glu, even_w_out,
              odd_w_in, mla_q_norm_g, mla_w_uq, mla_kv_norm_g, mla_w_ukv, odd_w_out,
              ffn_w_in, ffn_conv_w, ffn_conv_b, ffn_w_out):
    lower_bounds = jnp.cumsum(jax.nn.softmax(hgrn_lb_logits.astype(jnp.float32), axis=0), axis=0)
    h = x
    for layer in range(DEPTH):
        j = layer // 2
        hn = rmsnorm(h, norm_mix_g[layer])
        if layer % 2 == 0:
            mix = even_mixer(hn, even_w_in[j], lower_bounds[j], hgrn_norm_g[j],
                             s5_a_re[j], s5_a_im[j], s5_log_dt[j], s5_b_re[j], s5_b_im[j],
                             s5_c_re[j], s5_c_im[j], s5_d[j], s5_w_glu[j], s5_b_glu[j],
                             even_w_out[j])
        else:
            mix = mla(hn, positions, odd_w_in[j], mla_q_norm_g[j], mla_w_uq[j],
                      mla_kv_norm_g[j], mla_w_ukv[j], odd_w_out[j])
        h = h + mix
        h = h + conv_ffn(rmsnorm(h, norm_ffn_g[layer]), ffn_w_in[layer], ffn_conv_w[layer],
                         ffn_conv_b[layer], ffn_w_out[layer])
    return rmsnorm(h, final_norm_g)


def setup_inputs(seed=0):
    out = dict(first_inputs(seed))
    for name, value in second_inputs(seed + 1).items():
        if name != "x":
            out[name + "_2"] = value
    return out


def reference(
    x, attn_norm, w_in, w_out, nsa_q_gain, nsa_k_gain, cmp_pe, cmp_w1, cmp_w2, gm_ws, gm_b,
    ffn_norm, w_gate_up, w_down, rel_bias, positions_2, norm_mix_g_2, norm_ffn_g_2,
    final_norm_g_2, even_w_in_2, hgrn_lb_logits_2, hgrn_norm_g_2, s5_a_re_2, s5_a_im_2,
    s5_log_dt_2, s5_b_re_2, s5_b_im_2, s5_c_re_2, s5_c_im_2, s5_d_2, s5_w_glu_2, s5_b_glu_2,
    even_w_out_2, odd_w_in_2, mla_q_norm_g_2, mla_w_uq_2, mla_kv_norm_g_2, mla_w_ukv_2,
    odd_w_out_2, ffn_w_in_2, ffn_conv_w_2, ffn_conv_b_2, ffn_w_out_2,
):
    x = first_block(
        x, attn_norm, w_in, w_out, nsa_q_gain, nsa_k_gain, cmp_pe, cmp_w1, cmp_w2, gm_ws, gm_b,
        ffn_norm, w_gate_up, w_down, rel_bias,
    )
    return second_block(
        x, positions_2, norm_mix_g_2, norm_ffn_g_2, final_norm_g_2, even_w_in_2,
        hgrn_lb_logits_2, hgrn_norm_g_2, s5_a_re_2, s5_a_im_2, s5_log_dt_2, s5_b_re_2,
        s5_b_im_2, s5_c_re_2, s5_c_im_2, s5_d_2, s5_w_glu_2, s5_b_glu_2, even_w_out_2,
        odd_w_in_2, mla_q_norm_g_2, mla_w_uq_2, mla_kv_norm_g_2, mla_w_ukv_2, odd_w_out_2,
        ffn_w_in_2, ffn_conv_w_2, ffn_conv_b_2, ffn_w_out_2,
    )


_drawn_inputs = setup_inputs


def setup_inputs(seed=0):
    import zlib

    import numpy as np

    out = dict(_drawn_inputs(seed))
    spreads = {}
    factors = {'nsa_q_gain': 8.0,
     'nsa_k_gain': 8.0,
     'gm_b': 5.1,
     'norm_mix_g_2': 3.899,
     'norm_ffn_g_2': 3.883,
     'final_norm_g_2': 8.285,
     'hgrn_norm_g_2': 8.0,
     's5_a_re_2': 64.0,
     's5_a_im_2': 47.624,
     's5_log_dt_2': 50.2,
     's5_b_re_2': 64.0,
     's5_b_im_2': 64.0,
     's5_c_re_2': 64.0,
     's5_c_im_2': 64.0,
     's5_b_glu_2': 25.153,
     'mla_q_norm_g_2': 8.0,
     'mla_kv_norm_g_2': 8.0,
     'ffn_conv_b_2': 5.701}
    for name, (base, spread) in spreads.items():
        noise = np.random.default_rng([zlib.crc32(name.encode()), seed]).standard_normal(out[name].shape)
        drawn = base * np.exp(spread * noise) if base else spread * noise
        out[name] = __import__('jax').numpy.asarray(drawn.astype(out[name].dtype))
    for name, factor in factors.items():
        out[name] = (out[name] * factor).astype(out[name].dtype)
    return out
```

```python
from contextlib import ExitStack

import numpy as np

import concourse.bass as bass
from concourse import mybir

F32 = mybir.dt.float32
I32 = mybir.dt.int32
ALU = mybir.AluOpType
ACT = mybir.ActivationFunctionType
AX_X = mybir.AxisListType.X

P = 128
T = 256
NT = T // P
D = 1024
KC = D // P
DEPTH = 2
HD = 64
NH = 6
HPG = 3
RET_W = NH * HD
IN_W = 3218
O_RQ, O_RK, O_RV, O_RG = 0, RET_W, 2 * RET_W, 3 * RET_W
O_NQ = 4 * RET_W
O_KV = O_NQ + RET_W
O_NG = O_KV + 768
O_GM = O_NG + 18
GM_W = 256
NCMP = 15
CMP_LEN, CMP_STRIDE = 32, 16
FF = 2816
FC = FF // P
FSTEP = 2
NSTEP = FC // FSTEP
COLS = 512
EPS = 1e-6
NEG = -1e30
NBUCKET = 32
LINE = 512
HG = 4
HC = 64
NCH = T // HC
SD = 512
ST = 16
MH = 8
MQ, MKV, MR, MN, MV = 384, 256, 64, 128, 128
MQK = MN + MR
TWO_PI = 2.0 * np.pi
MAGIC = 12582912.0
CW1 = 6.28125
CW2 = float(np.float32(0.0019350051879882812))
CW3 = float(TWO_PI - CW1 - CW2)
PI_SAFE = 3.1415925


def shape_constants():
    f = np.float32
    p = np.arange(P)
    ident = np.eye(P, dtype=f)
    triu = (p[:, None] <= p[None, :]).astype(f)
    tri64 = np.concatenate([triu[:HC, :HC], triu[:HC, :HC]], 0)
    causal = np.zeros((P, T), f)
    causal[:, P:] = np.where(p[None, :] > p[:, None], f(NEG), f(0))
    half = HD // 2
    inv = (f(10000.0) ** (-np.arange(half, dtype=f) / f(half))).astype(f)
    ang = np.arange(T, dtype=f)[:, None] * inv[None]
    rope = np.stack([np.cos(ang), np.sin(ang)], 1).astype(f)
    rope = rope.reshape(NT, P, 2, half).transpose(1, 0, 2, 3)
    log_gamma = np.log(1.0 - 2.0 ** (-5.0 - np.arange(NH)))
    m, n = np.arange(T)[:, None], np.arange(T)[None]
    dec = np.where(n >= m, np.exp(np.maximum(n - m, 0)[None] * log_gamma[:, None, None]), 0.0) * HD ** -0.5
    decay = dec[:, :P, :].transpose(1, 0, 2).astype(f)
    dist = 255 - np.arange(LINE)
    me = NBUCKET // 2
    nf = np.maximum(dist, 1).astype(f)
    large = me + (np.log(nf / f(me)) / f(np.log(128 / me)) * f(NBUCKET - me)).astype(np.int32)
    bucket = np.where(dist < me, np.maximum(dist, 0), np.minimum(large, NBUCKET - 1))
    onehot = np.zeros((NBUCKET + 1, LINE), f)
    onehot[np.where(dist >= 0, bucket, NBUCKET), np.arange(LINE)] = 1.0
    tok = np.arange(T)
    cend = np.arange(NCMP) * CMP_STRIDE + CMP_LEN - 1
    cmask = (tok[:, None] >= cend[None]).astype(f).reshape(NT, P, NCMP).transpose(1, 0, 2)
    gmask = (((p // 16) % 2)[:, None] == np.arange(2)[None]).astype(f)
    freq = (f(10000.0) ** (-np.arange(0, MR, 2, dtype=f) / f(MR))).astype(f)
    return {
        "const_ident": ident, "const_triu": triu, "const_tri64": tri64, "const_causal": causal,
        "const_rope": rope, "const_decay": decay, "const_onehot": onehot, "const_cmask": cmask,
        "const_gmask": gmask, "const_freq": np.tile(freq[None], (P, 1)),
    }


class Counts:

    def __init__(self):
        self.own, self.others = {}, {}

    def made(self, sem):
        self.own[sem.name] = self.own.get(sem.name, 0) + 1
        return self.own[sem.name]

    def next(self, sem, n=1):
        self.others[sem.name] = self.others.get(sem.name, 0) + n
        return self.others[sem.name]


class Banks:

    def __init__(self, tensor, full, free):
        self.t, self.full, self.free, self.at, self.n = tensor, full, free, {}, 0

    def turn(self):
        return self.free[self.n % len(self.free)], self.n // len(self.free)

    def fill(self, name):
        self.at[name] = self.n
        self.n += 1
        return self.bank(name)

    def bank(self, name):
        return self.t[:, self.at[name] % len(self.full), :]

    def fills(self, name):
        return self.full[self.at[name] % len(self.full)], 1

    def filled(self, name):
        return self.full[self.at[name] % len(self.full)], self.at[name] // len(self.full) + 1

    def frees(self, name):
        return self.free[self.at[name] % len(self.free)], 1

    def freed(self, name):
        return self.free[self.at[name] % len(self.free)], self.at[name] // len(self.free) + 1


class Stream:

    def __init__(self, tensor, landed, manifest, order):
        self.t, self.landed, self.manifest, self.order = tensor, landed, manifest, order
        self.n, self.count, self.last = 0, [0] * len(landed), [None] * len(landed)

    def next(self, name):
        self.slot = s = self.n % len(self.landed)
        self.n += 1
        self.count[s] += 16 * len(self.manifest[name])
        self.order.append((self, name, s, self.last[s]))
        return self.landed[s], self.count[s]

    def weights(self):
        return self.t[:, self.slot, :]

    def release(self, sem, value):
        self.last[self.slot] = (sem, value)


def build(nc, a, out):
    ctx = ExitStack()
    with ctx:
        def sb(name, shape, dt=F32):
            return ctx.enter_context(nc.sbuf_tensor(name, shape, dt))

        def sem(name):
            return ctx.enter_context(nc.semaphore(name))

        bias_line = nc.dram_tensor("bias_line", [NH, P, LINE], F32, kind="Internal")

        x = sb("x", [P, NT, D])
        rows = sb("rows", [P, NT, D])
        hT = sb("hT", [P, KC, T])
        NW, ND = 4, 2
        wslots = sb("wslots", [P, NW, KC * COLS])
        dslots = sb("dslots", [P, ND, FSTEP * D])
        ident = sb("ident", [P, P])
        triu = sb("triu", [P, P])
        tri64 = sb("tri64", [P, HC])
        causal = sb("causal", [P, T])
        rope = sb("rope", [P, NT, 2, HD // 2])
        cmask = sb("cmask", [P, NT, NCMP])
        gmask = sb("gmask", [P, 2])
        freq = sb("freq", [P, MR // 2])
        NVEC = 97
        vecs = sb("vecs", [P, 3, NVEC])
        V_ATTN, V_FFN, V_MIX2, V_FFN2, V_MQ, V_MKV, V_GLU, V_SD, V_LB, V_GMB, V_HG = 0, 16, 32, 48, 64, 67, 69, 73, 77, 85, 93
        relb = sb("relb", [NBUCKET + 1, NH])
        mhalf = sb("mhalf", [P, 64])
        halfpi = sb("halfpi", [P, 1])
        ss = sb("ss", [P, 64])
        rs = sb("rs", [P, 64])
        sg = sb("sg", [P, 2, T])
        cv = sb("cv", [P, 2, T])
        lbt = sb("lbt", [P, 16])
        posi = sb("posi", [P, NT], I32)
        hid = sb("hid", [P, 4, T])

        ARENA = 23200
        arena = sb("arena", [P, ARENA])

        class Carve:
            def __init__(self):
                self.at = 0

            def __call__(self, pattern=None, n=0, rows=P, **dims):
                v = arena[0:rows, self.at:self.at + n]
                self.at += n
                assert self.at <= ARENA, self.at
                return v.rearrange(pattern, **dims) if pattern else v

        c1 = Carve()
        proj = c1("p (t n) -> p t n", NT * IN_W, t=NT)
        decay = c1("p (h n) -> p h n", NH * T, h=NH)
        bias = c1("p (h n) -> p h n", NH * 3 * P, h=NH)
        peT = c1("p (j k) -> p j k", 2 * DEPTH * CMP_LEN, rows=HD, j=2 * DEPTH)
        gains = c1("p (l k d) -> p l k d", DEPTH * 4 * HD, l=DEPTH, k=4)
        gmws = c1("p (l g n) -> p l g n", DEPTH * 4 * P, l=DEPTH, g=4)
        cw2 = c1("p (j n) -> p j n", DEPTH * 2 * HD, rows=HD, j=2 * DEPTH)
        qk = c1(None, 6 * T)
        qTr, kTr = (qk[:, k * 3 * T:(k + 1) * 3 * T].rearrange("p (b n) -> p b n", b=3) for k in range(2))
        p_sb = qk[:, 0:1024].rearrange("p (b n) -> p b n", b=2)
        qTn = c1("p (b n) -> p b n", 3 * T, b=3)
        kTn = c1("p (b n) -> p b n", 2 * T, b=2)
        kTc = c1(None, 16)
        blocks = c1(None, 2 * CMP_LEN * 30)
        blk = blocks[0:HD].rearrange("p (j l n) -> p j l n", j=2, l=CMP_LEN)
        pcT = blocks[0:16, 0:NT * NH * P].rearrange("p (q n) -> p q n", q=NT * NH)
        onehot, line = blocks[0:NBUCKET + 1, 0:LINE], blocks[0:NH, LINE:2 * LINE]
        raw = c1(None, 1024)
        aT = raw[0:HD].rearrange("p (j g n) -> p j g n", j=2, g=2)
        s_sb = raw.rearrange("p (b n) -> p b n", b=2)
        turned = c1(None, 1024)
        sT = turned[:, 0:768].rearrange("p (b n) -> p b n", b=2)
        pT = turned.rearrange("p (b n) -> p b n", b=2)
        qn = c1("p (t n) -> p t n", NT * RET_W, t=NT)
        kn = c1("p (t n) -> p t n", NT * 256, t=NT)
        wsT = c1("p (g n) -> p g n", 4 * P, g=4)
        vn = c1("p (t n) -> p t n", NT * GM_W, t=NT)
        h1 = c1("p (j n) -> p j n", 2 * 30, rows=HD, j=2)
        kc = c1(None, 256, rows=16)
        kcn = c1(None, P, rows=16)
        s_c = c1("p (q n) -> p q n", NT * NH * NCMP, q=NT * NH)
        nmax = c1(None, 32)
        lsum = c1("p (t h b) -> p t h b", 36, t=NT, h=NH)
        gate = c1("p (t h b) -> p t h b", 36, t=NT, h=NH)
        rsq = osum = qn
        free_rows = rows[:].rearrange("p t n -> p (t n)")
        rtmp = [free_rows[:, 0:768], free_rows[:, 768:1536], qk[:, 0:768], qk[:, 768:1536]]
        nsq = free_rows[:, 0:768]
        sk = free_rows[:, 1536:2048]
        vraw = qn.rearrange("p t n -> p (t n)")[:, 0:3 * P].rearrange("p (k n) -> p k n", k=3)

        c2 = Carve()
        cosT = c2("p (i n) -> p i n", ST * T, i=ST)
        sinT = c2("p (i n) -> p i n", ST * T, i=ST)
        eg = c2("p (t n) -> p t n", NT * 1024, t=NT)
        qTe = c2("p (h n) -> p h n", HG * T, h=HG)
        lf = c2("p (h n) -> p h n", HG * T, h=HG)
        key = c2("p (h n) -> p h n", HG * T, h=HG)
        bcum = c2("p (h n) -> p h n", HG * T, h=HG)
        eb = c2("p (h n) -> p h n", HG * T, h=HG)
        uT = c2("p (h n) -> p h n", HG * T, h=HG)
        kk = c2("p (t h n) -> p t h n", NT * HG * P, t=NT, h=HG)
        late = c2(None, 2048)
        att = late[:, 0:512].rearrange("p (q n) -> p q n", q=NT * HG)
        state = late[:, 512:2048].rearrange("p (c h n) -> p c h n", c=3, h=HG)
        bbT = c2("p (r i n) -> p r i n", 2 * 4 * P, r=2, i=4)
        cT = c2("p (r i n) -> p r i n", 2 * 4 * P, r=2, i=4)
        mag = c2(None, ST)
        ones = c2(None, HC)
        small2 = c2(None, 32)
        bu = qTe, lf
        m1, m2, m3, m4 = key, bcum, eb, late[:, 0:1024].rearrange("p (j n) -> p j n", j=4)
        wre, wim = (eg[:, k, :].rearrange("p (j n) -> p j n", j=4) for k in range(2))
        zT = kk.rearrange("p t h n -> p (t h n)").rearrange("p (h n) -> p h n", h=4)
        braw = [key[:, 0, :].rearrange("p (i h) -> p i h", i=ST), key[:, 1, :].rearrange("p (i h) -> p i h", i=ST)]
        bpad = [qTe[:, 0:2, :].rearrange("p a n -> p (a n)").rearrange("p (i n) -> p i n", i=ST),
                qTe[:, 2:4, :].rearrange("p a n -> p (a n)").rearrange("p (i n) -> p i n", i=ST)]
        craw = [lf[:, 0, :].rearrange("p (i n) -> p i n", i=4), lf[:, 1, :].rearrange("p (i n) -> p i n", i=4)]
        cpad = [bcum[:, 0:2, :].rearrange("p a n -> p (a n)").rearrange("p (i n) -> p i n", i=4),
                bcum[:, 2:4, :].rearrange("p a n -> p (a n)").rearrange("p (i n) -> p i n", i=4)]
        bx = [key[:, 2, :].rearrange("p (i h) -> p i h", i=ST), key[:, 3, :].rearrange("p (i h) -> p i h", i=ST)]
        prm = eb.rearrange("p h n -> p (h n)")[:, 0:20 * ST].rearrange("p (k i) -> p k i", i=ST)
        etmp = [e.rearrange("p (i n) -> p i n", i=ST) for e in
                (eg.rearrange("p t n -> p (t n)"), late)]

        c3 = Carve()
        oin = c3("p (t n) -> p t n", NT * 704, t=NT)
        osq = c3("p (t n) -> p t n", NT * 640, t=NT)
        kr = c3("p (t n) -> p t n", NT * P, t=NT)
        cqT = c3("p (c n) -> p c n", 3 * T, c=3)
        ckvT = c3("p (c n) -> p c n", 2 * T, c=2)
        krT = c3(None, T)
        qnT = c3("p (h n) -> p h n", MH * T, h=MH)
        knT = c3("p (h n) -> p h n", MH * T, h=MH)
        qr = c3("p (t n) -> p t n", NT * MH * MR, t=NT)
        qrT = c3("p (b n) -> p b n", 4 * T, b=4)
        vt = c3("p (t n) -> p t n", NT * MH * MV, t=NT)
        mtmp = c3("p (k n) -> p k n", 4 * 512, k=4)
        ms = c3("p (b n) -> p b n", 2 * T, b=2)
        mp = c3("p (b n) -> p b n", 2 * T, b=2)
        mpT = c3("p (b n) -> p b n", 2 * T, b=2)
        mang = c3("p (k t n) -> p k t n", 4 * NT * 32, k=4, t=NT)
        mst = c3(None, 64)
        fg = c3(None, D)

        accum = ctx.enter_context(nc.psum_tensor("accum", [P, 4, COLS], F32))
        work = ctx.enter_context(nc.psum_tensor("work", [P, 4, COLS], F32))
        acc = Banks(accum, [sem(f"acc_full{i}") for i in range(4)], [sem(f"acc_free{i}") for i in range(4)])
        wk = Banks(work, [sem(f"work_full{i}") for i in range(4)], [sem(f"work_free{i}") for i in range(4)])

        man = {}

        def panel(name, w, k, cols, view=COLS):
            c0, c1_ = cols
            n = c1_ - c0
            man[name] = [(lambda s, n=n, k=k: s[:, 0:(k // P) * n].rearrange("p (c n) -> p c n", n=n),
                          w[:, c0:c1_].rearrange("(c p) n -> p c n", p=P))]

        def ffn_panels(tag, w_in, w_out):
            wv = w_in.rearrange("(c p) n -> p c n", p=P)
            dv = w_out.rearrange("(c p) n -> p c n", p=P)
            for j in range(NSTEP):
                c = j * FSTEP * P
                man["gu", tag, j] = [
                    (lambda s, h=h: s.rearrange("p (c h n) -> p c h n", c=KC, h=2)[:, :, h, :],
                     wv[:, :, h * FF + c:h * FF + c + FSTEP * P]) for h in range(2)]
                man["dn", tag, j] = [(lambda s: s.rearrange("p (c n) -> p c n", c=FSTEP),
                                      dv[:, j * FSTEP:(j + 1) * FSTEP, :])]

        IN_COLS = [(c, min(c + COLS, IN_W)) for c in range(0, IN_W, COLS)]
        OUT_COLS = [(0, COLS), (COLS, D)]
        for l in range(DEPTH):
            for g, c in enumerate(IN_COLS):
                panel(("in", l, g), a["w_in"][l], D, c)
            man["w1", l] = [(lambda s, j=j: s[0:HD].rearrange("p (j l h) -> p j l h", j=2, l=CMP_LEN)[:, j],
                             a["cmp_w1"][l, j].rearrange("(l d) h -> d l h", d=HD)) for j in range(2)]
            for g, c in enumerate(OUT_COLS):
                panel(("out", l, g), a["w_out"][l], D, c)
            ffn_panels(l, a["w_gate_up"][l], a["w_down"][l])
            ffn_panels(2 + l, a["ffn_w_in_2"][l], a["ffn_w_out_2"][l])
        for g in range(5):
            panel(("even", g), a["even_w_in_2"][0], D, (g * COLS, (g + 1) * COLS))
        panel(("glu",), a["s5_w_glu_2"][0], SD, (0, SD))
        ODD_COLS = [(0, 512), (512, 704)]
        for g in range(2):
            panel(("out", 2, g), a["even_w_out_2"][0], D, OUT_COLS[g])
            panel(("out", 3, g), a["odd_w_out_2"][0], D, OUT_COLS[g])
            panel(("odd", g), a["odd_w_in_2"][0], D, ODD_COLS[g])
            panel(("uq", g), a["mla_w_uq_2"][0], MQ, (g * 768, (g + 1) * 768))
        panel(("ukv",), a["mla_w_ukv_2"][0], MKV, (0, 2048))

        order = []
        W = Stream(wslots, [sem(f"panel_in{i}") for i in range(NW)], man, order)
        Dn = Stream(dslots, [sem(f"down_in{i}") for i in range(ND)], man, order)

        names = """x_in params_in setup_ready vec_ready consts2_in s5_params_in line_ready line_out bias_in mla_in
          pe_chain act_chain dve_chain pool_chain
          x_ready norm_sums norm_scale normed hT_ready
          proj_ready rotated turned_ret decayed ret_mixed
          head_sums head_scale nsa_rows nsa_turned blocks_ready blocks_read gelu_ready
          h1_ready kc_raw kc_rows kTc_ready scores_ready probs_ready probsT_ready pv_done
          cmp_scores cmp_exp cmp_probs cmp_turned gates_ready gm_rows silu_ready mixed
          act_silu hid_ready down_done conv_in conv_done
          s5_dt s5_arg s5_trig lb_arg lb_exp s5_tables s5_pad s5_wT table_done
          hg_tanh hg_forget hg_ln hg_cum hg_exp hg_q hg_kk hg_kkT hg_att hg_state hg_out
          drive_ready states_ready states_used s5_y s5_z glu_tanh
          odd_ready odd_rows odd_T heads_ready qrope_rows qrope_T
          m_scores m_probs m_norm m_probsT m_pv pos_ready pos_arg pos_trig out_rows stored""".split()
        S = {n: sem(n) for n in names}

        P1 = [(ident[:], a["const_ident"]), (triu[:], a["const_triu"]), (tri64[:], a["const_tri64"]),
              (causal[:], a["const_causal"]), (rope[:], a["const_rope"]), (cmask[:], a["const_cmask"]),
              (gmask[:], a["const_gmask"]), (freq[:], a["const_freq"]),
              (onehot, a["const_onehot"]), (relb[0:NBUCKET, :], a["rel_bias"])]

        def vec(at, n, src, slot=0):
            P1.append((vraw[at:at + n, slot, :], src))

        vec(V_ATTN, 16, a["attn_norm"].rearrange("l (c p) -> (l c) p", p=P))
        vec(V_FFN, 16, a["ffn_norm"].rearrange("l (c p) -> (l c) p", p=P))
        vec(V_MIX2, 16, a["norm_mix_g_2"].rearrange("l (c p) -> (l c) p", p=P))
        vec(V_FFN2, 16, a["norm_ffn_g_2"].rearrange("l (c p) -> (l c) p", p=P))
        vec(V_MQ, 3, a["mla_q_norm_g_2"].rearrange("l (c p) -> (l c) p", p=P))
        vec(V_MKV, 2, a["mla_kv_norm_g_2"].rearrange("l (c p) -> (l c) p", p=P))
        vec(V_GLU, 4, a["s5_b_glu_2"].rearrange("l (c p) -> (l c) p", p=P))
        vec(V_SD, 4, a["s5_d_2"].rearrange("l (c p) -> (l c) p", p=P))
        vec(V_LB, 8, a["hgrn_lb_logits_2"].rearrange("l (c p) -> (l c) p", p=P))
        vec(V_GMB, 8, a["gm_b"].rearrange("l g p -> (l g) p"))
        vec(V_HG, 4, a["hgrn_norm_g_2"].rearrange("l (c p) -> (l c) p", p=P))
        for l in range(DEPTH):
            vec(0, 66, a["ffn_conv_w_2"][l].rearrange("w (c p) -> (w c) p", p=P), 1 + l)
            vec(66, 22, a["ffn_conv_b_2"][l:l + 1].rearrange("l (c p) -> (l c) p", p=P), 1 + l)
        peraw = rows[:, 0, 0:HD]
        P1.append((peraw, a["cmp_pe"].rearrange("l j k d -> (l j k) d")))
        P1.append((gains[:, :, 0, :].rearrange("p l d -> p l d"), a["nsa_q_gain"].partition_broadcast(P)))
        for l in range(DEPTH):
            P1.append((gains[:, l, 1:4, :], a["nsa_k_gain"][l].partition_broadcast(P)))
            P1.append((gmws[:, l, :, :], a["gm_ws"][l].rearrange("g t s -> t g s")))
            P1.append((cw2[:, 2 * l:2 * l + 2, :], a["cmp_w2"][l].rearrange("j d h -> d j h")))
        P1.append((decay, a["const_decay"]))
        P1.append((posi[:], a["positions_2"].rearrange("b (t p) -> p (b t)", p=P)))

        pview = lambda n: a[n][0].rearrange("(i g) p -> (g p) i", g=2)
        P2 = [(braw[r], a[n][0].rearrange("(i g) p h -> (g p) i h", g=2)) for r, n in enumerate(("s5_b_re_2", "s5_b_im_2"))]
        P2 += [(craw[r], a[n][0].rearrange("(i g) h p -> (g h) i p", i=4)) for r, n in enumerate(("s5_c_re_2", "s5_c_im_2"))]
        P2 += [(prm[:, 0, :], pview("s5_a_re_2")), (prm[:, 1, :], pview("s5_a_im_2"))]
        for g in range(2):
            P2.append((prm[64 * g:64 * g + 64, 2, :],
                       a["s5_log_dt_2"][0].rearrange("(i g) -> g i", g=2)[g].partition_broadcast(64)))

        block = ctx.enter_context(nc.Block())

        @block.tensor
        def _(pe):
            ln, own = Counts(), S["pe_chain"]
            mm = nc.tensor.matmul
            tr = nc.tensor.transpose

            def turn_rows(n, src, blocks):
                for t in range(NT):
                    for q in range(blocks // 4):
                        pe.wait_ge(*wk.turn())
                        b = wk.fill(("T", n, t, q))
                        for k in range(4):
                            c = (4 * q + k) * P
                            i = tr(b[:, k * P:(k + 1) * P], src[:, t, c:c + P], ident[:])
                        i.then_inc(*wk.fills(("T", n, t, q)))

            def rows_by(tag, lhs, kcs, name, width, key_):
                pe.wait_ge(*W.next(name))
                w = W.weights()[:, 0:kcs * width].rearrange("p (c n) -> p c n", n=width)
                for t in range(NT):
                    pe.wait_ge(*acc.turn())
                    b = acc.fill(key_ + (t,))
                    for c in range(kcs):
                        i = mm(b[:, 0:width], lhs[:, c, t * P:(t + 1) * P], w[:, c, :], start=(c == 0), stop=(c == kcs - 1))
                    i.then_inc(*acc.fills(key_ + (t,)))
                W.release(*acc.filled(key_ + (NT - 1,)))

            def hT_of(n):
                pe.wait_ge(S["normed"], ln.next(S["normed"]))
                turn_rows(n, rows, KC)
                pe.wait_ge(S["hT_ready"], ln.next(S["hT_ready"], 4))

            def out_product(l):
                pe.wait_ge(S["hT_ready"], ln.next(S["hT_ready"], 4))
                for g in range(2):
                    rows_by("out", hT, KC, ("out", l, g), COLS, ("out", l, g))

            def ffn(n, tag):
                hT_of(n)
                y = []
                for q in range(4):
                    pe.wait_ge(*acc.turn())
                    y.append(acc.fill(("y", tag, q)))

                def down(f):
                    if f % FSTEP == 0:
                        pe.wait_ge(*Dn.next(("dn", tag, f // FSTEP)))
                        down.w = Dn.weights().rearrange("p (c n) -> p c n", c=FSTEP)
                    pe.wait_ge(S["hid_ready"], ln.next(S["hid_ready"]))
                    for t in range(NT):
                        for h in range(2):
                            i = mm(y[2 * t + h], hid[:, f % 4, t * P:(t + 1) * P], down.w[:, f % FSTEP, h * COLS:(h + 1) * COLS],
                                   start=(f == 0), stop=(f == FC - 1))
                            if f == FC - 1:
                                i.then_inc(*acc.fills(("y", tag, 2 * t + h)))
                    if f < FC - 1:
                        i.then_inc(S["down_done"], 1)
                        ffn.downs += 1
                        if f % FSTEP == FSTEP - 1:
                            Dn.release(S["down_done"], ffn.downs)
                    else:
                        Dn.release(*acc.filled(("y", tag, 3)))

                for f in range(FC):
                    if f % FSTEP == 0:
                        pe.wait_ge(*W.next(("gu", tag, f // FSTEP)))
                        w = W.weights().rearrange("p (c h n) -> p c h n", c=KC, h=2)
                    pe.wait_ge(*wk.turn())
                    b = wk.fill(("gu", tag, f))
                    for h in range(2):
                        for c in range(KC):
                            i = mm(b[:, h * T:(h + 1) * T], w[:, c, h, (f % FSTEP) * P:(f % FSTEP + 1) * P], hT[:, c, :],
                                   start=(c == 0), stop=(c == KC - 1))
                    i.then_inc(*wk.fills(("gu", tag, f)))
                    if f % FSTEP == FSTEP - 1:
                        W.release(*wk.filled(("gu", tag, f)))
                    if f >= 1:
                        down(f - 1)
                down(FC - 1)

            ffn.downs = 0

            pe.wait_ge(S["params_in"], 16 * len(P1))
            pe.wait_ge(S["setup_ready"], ln.next(S["setup_ready"]))
            for k, n in enumerate((NVEC, 88, 88)):
                pe.wait_ge(*wk.turn())
                b = wk.fill(("vec", k))
                tr(b[:, 0:n], vraw[0:n, k, :], ident[0:n, 0:n]).then_inc(*wk.fills(("vec", k)))
            pe.wait_ge(*wk.turn())
            b = wk.fill(("pe",))
            tr(b[0:HD, 0:P], peraw, ident[:]).then_inc(*wk.fills(("pe",)))
            pe.wait_ge(*wk.turn())
            b = wk.fill(("line",))
            mm(b[0:NH, :], relb[:], onehot, start=True, stop=True).then_inc(*wk.fills(("line",)))

            for l in range(DEPTH):
                hT_of(("mix", l))
                for g, (c0, c1_) in enumerate(IN_COLS):
                    rows_by("in", hT, KC, ("in", l, g), c1_ - c0, ("in", l, g))
                pe.wait_ge(S["rotated"], ln.next(S["rotated"]))
                for t in range(NT):
                    for k, off in enumerate((O_RQ, O_RK)):
                        pe.wait_ge(*wk.turn())
                        b = wk.fill(("rT", l, t, k))
                        for q in range(3):
                            i = tr(b[:, q * P:(q + 1) * P], proj[:, t, off + q * P:off + (q + 1) * P], ident[:])
                        i.then_inc(*wk.fills(("rT", l, t, k)))
                pe.wait_ge(S["turned_ret"], ln.next(S["turned_ret"], 4))
                o = []
                for t in range(NT):
                    pe.wait_ge(*acc.turn())
                    o.append(acc.fill(("ro", l, t)))

                def ret_out(h):
                    pe.wait_ge(S["decayed"], ln.next(S["decayed"]))
                    s = sT[:, h % 2, :]
                    e = slice(h * HD, (h + 1) * HD)
                    v = [proj[:, t, O_RV + h * HD:O_RV + (h + 1) * HD] for t in range(NT)]
                    i = mm(o[0][:, e], s[:, 0:P], v[0], start=True, stop=True)
                    if h == NH - 1:
                        i.then_inc(*acc.fills(("ro", l, 0)))
                    mm(o[1][:, e], s[:, P:2 * P], v[0], start=True, stop=False)
                    i = mm(o[1][:, e], s[:, 2 * P:3 * P], v[1], start=False, stop=True)
                    if h == NH - 1:
                        i.then_inc(*acc.fills(("ro", l, 1)))
                    else:
                        i.then_inc(S["ret_mixed"], 1)

                for h in range(NH):
                    pe.wait_ge(*wk.turn())
                    b = wk.fill(("rs", l, h))
                    r = slice(HD * (h % 2), HD * (h % 2) + HD)
                    mm(b[:, 0:T], kTr[r, h // 2, 0:P], qTr[r, h // 2, :], start=True, stop=True)
                    mm(b[:, T:T + P], kTr[r, h // 2, P:T], qTr[r, h // 2, P:T], start=True, stop=True).then_inc(*wk.fills(("rs", l, h)))
                    if h >= 1:
                        ret_out(h - 1)
                ret_out(NH - 1)
                for j in range(2):
                    pe.wait_ge(*wk.turn())
                    b = wk.fill(("aT", l, j))
                    for g in range(2):
                        for t in range(NT):
                            c = O_KV + j * P + g * HD
                            i = tr(b[0:HD, (g * NT + t) * P:(g * NT + t + 1) * P], proj[:, t, c:c + HD], ident[:])
                    i.then_inc(*wk.fills(("aT", l, j)))
                pe.wait_ge(S["nsa_rows"], ln.next(S["nsa_rows"]))
                for t in range(NT):
                    pe.wait_ge(*wk.turn())
                    b = wk.fill(("nqT", l, t))
                    for q in range(3):
                        i = tr(b[:, q * P:(q + 1) * P], qn[:, t, q * P:(q + 1) * P], ident[:])
                    i.then_inc(*wk.fills(("nqT", l, t)))
                pe.wait_ge(*wk.turn())
                b = wk.fill(("nkT", l))
                for br in range(2):
                    for t in range(NT):
                        i = tr(b[:, (br * NT + t) * P:(br * NT + t + 1) * P], kn[:, t, br * P:(br + 1) * P], ident[:])
                i.then_inc(*wk.fills(("nkT", l)))
                pe.wait_ge(*wk.turn())
                b = wk.fill(("wsT", l))
                for g in range(4):
                    i = tr(b[:, g * P:(g + 1) * P], gmws[:, l, g, :], ident[:])
                i.then_inc(*wk.fills(("wsT", l)))
                pe.wait_ge(*W.next(("w1", l)))
                w1 = W.weights()[0:HD].rearrange("p (j l h) -> p j l h", j=2, l=CMP_LEN)
                pe.wait_ge(S["blocks_ready"], ln.next(S["blocks_ready"]))
                pe.wait_ge(*wk.turn())
                b = wk.fill(("h1", l))
                for j in range(2):
                    for k in range(CMP_LEN):
                        i = mm(b[0:HD, j * 32:j * 32 + 30], w1[:, j, k, :], blk[:, j, k, :], start=(k == 0), stop=(k == CMP_LEN - 1))
                i.then_inc(*wk.fills(("h1", l)))
                W.release(*wk.filled(("h1", l)))
                pe.wait_ge(S["h1_ready"], ln.next(S["h1_ready"]))
                pe.wait_ge(*wk.turn())
                b = wk.fill(("kc", l))
                for j in range(2):
                    for g in range(2):
                        c = (j * 2 + g) * HD
                        i = mm(b[0:NCMP, c:c + HD], h1[:, j, g * NCMP:(g + 1) * NCMP], cw2[:, 2 * l + j, :], start=True, stop=True)
                i.then_inc(*wk.fills(("kc", l)))
                pe.wait_ge(S["gm_rows"], ln.next(S["gm_rows"]))
                pe.wait_ge(*acc.turn())
                b = acc.fill(("gm", l))
                for g in range(4):
                    i = mm(b[:, g * P:(g + 1) * P].rearrange("p (t n) -> p t n", t=NT), wsT[:, g, :],
                           vn[:, :, g * HD:(g + 1) * HD], start=True, stop=True)
                i.then_inc(*acc.fills(("gm", l)))
                pe.wait_ge(S["kc_rows"], ln.next(S["kc_rows"]))
                pe.wait_ge(*wk.turn())
                b = wk.fill(("kcT", l))
                tr(b[:, 0:NCMP], kcn[0:NCMP, :], ident[0:NCMP, 0:NCMP]).then_inc(*wk.fills(("kcT", l)))
                pe.wait_ge(S["nsa_turned"], ln.next(S["nsa_turned"], 3))
                pe.wait_ge(S["kTc_ready"], ln.next(S["kTc_ready"]))
                for g in range(2):
                    pe.wait_ge(*wk.turn())
                    b = wk.fill(("sc", l, g))
                    r = slice(HD * g, HD * g + HD)
                    for t in range(NT):
                        for q in range(HPG):
                            c = (t * HPG + q) * 16
                            i = mm(b[:, c:c + NCMP], qTn[r, q, t * P:(t + 1) * P], kTc[r, 0:NCMP], start=True, stop=True)
                    i.then_inc(*wk.fills(("sc", l, g)))
                steps = [(t, h) for t in range(NT) for h in range(NH)]
                banks = {}

                def score(n):
                    t, h = steps[n]
                    g, q = h // HPG, h % HPG
                    r = slice(HD * g, HD * g + HD)
                    K = P * (t + 1)
                    pe.wait_ge(*wk.turn())
                    b = wk.fill(("s", l, n))
                    for br in range(2):
                        i = mm(b[:, br * T:br * T + K], qTn[r, q, t * P:(t + 1) * P], kTn[r, br, 0:K], start=True, stop=True)
                    i.then_inc(*wk.fills(("s", l, n)))

                def turn_probs(n):
                    t, h = steps[n]
                    pe.wait_ge(S["probs_ready"], ln.next(S["probs_ready"]))
                    pe.wait_ge(*wk.turn())
                    b = wk.fill(("pT", l, n))
                    for br in range(2):
                        for k in range(t + 1):
                            c = (br * (t + 1) + k) * P
                            i = tr(b[:, c:c + P], p_sb[:, n % 2, br * T + k * P:br * T + (k + 1) * P], ident[:])
                    i.then_inc(*wk.fills(("pT", l, n)))

                def weigh(n):
                    t, h = steps[n]
                    if h == 0:
                        for br in range(3):
                            pe.wait_ge(*acc.turn())
                            banks[br] = acc.fill(("no", l, t, br))
                        if t == 0:
                            pe.wait_ge(S["cmp_turned"], ln.next(S["cmp_turned"], 3))
                    g = h // HPG
                    e = slice(h * HD, (h + 1) * HD)
                    i = mm(banks[0][:, e], pcT[0:NCMP, t * NH + h, :], kc[0:NCMP, P + g * HD:P + (g + 1) * HD], start=True, stop=True)
                    if h == NH - 1:
                        i.then_inc(*acc.fills(("no", l, t, 0)))
                    pe.wait_ge(S["probsT_ready"], ln.next(S["probsT_ready"]))
                    for br in range(2):
                        c = O_KV + (1 + br) * 256 + P + g * HD
                        for k in range(t + 1):
                            i = mm(banks[1 + br][:, e], pT[:, n % 2, (br * (t + 1) + k) * P:(br * (t + 1) + k + 1) * P],
                                   proj[:, k, c:c + HD], start=(k == 0), stop=(k == t))
                        if h == NH - 1:
                            i.then_inc(*acc.fills(("no", l, t, 1 + br)))
                    if h < NH - 1:
                        i.then_inc(S["pv_done"], 1)

                for n in range(len(steps) + 2):
                    if n < len(steps):
                        score(n)
                    if n == 1:
                        pe.wait_ge(S["cmp_probs"], ln.next(S["cmp_probs"]))
                        for k in range(3):
                            pe.wait_ge(*wk.turn())
                            b = wk.fill(("pcT", l, k))
                            for q in range(4):
                                i = tr(b[0:NCMP, q * P:(q + 1) * P], s_c[:, 4 * k + q, :], ident[:])
                            i.then_inc(*wk.fills(("pcT", l, k)))
                    if 1 <= n <= len(steps):
                        turn_probs(n - 1)
                    if n >= 2:
                        weigh(n - 2)
                pe.wait_ge(S["mixed"], ln.next(S["mixed"]))
                turn_rows(("mixed", l), rows, KC)
                out_product(l)
                ffn(("ffn", l), l)
                if l == DEPTH - 1:
                    pe.wait_ge(S["s5_pad"], ln.next(S["s5_pad"]))
                    for r in range(2):
                        pe.wait_ge(*wk.turn())
                        b = wk.fill(("bbT", r))
                        for k in range(4):
                            i = tr(b[:, k * P:(k + 1) * P], bpad[r][:, 4 * k:4 * k + 4, :].rearrange("p i n -> p (i n)"), ident[:])
                        i.then_inc(*wk.fills(("bbT", r)))
                        pe.wait_ge(*wk.turn())
                        b = wk.fill(("cT", r))
                        for k in range(4):
                            i = tr(b[:, k * P:(k + 1) * P], cpad[r][:, k, :], ident[:])
                        i.then_inc(*wk.fills(("cT", r)))

            hT_of(("mix", 2))
            for g in (1, 0, 2, 3, 4):
                if g in (2, 3):
                    rows_by("even", hT, KC, ("even", g), COLS, ("even", g))
                    continue
                pe.wait_ge(*W.next(("even", g)))
                w = W.weights().rearrange("p (c n) -> p c n", c=KC)
                for q in range(2):
                    pe.wait_ge(*acc.turn())
                    b = acc.fill(("even", g, q))
                    for k in range(2):
                        for c in range(KC):
                            i = mm(b[:, k * T:(k + 1) * T], w[:, c, (2 * q + k) * P:(2 * q + k + 1) * P], hT[:, c, :],
                                   start=(c == 0), stop=(c == KC - 1))
                    i.then_inc(*acc.fills(("even", g, q)))
                W.release(*acc.filled(("even", g, 1)))
            pe.wait_ge(S["hg_q"], ln.next(S["hg_q"]))
            pe.wait_ge(*wk.turn())
            b = wk.fill(("att",))
            for n in range(NCH):
                t, po = n // 2, HC * (n % 2)
                for h in range(HG):
                    c = (t * HG + h) * HC
                    i = mm(b[po:po + HC, c:c + HC], bcum[:, h, n * HC:(n + 1) * HC], eb[:, h, n * HC:(n + 1) * HC], start=True, stop=True)
            i.then_inc(*wk.fills(("att",)))
            pe.wait_ge(S["hg_kk"], ln.next(S["hg_kk"]))
            for t in range(NT):
                pe.wait_ge(*wk.turn())
                b = wk.fill(("kkT", t))
                for h in range(HG):
                    i = tr(b[:, h * P:(h + 1) * P], key[:, h, t * P:(t + 1) * P], ident[:])
                i.then_inc(*wk.fills(("kkT", t)))
            pe.wait_ge(S["hg_kkT"], ln.next(S["hg_kkT"], 2))
            for n in range(NCH - 1):
                t, po = n // 2, HC * (n % 2)
                pe.wait_ge(*wk.turn())
                b = wk.fill(("ds", n))
                for h in range(HG):
                    i = mm(b[:, h * P:(h + 1) * P], kk[po:po + HC, t, h, :], eg[po:po + HC, t, h * P:(h + 1) * P], start=True, stop=True)
                i.then_inc(*wk.fills(("ds", n)))
            pe.wait_ge(S["hg_att"], ln.next(S["hg_att"]))
            o = []
            for t in range(NT):
                pe.wait_ge(*acc.turn())
                o.append(acc.fill(("eo", t)))
            for n in range(NCH):
                t, po = n // 2, HC * (n % 2)
                if n:
                    pe.wait_ge(S["hg_state"], ln.next(S["hg_state"]))
                for h in range(HG):
                    dst = o[t][po:po + HC, h * P:(h + 1) * P]
                    i = mm(dst, att[po:po + HC, t * HG + h, :], eg[po:po + HC, t, h * P:(h + 1) * P], start=True, stop=(n == 0))
                    if n:
                        i = mm(dst, eb[:, h, n * HC:(n + 1) * HC], state[:, n - 1, h, :], start=False, stop=True)
                if n % 2:
                    i.then_inc(*acc.fills(("eo", t)))
            for q in range(4):
                for j in range(4):
                    pe.wait_ge(*wk.turn())
                    b = wk.fill(("bu", q, j))
                    r = slice(32 * j, 32 * j + 32)
                    mm(b[:, 0:T], bbT[r, 0, q, :], uT[r, q, :], start=True, stop=True, tile_position=(32 * j, 0))
                    mm(b[:, T:2 * T], bbT[r, 1, q, :], uT[r, q, :], start=True, stop=True, tile_position=(32 * j, 0)).then_inc(*wk.fills(("bu", q, j)))
                pe.wait_ge(S["states_ready"], ln.next(S["states_ready"]))
                pe.wait_ge(*acc.turn())
                b = acc.fill(("sy", q))
                for j in range(4):
                    r = slice(32 * j, 32 * j + 32)
                    mm(b[r, 0:T], cT[:, 0, q, r], m1[:, j, :], start=True, stop=False)
                    i = mm(b[r, 0:T], cT[:, 1, q, r], m3[:, j, :], start=False, stop=True)
                i.then_inc(*acc.fills(("sy", q)))
            pe.wait_ge(*W.next(("glu",)))
            w = W.weights()[:, 0:4 * SD].rearrange("p (c n) -> p c n", c=4)
            pe.wait_ge(S["s5_z"], ln.next(S["s5_z"], 4))
            for q in range(2):
                pe.wait_ge(*acc.turn())
                b = acc.fill(("glu", q))
                for k in range(2):
                    for c in range(4):
                        i = mm(b[:, k * T:(k + 1) * T], w[:, c, (2 * q + k) * P:(2 * q + k + 1) * P], zT[:, c, :], start=(c == 0), stop=(c == 3))
                i.then_inc(*acc.fills(("glu", q)))
            W.release(*acc.filled(("glu", 1)))
            pe.wait_ge(S["mixed"], ln.next(S["mixed"]))
            for t in range(NT):
                pe.wait_ge(*wk.turn())
                b = wk.fill(("eT", t))
                for h in range(HG):
                    i = tr(b[:, h * P:(h + 1) * P], rows[:, t, h * P:(h + 1) * P], ident[:])
                i.then_inc(*wk.fills(("eT", t)))
            out_product(2)
            ffn(("ffn", 2), 2)

            hT_of(("mix", 3))
            for g, (c0, c1_) in enumerate(ODD_COLS):
                rows_by("odd", hT, KC, ("odd", g), c1_ - c0, ("odd", g))
            pe.wait_ge(S["odd_rows"], ln.next(S["odd_rows"]))
            for t in range(NT):
                pe.wait_ge(*wk.turn())
                b = wk.fill(("oT", t, 0))
                for c in range(3):
                    i = tr(b[:, c * P:(c + 1) * P], oin[:, t, c * P:(c + 1) * P], ident[:])
                i.then_inc(*wk.fills(("oT", t, 0)))
                pe.wait_ge(*wk.turn())
                b = wk.fill(("oT", t, 1))
                for c in range(2):
                    tr(b[:, c * P:(c + 1) * P], oin[:, t, MQ + c * P:MQ + (c + 1) * P], ident[:])
                tr(b[:, 2 * P:3 * P], kr[:, t, :], ident[:]).then_inc(*wk.fills(("oT", t, 1)))
            pe.wait_ge(S["odd_T"], ln.next(S["odd_T"], 4))
            for g in range(2):
                pe.wait_ge(*W.next(("uq", g)))
                w = W.weights()[:, 0:3 * 768].rearrange("p (c h n) -> p c h n", c=3, h=4)
                for q in range(2):
                    pe.wait_ge(*acc.turn())
                    b = acc.fill(("qn", g, q))
                    for k in range(2):
                        for c in range(3):
                            i = mm(b[:, k * T:(k + 1) * T], w[:, c, 2 * q + k, 0:MN], cqT[:, c, :], start=(c == 0), stop=(c == 2))
                    i.then_inc(*acc.fills(("qn", g, q)))
                pe.wait_ge(*acc.turn())
                b = acc.fill(("qr", g))
                for t in range(NT):
                    for c in range(3):
                        i = mm(b[:, t * T:(t + 1) * T].rearrange("p (h n) -> p h n", h=4), cqT[:, c, t * P:(t + 1) * P], w[:, c, :, MN:MQK],
                               start=(c == 0), stop=(c == 2))
                i.then_inc(*acc.fills(("qr", g)))
                W.release(*acc.filled(("qr", g)))
            pe.wait_ge(*W.next(("ukv",)))
            w = W.weights().rearrange("p (c h n) -> p c h n", c=2, h=MH)
            for q in range(4):
                pe.wait_ge(*acc.turn())
                b = acc.fill(("kn", q))
                for k in range(2):
                    for c in range(2):
                        i = mm(b[:, k * T:(k + 1) * T], w[:, c, 2 * q + k, 0:MN], ckvT[:, c, :], start=(c == 0), stop=(c == 1))
                i.then_inc(*acc.fills(("kn", q)))
            for t in range(NT):
                for h in range(2):
                    pe.wait_ge(*acc.turn())
                    b = acc.fill(("v", t, h))
                    for c in range(2):
                        i = mm(b.rearrange("p (h n) -> p h n", h=4), ckvT[:, c, t * P:(t + 1) * P], w[:, c, 4 * h:4 * h + 4, MN:MN + MV],
                               start=(c == 0), stop=(c == 1))
                    i.then_inc(*acc.fills(("v", t, h)))
            W.release(*acc.filled(("v", 1, 1)))
            pe.wait_ge(S["qrope_rows"], ln.next(S["qrope_rows"]))
            for t in range(NT):
                pe.wait_ge(*wk.turn())
                b = wk.fill(("qrT", t))
                for q in range(4):
                    i = tr(b[:, q * P:(q + 1) * P], qr[:, t, q * P:(q + 1) * P], ident[:])
                i.then_inc(*wk.fills(("qrT", t)))
            pe.wait_ge(S["qrope_T"], ln.next(S["qrope_T"], 2))
            pe.wait_ge(S["heads_ready"], ln.next(S["heads_ready"], 14))
            steps = [(t, h) for t in range(NT) for h in range(MH)]
            for n in range(len(steps) + 2):
                if n < len(steps):
                    t, h = steps[n]
                    K = P * (t + 1)
                    r = slice(HD * (h % 2), HD * (h % 2) + HD)
                    pe.wait_ge(*wk.turn())
                    b = wk.fill(("ms", n))
                    mm(b[:, 0:K], qnT[:, h, t * P:(t + 1) * P], knT[:, h, 0:K], start=True, stop=False)
                    mm(b[:, 0:K], qrT[r, h // 2, t * P:(t + 1) * P], krT[r, 0:K], start=False, stop=True).then_inc(*wk.fills(("ms", n)))
                if 1 <= n <= len(steps):
                    t, h = steps[n - 1]
                    pe.wait_ge(S["m_norm"], ln.next(S["m_norm"]))
                    pe.wait_ge(*wk.turn())
                    b = wk.fill(("mpT", n - 1))
                    for k in range(t + 1):
                        i = tr(b[:, k * P:(k + 1) * P], mp[:, (n - 1) % 2, k * P:(k + 1) * P], ident[:])
                    i.then_inc(*wk.fills(("mpT", n - 1)))
                if n >= 2:
                    t, h = steps[n - 2]
                    if h % 4 == 0:
                        pe.wait_ge(*acc.turn())
                        b2 = acc.fill(("mo", t, h // 4))
                    pe.wait_ge(S["m_probsT"], ln.next(S["m_probsT"]))
                    for k in range(t + 1):
                        i = mm(b2[:, (h % 4) * P:(h % 4 + 1) * P], vt[:, k, h * MV:(h + 1) * MV], mpT[:, n % 2, k * P:(k + 1) * P],
                               start=(k == 0), stop=(k == t))
                    if h % 4 == 3:
                        i.then_inc(*acc.fills(("mo", t, h // 4)))
                    else:
                        i.then_inc(S["m_pv"], 1)
            out_product(3)
            ffn(("ffn", 3), 3)

        @block.scalar
        def _(act):
            ln, own = Counts(), S["act_chain"]
            fn = nc.scalar.activation

            def norm():
                for t in range(NT):
                    act.wait_ge(S["x_ready"], ln.next(S["x_ready"]))
                    fn(rows[:, t, :], x[:, t, :], ACT.Square, accum_out=ss[:, t:t + 1]).then_inc(S["norm_sums"], 1)
                    act.wait_ge(S["norm_sums"], ln.made(S["norm_sums"]))
                act.wait_ge(S["norm_scale"], ln.next(S["norm_scale"]))
                fn(rows[:, 0, :], x[:, 0, :], ACT.Copy, scale=rs[:, 0:1]).then_inc(own, 1)
                act.wait_ge(own, ln.made(own))
                fn(rows[:, 1, :], x[:, 1, :], ACT.Copy, scale=rs[:, 1:2]).then_inc(S["normed"], 1)
                act.wait_ge(S["normed"], ln.made(S["normed"]))

            def swiglu(tag):
                for f in range(FC):
                    if tag == DEPTH - 1 and f == 4:
                        act.wait_ge(S["s5_params_in"], 16 * len(P2))
                        fn(prm[:, 3, :], prm[:, 2, :], ACT.Exp).then_inc(S["s5_dt"], 1)
                        act.wait_ge(S["s5_dt"], ln.made(S["s5_dt"]))
                    if tag == DEPTH - 1 and f == 8:
                        act.wait_ge(S["s5_arg"], ln.next(S["s5_arg"]))
                        fn(mag, prm[:, 4, :], ACT.Exp).then_inc(own, 1)
                        act.wait_ge(own, ln.made(own))
                        fn(prm[:, 6, :], prm[:, 5, :], ACT.Abs).then_inc(own, 1)
                        act.wait_ge(own, ln.made(own))
                        fn(prm[:, 6, :], prm[:, 6, :], ACT.Sin, scale=-1.0, bias=halfpi[:]).then_inc(own, 1)
                        act.wait_ge(own, ln.made(own))
                        fn(prm[:, 7, :], prm[:, 5, :], ACT.Sin).then_inc(S["s5_trig"], 1)
                        act.wait_ge(S["s5_trig"], ln.made(S["s5_trig"]))
                    act.wait_ge(*wk.filled(("gu", tag, f)))
                    b = wk.bank(("gu", tag, f))
                    if f >= 2:
                        act.wait_ge(S["hid_ready"], FC * tag + f - 1)
                    fn(sg[:, f % 2, :], b[:, 0:T], ACT.Silu).then_inc(S["act_silu"], 1)
                    act.wait_ge(S["act_silu"], ln.made(S["act_silu"]))

            def conv(tag):
                v = vecs[:, tag - 1, :]
                for f in range(FC):
                    act.wait_ge(*wk.filled(("gu", tag, f)))
                    b = wk.bank(("gu", tag, f))
                    fn(cv[:, f % 2, :], b[:, 0:T], ACT.Identity, scale=v[:, 44 + f:45 + f], bias=v[:, 66 + f:67 + f]).then_inc(S["conv_in"], 1)
                    act.wait_ge(S["conv_in"], ln.made(S["conv_in"]))
                    act.wait_ge(S["conv_done"], ln.next(S["conv_done"]))
                    if f >= 2:
                        act.wait_ge(S["hid_ready"], FC * tag + f - 1)
                    fn(sg[:, f % 2, :], cv[:, f % 2, :], ACT.Silu).then_inc(S["act_silu"], 1)
                    act.wait_ge(S["act_silu"], ln.made(S["act_silu"]))

            for dst, src in P1:
                act.dma_start(dst, src, allow_slow_non_contiguous=True).then_inc(S["params_in"], 16)
            act.wait_ge(*wk.filled(("line",)))
            b = wk.bank(("line",))
            fn(line, b[0:NH, :], ACT.Copy).then_inc(*wk.frees(("line",)))
            act.wait_ge(*wk.freed(("line",)))
            act.dma_start(bias_line.ap(), line.unsqueeze(1).to_broadcast([NH, P, LINE])).then_inc(S["line_out"], 16)
            act.wait_ge(S["line_out"], 16)
            for h in range(NH):
                act.dma_start(bias[:, h, :], bass.AP(bias_line, h * P * LINE + P - 1, [[LINE - 1, P], [1, 3 * P]])).then_inc(S["bias_in"], 16)

            act.wait_ge(S["lb_arg"], ln.next(S["lb_arg"]))
            fn(lbt[:, 0:8], lbt[:, 0:8], ACT.Exp).then_inc(S["lb_exp"], 1)
            act.wait_ge(S["lb_exp"], ln.made(S["lb_exp"]))

            for l in range(DEPTH):
                norm()
                for g, (c0, c1_) in enumerate(IN_COLS):
                    for t in range(NT):
                        act.wait_ge(*acc.filled(("in", l, g, t)))
                        b = acc.bank(("in", l, g, t))
                        fn(proj[:, t, c0:c1_], b[:, 0:c1_ - c0], ACT.Copy).then_inc(*acc.frees(("in", l, g, t)))
                        act.wait_ge(*acc.freed(("in", l, g, t)))
                        act.sem_inc(S["proj_ready"], 1)
                for t in range(NT):
                    for k, dst in enumerate((qTr, kTr)):
                        act.wait_ge(*wk.filled(("rT", l, t, k)))
                        b = wk.bank(("rT", l, t, k))
                        fn(dst[:, :, t * P:(t + 1) * P], b[:, 0:384].rearrange("p (b n) -> p b n", b=3), ACT.Copy).then_inc(*wk.frees(("rT", l, t, k)))
                        act.wait_ge(*wk.freed(("rT", l, t, k)))
                        act.sem_inc(S["turned_ret"], 1)
                fn(proj[:, :, O_GM:IN_W], proj[:, :, O_GM:IN_W], ACT.Gelu_apprx_tanh).then_inc(S["gelu_ready"], 1)
                act.wait_ge(S["gelu_ready"], ln.made(S["gelu_ready"]))
                fn(gate.rearrange("p t h b -> p t (h b)"), proj[:, :, O_NG:O_GM], ACT.Tanh, scale=0.5).then_inc(S["gates_ready"], 1)
                act.wait_ge(S["gates_ready"], ln.made(S["gates_ready"]))
                for j in range(2):
                    act.wait_ge(*wk.filled(("aT", l, j)))
                    b = wk.bank(("aT", l, j))
                    fn(aT[:, j].rearrange("p g n -> p (g n)"), b[0:HD, :], ACT.Copy).then_inc(*wk.frees(("aT", l, j)))
                    act.wait_ge(*wk.freed(("aT", l, j)))
                    act.sem_inc(S["blocks_read"], 1)
                for t in range(NT):
                    act.wait_ge(*wk.filled(("nqT", l, t)))
                    b = wk.bank(("nqT", l, t))
                    fn(qTn[:, :, t * P:(t + 1) * P], b[:, 0:384].rearrange("p (b n) -> p b n", b=3), ACT.Copy).then_inc(*wk.frees(("nqT", l, t)))
                    act.wait_ge(*wk.freed(("nqT", l, t)))
                    act.sem_inc(S["nsa_turned"], 1)
                act.wait_ge(*wk.filled(("nkT", l)))
                b = wk.bank(("nkT", l))
                fn(kTn.rearrange("p b n -> p (b n)"), b, ACT.Copy).then_inc(*wk.frees(("nkT", l)))
                act.wait_ge(*wk.freed(("nkT", l)))
                act.sem_inc(S["nsa_turned"], 1)
                act.wait_ge(*wk.filled(("h1", l)))
                b = wk.bank(("h1", l))
                fn(h1, b[0:HD, 0:64].rearrange("p (j n) -> p j n", j=2)[:, :, 0:30], ACT.Gelu_apprx_tanh).then_inc(*wk.frees(("h1", l)))
                act.wait_ge(*wk.freed(("h1", l)))
                act.sem_inc(S["h1_ready"], 1)
                fn(proj[:, :, O_RG:O_NQ], proj[:, :, O_RG:O_NQ], ACT.Silu).then_inc(S["silu_ready"], 1)
                act.wait_ge(S["silu_ready"], ln.made(S["silu_ready"]))
                act.wait_ge(S["cmp_scores"], ln.next(S["cmp_scores"]))
                fn(s_c, s_c, ACT.Exp).then_inc(S["cmp_exp"], 1)
                act.wait_ge(S["cmp_exp"], ln.made(S["cmp_exp"]))

                def exps(n):
                    t, h = n // NH, n % NH
                    K = P * (t + 1)
                    act.wait_ge(S["scores_ready"], ln.next(S["scores_ready"]))
                    for br in range(2):
                        i = fn(p_sb[:, n % 2, br * T:br * T + K], s_sb[:, n % 2, br * T:br * T + K], ACT.Exp,
                               bias=nmax[:, 2 * (n % 2) + br:2 * (n % 2) + br + 1], accum_out=lsum[:, t, h, 1 + br:2 + br])
                        to = S["probs_ready"] if br else own
                        i.then_inc(to, 1)
                        act.wait_ge(to, ln.made(to))

                def probsT(n):
                    t = n // NH
                    w = 2 * (t + 1) * P
                    if n >= 2 and (n - 2) % NH < NH - 1:
                        act.wait_ge(S["pv_done"], (NH - 1) * (NT * l + (n - 2) // NH) + (n - 2) % NH + 1)
                    elif n >= 2:
                        act.wait_ge(*acc.filled(("no", l, (n - 2) // NH, 2)))
                    act.wait_ge(*wk.filled(("pT", l, n)))
                    b = wk.bank(("pT", l, n))
                    fn(pT[:, n % 2, 0:w], b[:, 0:w], ACT.Copy).then_inc(*wk.frees(("pT", l, n)))
                    act.wait_ge(*wk.freed(("pT", l, n)))
                    act.sem_inc(S["probsT_ready"], 1)

                for n in range(NT * NH + 1):
                    if n < NT * NH:
                        exps(n)
                    if n == 0:
                        for k in range(3):
                            act.wait_ge(*wk.filled(("pcT", l, k)))
                            b = wk.bank(("pcT", l, k))
                            fn(pcT[0:NCMP, 4 * k:4 * k + 4, :], b[0:NCMP, :].rearrange("p (q n) -> p q n", q=4), ACT.Copy).then_inc(*wk.frees(("pcT", l, k)))
                            act.wait_ge(*wk.freed(("pcT", l, k)))
                            act.sem_inc(S["cmp_turned"], 1)
                    if n >= 1:
                        probsT(n - 1)
                if l == DEPTH - 1:
                    act.wait_ge(S["mixed"], ln.next(S["mixed"], DEPTH))
                    for dst, src in P2:
                        act.dma_start(dst, src, allow_slow_non_contiguous=True).then_inc(S["s5_params_in"], 16)
                norm()
                swiglu(l)

            norm()
            for g in (1, 0, 2, 3, 4):
                for q in range(2):
                    act.wait_ge(*acc.filled(("even", g, q)))
                    b = acc.bank(("even", g, q))
                    if g == 1:
                        fn(lf[:, 2 * q:2 * q + 2, :].rearrange("p h n -> p (h n)"), b, ACT.Tanh, scale=0.5).then_inc(*acc.frees(("even", g, q)))
                        act.wait_ge(*acc.freed(("even", g, q)))
                        act.sem_inc(S["hg_tanh"], 1)
                    elif g in (0, 4):
                        dst = qTe if g == 0 else uT
                        fn(dst[:, 2 * q:2 * q + 2, :].rearrange("p h n -> p (h n)"), b, ACT.Copy).then_inc(*acc.frees(("even", g, q)))
                        act.wait_ge(*acc.freed(("even", g, q)))
                        act.sem_inc(S["proj_ready"], 1)
                    else:
                        fn(eg[:, q, (g - 2) * 512:(g - 1) * 512], b, ACT.Copy).then_inc(*acc.frees(("even", g, q)))
                        act.wait_ge(*acc.freed(("even", g, q)))
                        act.sem_inc(S["proj_ready"], 1)
            act.wait_ge(S["hg_forget"], ln.next(S["hg_forget"]))
            fn(lf, lf, ACT.Ln).then_inc(S["hg_ln"], 1)
            act.wait_ge(S["hg_ln"], ln.made(S["hg_ln"]))
            act.wait_ge(S["hg_cum"], ln.next(S["hg_cum"]))
            fn(eb, bcum, ACT.Exp).then_inc(own, 1)
            act.wait_ge(own, ln.made(own))
            act.wait_ge(S["hg_cum"], ln.next(S["hg_cum"]))
            fn(bcum, bcum, ACT.Exp, scale=-1.0).then_inc(S["hg_exp"], 1)
            act.wait_ge(S["hg_exp"], ln.made(S["hg_exp"]))
            fn(lf, lf, ACT.Exp).then_inc(S["hg_exp"], 1)
            act.wait_ge(S["hg_exp"], ln.made(S["hg_exp"]))
            for t in range(NT):
                act.wait_ge(*wk.filled(("kkT", t)))
                b = wk.bank(("kkT", t))
                fn(kk[:, t].rearrange("p h n -> p (h n)"), b, ACT.Copy).then_inc(*wk.frees(("kkT", t)))
                act.wait_ge(*wk.freed(("kkT", t)))
                act.sem_inc(S["hg_kkT"], 1)
            fn(eg[:, :, 512:1024], eg[:, :, 512:1024], ACT.Silu).then_inc(S["silu_ready"], 1)
            act.wait_ge(S["silu_ready"], ln.made(S["silu_ready"]))
            for q in range(4):
                if q:
                    act.wait_ge(S["states_used"], q)
                else:
                    act.wait_ge(S["hg_out"], ln.next(S["hg_out"]))
                for j in range(4):
                    act.wait_ge(*wk.filled(("bu", q, j)))
                    b = wk.bank(("bu", q, j))
                    fn(bu[0][:, j, :], b[:, 0:T], ACT.Copy).then_inc(own, 1)
                    act.wait_ge(own, ln.made(own))
                    fn(bu[1][:, j, :], b[:, T:2 * T], ACT.Copy).then_inc(*wk.frees(("bu", q, j)))
                    act.wait_ge(*wk.freed(("bu", q, j)))
                act.sem_inc(S["drive_ready"], 1)
            for q in range(4):
                act.wait_ge(S["s5_y"], ln.next(S["s5_y"]))
                fn(zT[:, q, :], uT[:, q, :], ACT.Gelu_apprx_tanh).then_inc(S["s5_z"], 1)
                act.wait_ge(S["s5_z"], ln.made(S["s5_z"]))
            for q in range(2):
                act.wait_ge(*acc.filled(("glu", q)))
                b = acc.bank(("glu", q))
                for k in range(2):
                    i = fn(qTe[:, 2 * q + k, :], b[:, k * T:(k + 1) * T], ACT.Tanh, scale=0.5, bias=small2[:, 8 + 2 * q + k:9 + 2 * q + k])
                    if k:
                        i.then_inc(*acc.frees(("glu", q)))
                        act.wait_ge(*acc.freed(("glu", q)))
                    else:
                        i.then_inc(own, 1)
                        act.wait_ge(own, ln.made(own))
                act.sem_inc(S["glu_tanh"], 1)
            norm()
            conv(2)

            act.wait_ge(S["pos_arg"], ln.next(S["pos_arg"]))
            act.dma_start(fg, a["final_norm_g_2"].partition_broadcast(P)).then_inc(S["mla_in"], 16)
            fn(mang[:, 1], mang[:, 0], ACT.Abs).then_inc(own, 1)
            act.wait_ge(own, ln.made(own))
            fn(mang[:, 2], mang[:, 1], ACT.Sin, scale=-1.0, bias=halfpi[:]).then_inc(own, 1)
            act.wait_ge(own, ln.made(own))
            fn(mang[:, 3], mang[:, 0], ACT.Sin).then_inc(S["pos_trig"], 1)
            act.wait_ge(S["pos_trig"], ln.made(S["pos_trig"]))
            norm()
            for g, (c0, c1_) in enumerate(ODD_COLS):
                for t in range(NT):
                    act.wait_ge(*acc.filled(("odd", g, t)))
                    b = acc.bank(("odd", g, t))
                    fn(oin[:, t, c0:c1_], b[:, 0:c1_ - c0], ACT.Copy).then_inc(*acc.frees(("odd", g, t)))
                    act.wait_ge(*acc.freed(("odd", g, t)))
                    act.sem_inc(S["odd_ready"], 1)
            for g in range(2):
                for q in range(2):
                    act.wait_ge(*acc.filled(("qn", g, q)))
                    b = acc.bank(("qn", g, q))
                    h = 4 * g + 2 * q
                    fn(qnT[:, h:h + 2, :].rearrange("p h n -> p (h n)"), b, ACT.Copy).then_inc(*acc.frees(("qn", g, q)))
                    act.wait_ge(*acc.freed(("qn", g, q)))
                    act.sem_inc(S["heads_ready"], 1)
                act.wait_ge(*acc.filled(("qr", g)))
                b = acc.bank(("qr", g))
                fn(qr[:, :, g * T:(g + 1) * T], b.rearrange("p (t n) -> p t n", t=NT), ACT.Copy).then_inc(*acc.frees(("qr", g)))
                act.wait_ge(*acc.freed(("qr", g)))
                act.sem_inc(S["heads_ready"], 1)
            for q in range(4):
                act.wait_ge(*acc.filled(("kn", q)))
                b = acc.bank(("kn", q))
                fn(knT[:, 2 * q:2 * q + 2, :].rearrange("p h n -> p (h n)"), b, ACT.Copy).then_inc(*acc.frees(("kn", q)))
                act.wait_ge(*acc.freed(("kn", q)))
                act.sem_inc(S["heads_ready"], 1)
            for t in range(NT):
                for h in range(2):
                    act.wait_ge(*acc.filled(("v", t, h)))
                    b = acc.bank(("v", t, h))
                    fn(vt[:, t, h * 512:(h + 1) * 512], b, ACT.Copy).then_inc(*acc.frees(("v", t, h)))
                    act.wait_ge(*acc.freed(("v", t, h)))
                    act.sem_inc(S["heads_ready"], 1)
            for t in range(NT):
                act.wait_ge(*wk.filled(("qrT", t)))
                b = wk.bank(("qrT", t))
                fn(qrT[:, :, t * P:(t + 1) * P], b.rearrange("p (b n) -> p b n", b=4), ACT.Copy).then_inc(*wk.frees(("qrT", t)))
                act.wait_ge(*wk.freed(("qrT", t)))
                act.sem_inc(S["qrope_T"], 1)
            for n in range(NT * MH + 1):
                if n < NT * MH:
                    K = P * (n // MH + 1)
                    act.wait_ge(S["m_scores"], ln.next(S["m_scores"]))
                    fn(mp[:, n % 2, 0:K], ms[:, n % 2, 0:K], ACT.Exp, bias=mst[:, n:n + 1], accum_out=mst[:, 16 + n:17 + n]).then_inc(S["m_probs"], 1)
                    act.wait_ge(S["m_probs"], ln.made(S["m_probs"]))
                if n >= 1:
                    m = n - 1
                    K = P * (m // MH + 1)
                    if m >= 2 and (m - 2) % 4 < 3:
                        act.wait_ge(S["m_pv"], 3 * ((m - 2) // 4) + (m - 2) % 4 + 1)
                    elif m >= 2:
                        act.wait_ge(*acc.filled(("mo", (m - 2) // MH, ((m - 2) % MH) // 4)))
                    act.wait_ge(*wk.filled(("mpT", m)))
                    b = wk.bank(("mpT", m))
                    fn(mpT[:, m % 2, 0:K], b[:, 0:K], ACT.Copy).then_inc(*wk.frees(("mpT", m)))
                    act.wait_ge(*wk.freed(("mpT", m)))
                    act.sem_inc(S["m_probsT"], 1)
            norm()
            conv(3)
            norm()

        @block.gpsimd
        def _(pool):
            ln, own = Counts(), S["pool_chain"]
            tt, ts = nc.gpsimd.tensor_tensor, nc.gpsimd.tensor_scalar
            nc.gpsimd.memset(mhalf[:], -0.5).then_inc(own, 1)
            pool.wait_ge(own, ln.made(own))
            nc.gpsimd.memset(halfpi[:], float(np.pi / 2)).then_inc(own, 1)
            pool.wait_ge(own, ln.made(own))
            nc.gpsimd.memset(relb[NBUCKET:NBUCKET + 1, :], NEG).then_inc(S["setup_ready"], 1)
            pool.wait_ge(S["setup_ready"], ln.made(S["setup_ready"]))

            def inverse_root(parts, c0, n, width, sem_):
                ts(rs[0:parts, c0:c0 + n], ss[0:parts, c0:c0 + n], 1.0 / width, EPS, ALU.mult, ALU.add).then_inc(own, 1)
                pool.wait_ge(own, ln.made(own))
                tt(rs[0:parts, c0:c0 + n], rs[0:parts, c0:c0 + n], mhalf[0:parts, 0:n], ALU.pow).then_inc(sem_, 1)
                pool.wait_ge(sem_, ln.made(sem_))

            def norm():
                pool.wait_ge(S["norm_sums"], ln.next(S["norm_sums"], 2))
                inverse_root(P, 0, NT, D, S["norm_scale"])

            def heads(c0, n, width, parts=P):
                pool.wait_ge(S["head_sums"], ln.next(S["head_sums"]))
                inverse_root(parts, c0, n, width, S["head_scale"])

            def s5_tables():
                K = lambda k: prm[:, k, :]
                ar, ai, arg, th, co, si, den, xr, xi, k1, k2 = (K(k) for k in (0, 1, 4, 5, 6, 7, 8, 9, 10, 11, 12))
                pool.wait_ge(S["s5_dt"], ln.next(S["s5_dt"]))
                tt(arg, ar, K(3), ALU.mult).then_inc(own, 1)
                pool.wait_ge(own, ln.made(own))
                tt(th, ai, K(3), ALU.mult).then_inc(own, 1)
                pool.wait_ge(own, ln.made(own))
                ts(k1, th, 1.0 / TWO_PI, MAGIC, ALU.mult, ALU.add).then_inc(own, 1)
                pool.wait_ge(own, ln.made(own))
                ts(k1, k1, -MAGIC, None, ALU.add).then_inc(own, 1)
                pool.wait_ge(own, ln.made(own))
                for c in (CW1, CW2, CW3):
                    ts(k2, k1, -c, None, ALU.mult).then_inc(own, 1)
                    pool.wait_ge(own, ln.made(own))
                    tt(th, th, k2, ALU.add).then_inc(own, 1)
                    pool.wait_ge(own, ln.made(own))
                ts(th, th, PI_SAFE, -PI_SAFE, ALU.min, ALU.max).then_inc(S["s5_arg"], 1)
                pool.wait_ge(S["s5_arg"], ln.made(S["s5_arg"]))
                tt(den, ar, ar, ALU.mult).then_inc(own, 1)
                pool.wait_ge(own, ln.made(own))
                tt(k2, ai, ai, ALU.mult).then_inc(own, 1)
                pool.wait_ge(own, ln.made(own))
                tt(den, den, k2, ALU.add).then_inc(own, 1)
                pool.wait_ge(own, ln.made(own))
                nc.gpsimd.memset(k1, -1.0).then_inc(own, 1)
                pool.wait_ge(own, ln.made(own))
                tt(den, den, k1, ALU.pow).then_inc(own, 1)
                pool.wait_ge(own, ln.made(own))
                for m in bpad:
                    nc.gpsimd.memset(m, 0.0).then_inc(own, 1)
                    pool.wait_ge(own, ln.made(own))
                for g in range(2):
                    ts(cpad[0][:, :, 64 * g:64 * g + 64], craw[0], gmask[:, g:g + 1], None, ALU.mult).then_inc(own, 1)
                    pool.wait_ge(own, ln.made(own))
                    ts(cpad[1][:, :, 64 * g:64 * g + 64], craw[1], gmask[:, g:g + 1], -1.0, ALU.mult, ALU.mult).then_inc(own, 1)
                    pool.wait_ge(own, ln.made(own))
                pool.wait_ge(S["s5_trig"], ln.next(S["s5_trig"]))
                tt(xr, mag, co, ALU.mult).then_inc(own, 1)
                pool.wait_ge(own, ln.made(own))
                ts(xr, xr, -1.0, None, ALU.add).then_inc(own, 1)
                pool.wait_ge(own, ln.made(own))
                tt(xi, mag, si, ALU.mult).then_inc(own, 1)
                pool.wait_ge(own, ln.made(own))
                cr, ci = K(13), K(14)
                tt(cr, xr, ar, ALU.mult).then_inc(own, 1)
                pool.wait_ge(own, ln.made(own))
                tt(k2, xi, ai, ALU.mult).then_inc(own, 1)
                pool.wait_ge(own, ln.made(own))
                tt(cr, cr, k2, ALU.add).then_inc(own, 1)
                pool.wait_ge(own, ln.made(own))
                tt(cr, cr, den, ALU.mult).then_inc(own, 1)
                pool.wait_ge(own, ln.made(own))
                tt(ci, xi, ar, ALU.mult).then_inc(own, 1)
                pool.wait_ge(own, ln.made(own))
                tt(k2, xr, ai, ALU.mult).then_inc(own, 1)
                pool.wait_ge(own, ln.made(own))
                tt(ci, ci, k2, ALU.subtract).then_inc(own, 1)
                pool.wait_ge(own, ln.made(own))
                tt(ci, ci, den, ALU.mult).then_inc(own, 1)
                pool.wait_ge(own, ln.made(own))

                def each(ap, n):
                    return ap.unsqueeze(2).to_broadcast([ap.shape[0], ST, n])

                for r, (f1, f2, op) in enumerate(((cr, ci, ALU.subtract), (ci, cr, ALU.add))):
                    tt(bx[0], braw[0], each(f1, 16), ALU.mult).then_inc(own, 1)
                    pool.wait_ge(own, ln.made(own))
                    tt(bx[1], braw[1], each(f2, 16), ALU.mult).then_inc(own, 1)
                    pool.wait_ge(own, ln.made(own))
                    for g in range(2):
                        p_ = slice(64 * g, 64 * g + 64)
                        to = S["s5_pad"] if r and g else own
                        tt(bpad[r][p_, :, 16 * g:16 * g + 16], bx[0][p_], bx[1][p_], op).then_inc(to, 1)
                        pool.wait_ge(to, ln.made(to))
                nc.gpsimd.memset(cosT[:, :, 0:1], 1.0).then_inc(own, 1)
                pool.wait_ge(own, ln.made(own))
                nc.gpsimd.memset(sinT[:, :, 0:1], 0.0).then_inc(own, 1)
                pool.wait_ge(own, ln.made(own))
                n = 1
                while n < T:
                    A, B = etmp[0][:, :, 0:n], etmp[1][:, :, 0:n]
                    tt(A, cosT[:, :, 0:n], each(co, n), ALU.mult).then_inc(own, 1)
                    pool.wait_ge(own, ln.made(own))
                    tt(B, sinT[:, :, 0:n], each(si, n), ALU.mult).then_inc(own, 1)
                    pool.wait_ge(own, ln.made(own))
                    tt(cosT[:, :, n:2 * n], A, B, ALU.subtract).then_inc(own, 1)
                    pool.wait_ge(own, ln.made(own))
                    tt(A, sinT[:, :, 0:n], each(co, n), ALU.mult).then_inc(own, 1)
                    pool.wait_ge(own, ln.made(own))
                    tt(B, cosT[:, :, 0:n], each(si, n), ALU.mult).then_inc(own, 1)
                    pool.wait_ge(own, ln.made(own))
                    to = S["table_done"] if 2 * n == T else own
                    tt(sinT[:, :, n:2 * n], A, B, ALU.add).then_inc(to, 1)
                    pool.wait_ge(to, ln.made(to))
                    tt(k1, co, co, ALU.mult).then_inc(own, 1)
                    pool.wait_ge(own, ln.made(own))
                    tt(k2, si, si, ALU.mult).then_inc(own, 1)
                    pool.wait_ge(own, ln.made(own))
                    tt(si, co, si, ALU.mult).then_inc(own, 1)
                    pool.wait_ge(own, ln.made(own))
                    ts(si, si, 2.0, None, ALU.mult).then_inc(own, 1)
                    pool.wait_ge(own, ln.made(own))
                    tt(co, k1, k2, ALU.subtract).then_inc(own, 1)
                    pool.wait_ge(own, ln.made(own))
                    n *= 2

            for l in range(DEPTH):
                norm()
                heads(4, 20, HD)
                heads(24, 8, HD)
                heads(36, 12, HD)
                heads(32, 2, HD, NCMP)
                norm()
            s5_tables()
            norm()
            heads(4, 8, 128)
            norm()
            norm()
            heads(4, 2, MQ)
            heads(6, 2, MKV)
            norm()
            norm()

        @block.vector
        def _(dve):
            ln, own = Counts(), S["dve_chain"]
            v = nc.vector
            tt, ts, stt = v.tensor_tensor, v.tensor_scalar, v.scalar_tensor_tensor

            def over(ap, n):
                return ap.unsqueeze(len(ap.shape)).to_broadcast(list(ap.shape) + [n])

            def across(ap, at, n):
                s = list(ap.shape)
                return ap.unsqueeze(at).to_broadcast(s[:at] + [n] + s[at:])

            def into_hT(n, gain):
                for t in range(NT):
                    for q in range(2):
                        dve.wait_ge(*wk.filled(("T", n, t, q)))
                        b = wk.bank(("T", n, t, q)).rearrange("p (k n) -> p k n", k=4)
                        dst = hT[:, 4 * q:4 * q + 4, t * P:(t + 1) * P]
                        if gain is None:
                            i = v.tensor_copy(dst, b)
                        else:
                            i = tt(dst, b, over(vecs[:, 0, gain + 4 * q:gain + 4 * q + 4], P), ALU.mult)
                        i.then_inc(*wk.frees(("T", n, t, q)))
                        dve.wait_ge(*wk.freed(("T", n, t, q)))
                        dve.sem_inc(S["hT_ready"], 1)

            def add_out(names):
                for t in range(NT):
                    for g in range(2):
                        dve.wait_ge(*acc.filled(names(g, t)))
                        b = acc.bank(names(g, t))
                        xs = x[:, t, g * COLS:(g + 1) * COLS]
                        tt(xs, xs, b, ALU.add).then_inc(*acc.frees(names(g, t)))
                        dve.wait_ge(*acc.freed(names(g, t)))
                    dve.sem_inc(S["x_ready"], 1)

            def add_mix(l):
                for g in range(2):
                    for t in range(NT):
                        dve.wait_ge(*acc.filled(("out", l, g, t)))
                        b = acc.bank(("out", l, g, t))
                        xs = x[:, t, g * COLS:(g + 1) * COLS]
                        tt(xs, xs, b, ALU.add).then_inc(*acc.frees(("out", l, g, t)))
                        dve.wait_ge(*acc.freed(("out", l, g, t)))
                        if g == 1:
                            dve.sem_inc(S["x_ready"], 1)

            def ffn(n, tag, gain):
                into_hT(n, gain)
                for f in range(FC):
                    dve.wait_ge(*wk.filled(("gu", tag, f)))
                    b = wk.bank(("gu", tag, f))
                    if tag >= 2:
                        c, w = cv[:, f % 2, :], vecs[:, tag - 1, :]
                        dve.wait_ge(S["conv_in"], ln.next(S["conv_in"]))
                        stt(c[:, 1:T], b[:, 0:T - 1], w[:, 22 + f:23 + f], c[:, 1:T], ALU.mult, ALU.add).then_inc(own, 1)
                        dve.wait_ge(own, ln.made(own))
                        stt(c[:, 2:T], b[:, 0:T - 2], w[:, f:f + 1], c[:, 2:T], ALU.mult, ALU.add).then_inc(S["conv_done"], 1)
                        dve.wait_ge(S["conv_done"], ln.made(S["conv_done"]))
                    dve.wait_ge(S["act_silu"], ln.next(S["act_silu"]))
                    if f >= 4:
                        dve.wait_ge(S["down_done"], (FC - 1) * tag + f - 3)
                    tt(hid[:, f % 4, :], sg[:, f % 2, :], b[:, T:2 * T], ALU.mult).then_inc(*wk.frees(("gu", tag, f)))
                    dve.wait_ge(*wk.freed(("gu", tag, f)))
                    dve.sem_inc(S["hid_ready"], 1)
                add_out(lambda g, t: ("y", tag, 2 * t + g))

            def rotate(src, cos, sin, heads, tmp):
                lo, hi = src[:, :, :, 0:32], src[:, :, :, 32:64]
                c, s = across(cos, 2, heads), across(sin, 2, heads)
                tmp = [tmp[k].rearrange("p (t h d) -> p t h d", t=NT, h=heads) for k in range(4)]
                for k, (p_, q_) in enumerate(((lo, c), (hi, s), (hi, c), (lo, s))):
                    tt(tmp[k], p_, q_, ALU.mult).then_inc(own, 1)
                    dve.wait_ge(own, ln.made(own))
                tt(lo, tmp[0], tmp[1], ALU.subtract).then_inc(own, 1)
                dve.wait_ge(own, ln.made(own))
                tt(hi, tmp[2], tmp[3], ALU.add).then_inc(own, 1)
                dve.wait_ge(own, ln.made(own))

            def combine(l, t):
                dve.wait_ge(S["probs_ready"], NT * NH * l + NH * (t + 1))
                v.reciprocal(lsum[:, t], lsum[:, t]).then_inc(own, 1)
                dve.wait_ge(own, ln.made(own))
                tt(gate[:, t], gate[:, t], lsum[:, t], ALU.mult).then_inc(own, 1)
                dve.wait_ge(own, ln.made(own))
                dst = rows[:, t, RET_W:2 * RET_W].rearrange("p (h d) -> p h d", d=HD)
                for br in range(3):
                    dve.wait_ge(*acc.filled(("no", l, t, br)))
                    b = acc.bank(("no", l, t, br))[:, 0:RET_W].rearrange("p (h d) -> p h d", d=HD)
                    o = dst if br == 0 else osum[:, t, :].rearrange("p (h d) -> p h d", d=HD)
                    tt(o, b, over(gate[:, t, :, br], HD), ALU.mult).then_inc(*acc.frees(("no", l, t, br)))
                    dve.wait_ge(*acc.freed(("no", l, t, br)))
                    if br:
                        to = S["mixed"] if t and br == 2 else own
                        tt(dst, dst, o, ALU.add).then_inc(to, 1)
                        dve.wait_ge(to, ln.made(to))

            for k, n in enumerate((NVEC, 88, 88)):
                dve.wait_ge(*wk.filled(("vec", k)))
                b = wk.bank(("vec", k))
                v.tensor_copy(vecs[:, k, 0:n], b[:, 0:n]).then_inc(*wk.frees(("vec", k)))
                dve.wait_ge(*wk.freed(("vec", k)))
            dve.wait_ge(*wk.filled(("pe",)))
            b = wk.bank(("pe",))
            v.tensor_copy(peT[:].rearrange("p j k -> p (j k)"), b[0:HD, 0:P]).then_inc(*wk.frees(("pe",)))
            dve.wait_ge(*wk.freed(("pe",)))
            dve.wait_ge(S["x_in"], 16)
            dve.sem_inc(S["x_ready"], 2)
            l0, l1 = vecs[:, 0, V_LB:V_LB + 4], vecs[:, 0, V_LB + 4:V_LB + 8]
            tt(lbt[:, 8:12], l0, l1, ALU.max).then_inc(own, 1)
            dve.wait_ge(own, ln.made(own))
            tt(lbt[:, 0:4], l0, lbt[:, 8:12], ALU.subtract).then_inc(own, 1)
            dve.wait_ge(own, ln.made(own))
            tt(lbt[:, 4:8], l1, lbt[:, 8:12], ALU.subtract).then_inc(S["lb_arg"], 1)
            dve.wait_ge(S["lb_arg"], ln.made(S["lb_arg"]))
            dve.wait_ge(S["lb_exp"], ln.next(S["lb_exp"]))
            tt(lbt[:, 12:16], lbt[:, 0:4], lbt[:, 4:8], ALU.add).then_inc(own, 1)
            dve.wait_ge(own, ln.made(own))
            v.reciprocal(lbt[:, 12:16], lbt[:, 12:16]).then_inc(own, 1)
            dve.wait_ge(own, ln.made(own))
            tt(lbt[:, 8:12], lbt[:, 0:4], lbt[:, 12:16], ALU.mult).then_inc(own, 1)
            dve.wait_ge(own, ln.made(own))
            ts(lbt[:, 12:16], lbt[:, 8:12], -1.0, 1.0, ALU.mult, ALU.add).then_inc(own, 1)
            dve.wait_ge(own, ln.made(own))

            for l in range(DEPTH):
                into_hT(("mix", l), V_ATTN + KC * l)
                dve.wait_ge(S["proj_ready"], ln.next(S["proj_ready"], 4))
                rotate(proj[:, :, 0:2 * RET_W].rearrange("p t (h d) -> p t h d", d=HD), rope[:, :, 0, :], rope[:, :, 1, :], 2 * NH, rtmp)
                dve.sem_inc(S["rotated"], 1)
                dve.wait_ge(S["proj_ready"], ln.next(S["proj_ready"], 8))
                q3 = proj[:, :, O_NQ:O_KV]
                k4 = proj[:, :, O_KV + 256:O_KV + 768].rearrange("p t (b n) -> p t b n", b=2)[:, :, :, 0:P]
                sq = nsq.rearrange("p (t n) -> p t n", t=NT)
                tt(sq, q3, q3, ALU.mult).then_inc(own, 1)
                dve.wait_ge(own, ln.made(own))
                ssv = ss[:, 4:24].rearrange("p (t n) -> p t n", t=NT)
                v.tensor_reduce(ss[:, 4:16].rearrange("p (t h) -> p t h", t=NT), sq.rearrange("p t (h d) -> p t h d", d=HD), AX_X, ALU.add).then_inc(own, 1)
                dve.wait_ge(own, ln.made(own))
                sk4 = sk.rearrange("p (t b n) -> p t b n", t=NT, b=2)
                for t in range(NT):
                    tt(sk4[:, t], k4[:, t], k4[:, t], ALU.mult).then_inc(own, 1)
                    dve.wait_ge(own, ln.made(own))
                v.tensor_reduce(ss[:, 16:24], sk.rearrange("p (q d) -> p q d", d=HD), AX_X, ALU.add).then_inc(S["head_sums"], 1)
                dve.wait_ge(S["head_sums"], ln.made(S["head_sums"]))
                dve.wait_ge(S["head_scale"], ln.next(S["head_scale"]))
                for t in range(NT):
                    qv = qn[:, t, :].rearrange("p (q g d) -> p g q d", q=HPG, g=2)
                    src = proj[:, t, O_NQ:O_KV].rearrange("p (g q d) -> p g q d", q=HPG, g=2)
                    tt(qv, src, over(rs[:, 4 + t * NH:4 + (t + 1) * NH].rearrange("p (g q) -> p g q", g=2), HD), ALU.mult).then_inc(own, 1)
                    dve.wait_ge(own, ln.made(own))
                    stt(qn[:, t, :].rearrange("p (h d) -> p h d", d=HD), qn[:, t, :].rearrange("p (h d) -> p h d", d=HD), HD ** -0.5,
                                across(gains[:, l, 0, :], 1, NH), ALU.mult, ALU.mult).then_inc(own, 1)
                    dve.wait_ge(own, ln.made(own))
                    kv_ = kn[:, t, :].rearrange("p (b g d) -> p b g d", b=2, g=2)
                    tt(kv_, k4[:, t].rearrange("p b (g d) -> p b g d", g=2),
                               over(rs[:, 16 + 4 * t:20 + 4 * t].rearrange("p (b g) -> p b g", b=2), HD), ALU.mult).then_inc(own, 1)
                    dve.wait_ge(own, ln.made(own))
                    to = S["nsa_rows"] if t else own
                    tt(kv_, kv_, across(gains[:, l, 2:4, :], 2, 2), ALU.mult).then_inc(to, 1)
                    dve.wait_ge(to, ln.made(to))
                for h in range(NH):
                    dve.wait_ge(*wk.filled(("rs", l, h)))
                    b = wk.bank(("rs", l, h))
                    if h >= 2:
                        dve.wait_ge(S["ret_mixed"], (NH - 1) * l + h - 1)
                    tt(sT[:, h % 2, 0:T], b[:, 0:T], decay[:, h, :], ALU.mult).then_inc(own, 1)
                    dve.wait_ge(own, ln.made(own))
                    tt(sT[:, h % 2, T:T + P], b[:, T:T + P], decay[:, h, 0:P], ALU.mult).then_inc(*wk.frees(("rs", l, h)))
                    dve.wait_ge(*wk.freed(("rs", l, h)))
                    dve.sem_inc(S["decayed"], 1)
                dve.wait_ge(S["proj_ready"], ln.next(S["proj_ready"], 2))
                dve.wait_ge(S["gelu_ready"], ln.next(S["gelu_ready"]))
                zv = proj[:, :, O_GM + GM_W:IN_W]
                tt(vn, zv, zv, ALU.mult).then_inc(own, 1)
                dve.wait_ge(own, ln.made(own))
                v.tensor_reduce(ss[:, 24:32].rearrange("p (t h) -> p t h", t=NT), vn.rearrange("p t (h d) -> p t h d", d=HD), AX_X, ALU.add).then_inc(S["head_sums"], 1)
                dve.wait_ge(S["head_sums"], ln.made(S["head_sums"]))
                dve.wait_ge(S["blocks_read"], ln.next(S["blocks_read"], 2))
                for j in range(2):
                    for g in range(2):
                        src = aT[:, j, g, :]
                        win = bass.AP(src.tensor, src.offset, [list(src.ap[0]), [1, CMP_LEN], [CMP_STRIDE, NCMP]])
                        to = S["blocks_ready"] if j and g else own
                        tt(blk[:, j, :, g * NCMP:(g + 1) * NCMP], win, over(peT[:, 2 * l + j, :], NCMP), ALU.add).then_inc(to, 1)
                        dve.wait_ge(to, ln.made(to))
                dve.wait_ge(S["head_scale"], ln.next(S["head_scale"]))
                for t in range(NT):
                    tt(vn[:, t, :].rearrange("p (h d) -> p h d", d=HD), zv[:, t, :].rearrange("p (h d) -> p h d", d=HD),
                               over(rs[:, 24 + 4 * t:28 + 4 * t], HD), ALU.mult).then_inc(own, 1)
                    dve.wait_ge(own, ln.made(own))
                dve.wait_ge(*wk.filled(("wsT", l)))
                b = wk.bank(("wsT", l)).rearrange("p (g n) -> p g n", g=4)
                tt(wsT, b, across(triu[:], 1, 4), ALU.mult).then_inc(*wk.frees(("wsT", l)))
                dve.wait_ge(*wk.freed(("wsT", l)))
                dve.sem_inc(S["gm_rows"], 1)
                for t in range(NT):
                    dve.wait_ge(*acc.filled(("ro", l, t)))
                    b = acc.bank(("ro", l, t))
                    v.tensor_copy(rows[:, t, 0:RET_W], b[:, 0:RET_W]).then_inc(*acc.frees(("ro", l, t)))
                    dve.wait_ge(*acc.freed(("ro", l, t)))
                ro = rows[:, :, 0:RET_W]
                tt(rsq, ro, ro, ALU.mult).then_inc(own, 1)
                dve.wait_ge(own, ln.made(own))
                v.tensor_reduce(ss[:, 36:48].rearrange("p (t h) -> p t h", t=NT), rsq.rearrange("p t (h d) -> p t h d", d=HD), AX_X, ALU.add).then_inc(S["head_sums"], 1)
                dve.wait_ge(S["head_sums"], ln.made(S["head_sums"]))
                dve.wait_ge(*wk.filled(("kc", l)))
                b = wk.bank(("kc", l))
                v.tensor_copy(kc[0:NCMP, :], b[0:NCMP, 0:256]).then_inc(*wk.frees(("kc", l)))
                dve.wait_ge(*wk.freed(("kc", l)))
                tt(kcn[0:NCMP, :], kc[0:NCMP, 0:P], kc[0:NCMP, 0:P], ALU.mult).then_inc(own, 1)
                dve.wait_ge(own, ln.made(own))
                v.tensor_reduce(ss[0:NCMP, 32:34], kcn[0:NCMP, :].rearrange("p (g d) -> p g d", g=2), AX_X, ALU.add).then_inc(S["head_sums"], 1)
                dve.wait_ge(S["head_sums"], ln.made(S["head_sums"]))
                dve.wait_ge(S["head_scale"], ln.next(S["head_scale"], 2))
                kc3 = kcn[0:NCMP, :].rearrange("p (g d) -> p g d", g=2)
                tt(kc3, kc[0:NCMP, 0:P].rearrange("p (g d) -> p g d", g=2), over(rs[0:NCMP, 32:34], HD), ALU.mult).then_inc(own, 1)
                dve.wait_ge(own, ln.made(own))
                tt(kc3, kc3, across(gains[0:NCMP, l, 1, :], 1, 2), ALU.mult).then_inc(S["kc_rows"], 1)
                dve.wait_ge(S["kc_rows"], ln.made(S["kc_rows"]))
                dve.wait_ge(*wk.filled(("kcT", l)))
                b = wk.bank(("kcT", l))
                v.tensor_copy(kTc[:, 0:NCMP], b[:, 0:NCMP]).then_inc(*wk.frees(("kcT", l)))
                dve.wait_ge(*wk.freed(("kcT", l)))
                dve.sem_inc(S["kTc_ready"], 1)
                if l == 0:
                    dve.wait_ge(S["bias_in"], 16 * NH)
                for g in range(2):
                    dve.wait_ge(*wk.filled(("sc", l, g)))
                    b = wk.bank(("sc", l, g))[:, 0:NT * HPG * 16].rearrange("p (q n) -> p q n", n=16)
                    for t in range(NT):
                        at = (1 - t) * P + CMP_LEN - 1
                        i = tt(s_c[:, t * NH + g * HPG:t * NH + (g + 1) * HPG], b[:, t * HPG:(t + 1) * HPG, 0:NCMP],
                               bias[:, g * HPG:(g + 1) * HPG, at:at + 14 * CMP_STRIDE + 1:CMP_STRIDE], ALU.add)
                        if t == 0:
                            i.then_inc(own, 1)
                            dve.wait_ge(own, ln.made(own))
                        else:
                            i.then_inc(*wk.frees(("sc", l, g)))
                            dve.wait_ge(*wk.freed(("sc", l, g)))
                v.tensor_reduce(nmax[:, 8:20], s_c, AX_X, ALU.max).then_inc(own, 1)
                dve.wait_ge(own, ln.made(own))
                tt(s_c, s_c, over(nmax[:, 8:20], NCMP), ALU.subtract).then_inc(S["cmp_scores"], 1)
                dve.wait_ge(S["cmp_scores"], ln.made(S["cmp_scores"]))
                dve.wait_ge(S["cmp_exp"], ln.next(S["cmp_exp"]))
                v.tensor_reduce(lsum[:, :, :, 0], s_c, AX_X, ALU.add).then_inc(own, 1)
                dve.wait_ge(own, ln.made(own))
                sc4 = s_c.rearrange("p (t h) n -> p t h n", t=NT)
                tt(sc4, sc4, across(cmask[:], 2, NH), ALU.mult).then_inc(S["cmp_probs"], 1)
                dve.wait_ge(S["cmp_probs"], ln.made(S["cmp_probs"]))
                for n in range(NT * NH):
                    t, h = n // NH, n % NH
                    K = P * (t + 1)
                    dve.wait_ge(*wk.filled(("s", l, n)))
                    b = wk.bank(("s", l, n)).rearrange("p (b n) -> p b n", b=2)[:, :, 0:K]
                    if n >= 2:
                        dve.wait_ge(S["probs_ready"], NT * NH * l + n - 1)
                    s = s_sb[:, n % 2, :].rearrange("p (b n) -> p b n", b=2)[:, :, 0:K]
                    tt(s, b, across(bias[:, h, (1 - t) * P:(1 - t) * P + K], 1, 2), ALU.add).then_inc(*wk.frees(("s", l, n)))
                    dve.wait_ge(*wk.freed(("s", l, n)))
                    v.tensor_reduce(nmax[:, 2 * (n % 2):2 * (n % 2) + 2], s, AX_X, ALU.max, negate=True).then_inc(S["scores_ready"], 1)
                    dve.wait_ge(S["scores_ready"], ln.made(S["scores_ready"]))
                    if n == 1:
                        dve.wait_ge(*acc.filled(("gm", l)))
                        g_ = acc.bank(("gm", l)).rearrange("p (g t n) -> p g t n", g=4, t=NT)
                        for g in range(4):
                            dst = rows[:, :, 2 * RET_W + g * HD:2 * RET_W + (g + 1) * HD]
                            i = stt(dst, g_[:, g], vecs[:, 0, V_GMB + 4 * l + g:V_GMB + 4 * l + g + 1], proj[:, :, O_GM + g * HD:O_GM + (g + 1) * HD], ALU.add, ALU.mult)
                            if g < 3:
                                i.then_inc(own, 1)
                                dve.wait_ge(own, ln.made(own))
                            else:
                                i.then_inc(*acc.frees(("gm", l)))
                                dve.wait_ge(*acc.freed(("gm", l)))
                    if n == 2:
                        dve.wait_ge(S["silu_ready"], ln.next(S["silu_ready"]))
                        for t_ in range(NT):
                            r3 = ro[:, t_, :].rearrange("p (h d) -> p h d", d=HD)
                            tt(r3, r3, over(rs[:, 36 + NH * t_:36 + NH * (t_ + 1)], HD), ALU.mult).then_inc(own, 1)
                            dve.wait_ge(own, ln.made(own))
                        tt(ro, ro, proj[:, :, O_RG:O_NQ], ALU.mult).then_inc(own, 1)
                        dve.wait_ge(own, ln.made(own))
                    if n == 3:
                        dve.wait_ge(S["gates_ready"], ln.next(S["gates_ready"]))
                        ts(gate, gate, 0.5, 0.5, ALU.mult, ALU.add).then_inc(own, 1)
                        dve.wait_ge(own, ln.made(own))
                    if n == NH + 2:
                        combine(l, 0)
                combine(l, 1)
                into_hT(("mixed", l), None)
                add_mix(l)
                ffn(("ffn", l), l, V_FFN + KC * l)
            for r in range(2):
                for key_, dst in (("bbT", bbT), ("cT", cT)):
                    dve.wait_ge(*wk.filled((key_, r)))
                    b = wk.bank((key_, r))
                    v.tensor_copy(dst[:, r].rearrange("p i n -> p (i n)"), b).then_inc(*wk.frees((key_, r)))
                    dve.wait_ge(*wk.freed((key_, r)))

            into_hT(("mix", 2), V_MIX2)
            v.memset(ones, 1.0).then_inc(own, 1)
            dve.wait_ge(own, ln.made(own))
            ts(small2[:, 8:12], vecs[:, 0, V_GLU:V_GLU + 4], 0.5, None, ALU.mult).then_inc(own, 1)
            dve.wait_ge(own, ln.made(own))
            dve.wait_ge(S["hg_tanh"], ln.next(S["hg_tanh"], 2))
            ts(lf, lf, 0.5, 0.5, ALU.mult, ALU.add).then_inc(own, 1)
            dve.wait_ge(own, ln.made(own))
            for h in range(HG):
                ts(lf[:, h, :], lf[:, h, :], lbt[:, 12 + h:13 + h], lbt[:, 8 + h:9 + h], ALU.mult, ALU.add).then_inc(own, 1)
                dve.wait_ge(own, ln.made(own))
            ts(key, lf, -1.0, 1.0, ALU.mult, ALU.add).then_inc(S["hg_forget"], 1)
            dve.wait_ge(S["hg_forget"], ln.made(S["hg_forget"]))
            dve.wait_ge(S["hg_ln"], ln.next(S["hg_ln"]))
            for h in range(HG):
                for n in range(NCH):
                    c = slice(n * HC, (n + 1) * HC)
                    to = S["hg_cum"] if (h, n) == (HG - 1, NCH - 1) else own
                    v.tensor_tensor_scan(bcum[:, h, c], ones, lf[:, h, c], 0.0, ALU.mult, ALU.add).then_inc(to, 1)
                    dve.wait_ge(to, ln.made(to))
            chunks = lambda m: m.rearrange("p h n -> p (h n)").rearrange("p (q c) -> p q c", c=HC)
            tt(chunks(lf), over(chunks(bcum)[:, :, HC - 1], HC), chunks(bcum), ALU.subtract).then_inc(S["hg_cum"], 1)
            dve.wait_ge(S["hg_cum"], ln.made(S["hg_cum"]))
            dve.wait_ge(S["proj_ready"], ln.next(S["proj_ready"], 8))
            dve.wait_ge(S["hg_exp"], ln.next(S["hg_exp"]))
            dec = small2[:, 16:32]
            v.tensor_copy(dec, chunks(eb)[:, :, HC - 1]).then_inc(own, 1)
            dve.wait_ge(own, ln.made(own))
            tt(eb, eb, qTe, ALU.mult).then_inc(own, 1)
            dve.wait_ge(own, ln.made(own))
            tt(bcum, bcum, key, ALU.mult).then_inc(S["hg_q"], 1)
            dve.wait_ge(S["hg_q"], ln.made(S["hg_q"]))
            dve.wait_ge(S["hg_exp"], ln.next(S["hg_exp"]))
            tt(key, key, lf, ALU.mult).then_inc(S["hg_kk"], 1)
            dve.wait_ge(S["hg_kk"], ln.made(S["hg_kk"]))
            dve.wait_ge(*wk.filled(("att",)))
            b = wk.bank(("att",)).rearrange("p (q n) -> p q n", n=HC)
            tt(att, b, across(tri64[:], 1, NT * HG), ALU.mult).then_inc(*wk.frees(("att",)))
            dve.wait_ge(*wk.freed(("att",)))
            dve.sem_inc(S["hg_att"], 1)
            for n in range(NCH - 1):
                dve.wait_ge(*wk.filled(("ds", n)))
                b = wk.bank(("ds", n)).rearrange("p (h n) -> p h n", h=HG)
                if n == 0:
                    v.tensor_copy(state[:, 0], b).then_inc(*wk.frees(("ds", n)))
                    dve.wait_ge(*wk.freed(("ds", n)))
                else:
                    for h in range(HG):
                        i = stt(state[:, n, h, :], state[:, n - 1, h, :], dec[:, h * NCH + n:h * NCH + n + 1], b[:, h, :], ALU.mult, ALU.add)
                        if h < HG - 1:
                            i.then_inc(own, 1)
                            dve.wait_ge(own, ln.made(own))
                        else:
                            i.then_inc(*wk.frees(("ds", n)))
                            dve.wait_ge(*wk.freed(("ds", n)))
                dve.sem_inc(S["hg_state"], 1)
            for t in range(NT):
                dve.wait_ge(*acc.filled(("eo", t)))
                b = acc.bank(("eo", t))
                v.tensor_copy(rows[:, t, 0:512], b).then_inc(*acc.frees(("eo", t)))
                dve.wait_ge(*acc.freed(("eo", t)))
            dve.sem_inc(S["hg_out"], 1)
            er = rows[:, :, 0:512]
            k2 = kk.rearrange("p t h n -> p t (h n)")
            tt(k2, er, er, ALU.mult).then_inc(own, 1)
            dve.wait_ge(own, ln.made(own))
            v.tensor_reduce(ss[:, 4:12], kk.rearrange("p t h n -> p (t h) n"), AX_X, ALU.add).then_inc(S["head_sums"], 1)
            dve.wait_ge(S["head_sums"], ln.made(S["head_sums"]))
            dve.wait_ge(S["head_scale"], ln.next(S["head_scale"]))
            for t in range(NT):
                r3 = rows[:, t, 0:512].rearrange("p (h d) -> p h d", h=HG)
                tt(r3, r3, over(rs[:, 4 + HG * t:4 + HG * (t + 1)], P), ALU.mult).then_inc(own, 1)
                dve.wait_ge(own, ln.made(own))
            dve.wait_ge(S["silu_ready"], ln.next(S["silu_ready"]))
            tt(er, er, eg[:, :, 512:1024], ALU.mult).then_inc(S["mixed"], 1)
            dve.wait_ge(S["mixed"], ln.made(S["mixed"]))

            dve.wait_ge(S["table_done"], ln.next(S["table_done"]))
            for q in range(4):
                co, si = cosT[:, 4 * q:4 * q + 4, :], sinT[:, 4 * q:4 * q + 4, :]
                dve.wait_ge(S["drive_ready"], ln.next(S["drive_ready"]))
                tt(m2, co, bu[0], ALU.mult).then_inc(own, 1)
                dve.wait_ge(own, ln.made(own))
                tt(m4, si, bu[1], ALU.mult).then_inc(own, 1)
                dve.wait_ge(own, ln.made(own))
                tt(wre, m2, m4, ALU.add).then_inc(own, 1)
                dve.wait_ge(own, ln.made(own))
                tt(m2, co, bu[1], ALU.mult).then_inc(own, 1)
                dve.wait_ge(own, ln.made(own))
                tt(m4, si, bu[0], ALU.mult).then_inc(own, 1)
                dve.wait_ge(own, ln.made(own))
                tt(wim, m2, m4, ALU.subtract).then_inc(S["states_used"], 1)
                dve.wait_ge(S["states_used"], ln.made(S["states_used"]))
                for j in range(4):
                    f = mag[:, 4 * q + j:4 * q + j + 1].to_broadcast([P, T])
                    v.tensor_tensor_scan(m2[:, j, :], f, wre[:, j, :], 0.0, ALU.mult, ALU.add).then_inc(own, 1)
                    dve.wait_ge(own, ln.made(own))
                    v.tensor_tensor_scan(m4[:, j, :], f, wim[:, j, :], 0.0, ALU.mult, ALU.add).then_inc(own, 1)
                    dve.wait_ge(own, ln.made(own))
                tt(wre, co, m2, ALU.mult).then_inc(own, 1)
                dve.wait_ge(own, ln.made(own))
                tt(wim, si, m4, ALU.mult).then_inc(own, 1)
                dve.wait_ge(own, ln.made(own))
                tt(m1, wre, wim, ALU.subtract).then_inc(own, 1)
                dve.wait_ge(own, ln.made(own))
                tt(wre, si, m2, ALU.mult).then_inc(own, 1)
                dve.wait_ge(own, ln.made(own))
                tt(wim, co, m4, ALU.mult).then_inc(own, 1)
                dve.wait_ge(own, ln.made(own))
                tt(m3, wre, wim, ALU.add).then_inc(S["states_ready"], 1)
                dve.wait_ge(S["states_ready"], ln.made(S["states_ready"]))
                dve.wait_ge(*acc.filled(("sy", q)))
                b = acc.bank(("sy", q))
                stt(uT[:, q, :], uT[:, q, :], vecs[:, 0, V_SD + q:V_SD + q + 1], b[:, 0:T], ALU.mult, ALU.add).then_inc(*acc.frees(("sy", q)))
                dve.wait_ge(*acc.freed(("sy", q)))
                dve.sem_inc(S["s5_y"], 1)
            for t in range(NT):
                dve.wait_ge(*wk.filled(("eT", t)))
                b = wk.bank(("eT", t)).rearrange("p (k n) -> p k n", k=4)
                tt(hT[:, 0:4, t * P:(t + 1) * P], b, over(vecs[:, 0, V_HG:V_HG + 4], P), ALU.mult).then_inc(*wk.frees(("eT", t)))
                dve.wait_ge(*wk.freed(("eT", t)))
                dve.sem_inc(S["hT_ready"], 1)
            for q in range(2):
                dve.wait_ge(S["glu_tanh"], ln.next(S["glu_tanh"]))
                h = slice(2 * q, 2 * q + 2)
                ts(qTe[:, h], qTe[:, h], 0.5, 0.5, ALU.mult, ALU.add).then_inc(own, 1)
                dve.wait_ge(own, ln.made(own))
                tt(hT[:, 4 + 2 * q:6 + 2 * q, :], zT[:, h], qTe[:, h], ALU.mult).then_inc(S["hT_ready"], 1)
                dve.wait_ge(S["hT_ready"], ln.made(S["hT_ready"]))
            add_mix(2)
            v.tensor_copy(mst[:, 48:50], posi[:]).then_inc(own, 1)
            dve.wait_ge(own, ln.made(own))
            for t in range(NT):
                ts(mang[:, 0, t, :], freq[:], mst[:, 48 + t:49 + t], None, ALU.mult).then_inc(own, 1)
                dve.wait_ge(own, ln.made(own))
            ts(mang[:, 1], mang[:, 0], 1.0 / TWO_PI, MAGIC, ALU.mult, ALU.add).then_inc(own, 1)
            dve.wait_ge(own, ln.made(own))
            ts(mang[:, 1], mang[:, 1], -MAGIC, None, ALU.add).then_inc(own, 1)
            dve.wait_ge(own, ln.made(own))
            for c in (CW1, CW2, CW3):
                stt(mang[:, 0], mang[:, 1], -c, mang[:, 0], ALU.mult, ALU.add).then_inc(own, 1)
                dve.wait_ge(own, ln.made(own))
            ts(mang[:, 0], mang[:, 0], PI_SAFE, -PI_SAFE, ALU.min, ALU.max).then_inc(S["pos_arg"], 1)
            dve.wait_ge(S["pos_arg"], ln.made(S["pos_arg"]))
            ffn(("ffn", 2), 2, V_FFN2)

            into_hT(("mix", 3), V_MIX2 + KC)
            dve.wait_ge(S["odd_ready"], ln.next(S["odd_ready"], 4))
            lat = oin[:, :, 0:MQ + MKV]
            tt(osq, lat, lat, ALU.mult).then_inc(own, 1)
            dve.wait_ge(own, ln.made(own))
            v.tensor_reduce(ss[:, 4:6], osq[:, :, 0:MQ], AX_X, ALU.add).then_inc(S["head_sums"], 1)
            dve.wait_ge(S["head_sums"], ln.made(S["head_sums"]))
            v.tensor_reduce(ss[:, 6:8], osq[:, :, MQ:MQ + MKV], AX_X, ALU.add).then_inc(S["head_sums"], 1)
            dve.wait_ge(S["head_sums"], ln.made(S["head_sums"]))
            dve.wait_ge(S["pos_trig"], ln.next(S["pos_trig"]))
            cos, sin = mang[:, 2], mang[:, 3]
            rotate(oin[:, :, MQ + MKV:].rearrange("p t (h d) -> p t h d", h=1), cos, sin, 1, [mtmp[:, k, 0:NT * 32] for k in range(4)])
            for k in range(2):
                v.tensor_copy(kr[:, :, k * MR:(k + 1) * MR], oin[:, :, MQ + MKV:]).then_inc(own, 1)
                dve.wait_ge(own, ln.made(own))
            dve.wait_ge(S["head_scale"], ln.next(S["head_scale"], 2))
            for t in range(NT):
                ts(oin[:, t, 0:MQ], oin[:, t, 0:MQ], rs[:, 4 + t:5 + t], None, ALU.mult).then_inc(own, 1)
                dve.wait_ge(own, ln.made(own))
                to = S["odd_rows"] if t else own
                ts(oin[:, t, MQ:MQ + MKV], oin[:, t, MQ:MQ + MKV], rs[:, 6 + t:7 + t], None, ALU.mult).then_inc(to, 1)
                dve.wait_ge(to, ln.made(to))
            for t in range(NT):
                c = slice(t * P, (t + 1) * P)
                dve.wait_ge(*wk.filled(("oT", t, 0)))
                b = wk.bank(("oT", t, 0))[:, 0:MQ].rearrange("p (c n) -> p c n", c=3)
                tt(cqT[:, :, c], b, over(vecs[:, 0, V_MQ:V_MQ + 3], P), ALU.mult).then_inc(*wk.frees(("oT", t, 0)))
                dve.wait_ge(*wk.freed(("oT", t, 0)))
                dve.sem_inc(S["odd_T"], 1)
                dve.wait_ge(*wk.filled(("oT", t, 1)))
                b = wk.bank(("oT", t, 1))
                tt(ckvT[:, :, c], b[:, 0:MKV].rearrange("p (c n) -> p c n", c=2), over(vecs[:, 0, V_MKV:V_MKV + 2], P), ALU.mult).then_inc(own, 1)
                dve.wait_ge(own, ln.made(own))
                v.tensor_copy(krT[:, c], b[:, MKV:MKV + P]).then_inc(*wk.frees(("oT", t, 1)))
                dve.wait_ge(*wk.freed(("oT", t, 1)))
                dve.sem_inc(S["odd_T"], 1)
            dve.wait_ge(S["heads_ready"], ln.next(S["heads_ready"], 6))
            rotate(qr.rearrange("p t (h d) -> p t h d", h=MH), cos, sin, MH, [mtmp[:, k, :] for k in range(4)])
            dve.sem_inc(S["qrope_rows"], 1)
            for n in range(NT * MH + 1):
                if n < NT * MH:
                    K = P * (n // MH + 1)
                    dve.wait_ge(*wk.filled(("ms", n)))
                    b = wk.bank(("ms", n))[:, 0:K]
                    if n >= 2:
                        dve.wait_ge(S["m_probs"], n - 1)
                    s_ = ms[:, n % 2, 0:K]
                    stt(s_, b, MQK ** -0.5, causal[:, T - K:T], ALU.mult, ALU.add).then_inc(*wk.frees(("ms", n)))
                    dve.wait_ge(*wk.freed(("ms", n)))
                    v.tensor_reduce(mst[:, n:n + 1], s_, AX_X, ALU.max, negate=True).then_inc(S["m_scores"], 1)
                    dve.wait_ge(S["m_scores"], ln.made(S["m_scores"]))
                if n >= 1:
                    m = n - 1
                    K = P * (m // MH + 1)
                    dve.wait_ge(S["m_probs"], ln.next(S["m_probs"]))
                    v.reciprocal(mst[:, 32:33], mst[:, 16 + m:17 + m]).then_inc(own, 1)
                    dve.wait_ge(own, ln.made(own))
                    ts(mp[:, m % 2, 0:K], mp[:, m % 2, 0:K], mst[:, 32:33], None, ALU.mult).then_inc(S["m_norm"], 1)
                    dve.wait_ge(S["m_norm"], ln.made(S["m_norm"]))
            for t in range(NT):
                for q in range(2):
                    dve.wait_ge(*acc.filled(("mo", t, q)))
                    b = acc.bank(("mo", t, q)).rearrange("p (h n) -> p h n", h=4)
                    v.tensor_copy(hT[:, 4 * q:4 * q + 4, t * P:(t + 1) * P], b).then_inc(*acc.frees(("mo", t, q)))
                    dve.wait_ge(*acc.freed(("mo", t, q)))
                    dve.sem_inc(S["hT_ready"], 1)
            add_mix(3)
            ffn(("ffn", 3), 3, V_FFN2 + KC)
            dve.wait_ge(S["normed"], ln.next(S["normed"], 9))
            dve.wait_ge(S["mla_in"], 16)
            for t in range(NT):
                tt(rows[:, t, :], rows[:, t, :], fg, ALU.mult).then_inc(S["out_rows"], 1)
                dve.wait_ge(S["out_rows"], ln.made(S["out_rows"]))

        @block.sync
        def _(sp):
            xv = a["x"].rearrange("b (t p) d -> p (b t) d", p=P)
            sp.dma_start(x[:], xv).then_inc(S["x_in"], 16)
            for stream, name, s, last in order:
                if last:
                    sp.wait_ge(*last)
                for dst, src in man[name]:
                    sp.dma_start(dst(stream.t[:, s, :]), src).then_inc(stream.landed[s], 16)
            ov = out.rearrange("b (t p) d -> p (b t) d", p=P)
            for t in range(NT):
                sp.wait_ge(S["out_rows"], t + 1)
                sp.dma_start(ov[:, t, :], rows[:, t, :]).then_inc(S["stored"], 16)
            sp.wait_ge(S["stored"], 16 * NT)


_INS = """x attn_norm w_in w_out nsa_q_gain nsa_k_gain cmp_pe cmp_w1 cmp_w2 gm_ws gm_b ffn_norm w_gate_up w_down rel_bias
    positions_2 norm_mix_g_2 norm_ffn_g_2 final_norm_g_2 even_w_in_2 hgrn_lb_logits_2 hgrn_norm_g_2 s5_a_re_2 s5_a_im_2
    s5_log_dt_2 s5_b_re_2 s5_b_im_2 s5_c_re_2 s5_c_im_2 s5_d_2 s5_w_glu_2 s5_b_glu_2 even_w_out_2 odd_w_in_2 mla_q_norm_g_2
    mla_w_uq_2 mla_kv_norm_g_2 mla_w_ukv_2 odd_w_out_2 ffn_w_in_2 ffn_conv_w_2 ffn_conv_b_2 ffn_w_out_2""".split()


def kernel(**inputs):
    import concourse.bacc as bacc
    from concourse.bass_utils import run_bass_kernel_spmd

    nc = bacc.Bacc("TRN2", target_bir_lowering=False, num_devices=1)
    arrays, aps = {}, {}
    for name in _INS:
        v = np.ascontiguousarray(inputs[name])
        arrays["in_" + name] = v
        aps[name] = nc.dram_tensor("in_" + name, v.shape, mybir.dt.from_np(v.dtype), kind="ExternalInput").ap()
    for name, v in shape_constants().items():
        v = np.ascontiguousarray(v)
        arrays[name] = v
        aps[name] = nc.dram_tensor(name, v.shape, F32, kind="ExternalInput").ap()
    out = nc.dram_tensor("out", (1, T, D), F32, kind="ExternalOutput").ap()
    build(nc, aps, out)
    r = run_bass_kernel_spmd(nc, [arrays], core_ids=[0])
    return r.results[0]["out"]
```

```python
from contextlib import ExitStack

import numpy as np

import concourse.bass as bass
from concourse import mybir

F32 = mybir.dt.float32
F32R = mybir.dt.float32r
I32 = mybir.dt.int32
ALU = mybir.AluOpType
ACT = mybir.ActivationFunctionType
AX_X = mybir.AxisListType.X

P = 128
T = 256
NT = T // P
D = 1024
KC = D // P
DEPTH = 2
HD = 64
NH = 6
HPG = 3
RET_W = NH * HD
IN_W = 3218
O_RQ, O_RK, O_RV, O_RG = 0, RET_W, 2 * RET_W, 3 * RET_W
O_NQ = 4 * RET_W
O_KV = O_NQ + RET_W
O_NG = O_KV + 768
O_GM = O_NG + 18
GM_W = 256
NCMP = 15
CMP_LEN, CMP_STRIDE = 32, 16
FF = 2816
FC = FF // P
FSTEP = 2
NSTEP = FC // FSTEP
COLS = 512
EPS = 1e-6
NEG = -1e30
NBUCKET = 32
LINE = 512
HG = 4
HC = 64
NCH = T // HC
SD = 512
ST = 16
MH = 8
MQ, MKV, MR, MN, MV = 384, 256, 64, 128, 128
MQK = MN + MR
TWO_PI = 2.0 * np.pi
MAGIC = 12582912.0
CW1 = 6.28125
CW2 = float(np.float32(0.0019350051879882812))
CW3 = float(TWO_PI - CW1 - CW2)
PI_SAFE = 3.1415925


def shape_constants():
    f = np.float32
    p = np.arange(P)
    ident = np.eye(P, dtype=f)
    triu = (p[:, None] <= p[None, :]).astype(f)
    tri64 = np.concatenate([triu[:HC, :HC], triu[:HC, :HC]], 0)
    causal = np.zeros((P, T), f)
    causal[:, P:] = np.where(p[None, :] > p[:, None], f(NEG), f(0))
    half = HD // 2
    inv = (f(10000.0) ** (-np.arange(half, dtype=f) / f(half))).astype(f)
    ang = np.arange(T, dtype=f)[:, None] * inv[None]
    rope = np.stack([np.cos(ang), np.sin(ang)], 1).astype(f)
    rope = rope.reshape(NT, P, 2, half).transpose(1, 0, 2, 3)
    log_gamma = np.log(1.0 - 2.0 ** (-5.0 - np.arange(NH)))
    m, n = np.arange(T)[:, None], np.arange(T)[None]
    dec = np.where(n >= m, np.exp(np.maximum(n - m, 0)[None] * log_gamma[:, None, None]), 0.0) * HD ** -0.5
    decay = dec[:, :P, :].transpose(1, 0, 2).astype(f)
    dist = 255 - np.arange(LINE)
    me = NBUCKET // 2
    nf = np.maximum(dist, 1).astype(f)
    large = me + (np.log(nf / f(me)) / f(np.log(128 / me)) * f(NBUCKET - me)).astype(np.int32)
    bucket = np.where(dist < me, np.maximum(dist, 0), np.minimum(large, NBUCKET - 1))
    onehot = np.zeros((NBUCKET + 1, LINE), f)
    onehot[np.where(dist >= 0, bucket, NBUCKET), np.arange(LINE)] = 1.0
    tok = np.arange(T)
    cend = np.arange(NCMP) * CMP_STRIDE + CMP_LEN - 1
    cmask = (tok[:, None] >= cend[None]).astype(f).reshape(NT, P, NCMP).transpose(1, 0, 2)
    gmask = (((p // 16) % 2)[:, None] == np.arange(2)[None]).astype(f)
    freq = (f(10000.0) ** (-np.arange(0, MR, 2, dtype=f) / f(MR))).astype(f)
    return {
        "const_ident": ident, "const_triu": triu, "const_tri64": tri64, "const_causal": causal,
        "const_rope": rope, "const_decay": decay, "const_onehot": onehot, "const_cmask": cmask,
        "const_gmask": gmask, "const_freq": np.tile(freq[None], (P, 1)),
    }


class Counts:

    def __init__(self):
        self.own, self.others = {}, {}

    def made(self, sem):
        self.own[sem.name] = self.own.get(sem.name, 0) + 1
        return self.own[sem.name]

    def next(self, sem, n=1):
        self.others[sem.name] = self.others.get(sem.name, 0) + n
        return self.others[sem.name]


class Banks:

    def __init__(self, tensor, full, free):
        self.t, self.full, self.free, self.at, self.n = tensor, full, free, {}, 0

    def turn(self):
        return self.free[self.n % len(self.free)], self.n // len(self.free)

    def fill(self, name):
        self.at[name] = self.n
        self.n += 1
        return self.bank(name)

    def bank(self, name):
        return self.t[:, self.at[name] % len(self.full), :]

    def fills(self, name):
        return self.full[self.at[name] % len(self.full)], 1

    def filled(self, name):
        return self.full[self.at[name] % len(self.full)], self.at[name] // len(self.full) + 1

    def frees(self, name):
        return self.free[self.at[name] % len(self.free)], 1

    def freed(self, name):
        return self.free[self.at[name] % len(self.free)], self.at[name] // len(self.free) + 1


class Weights:

    def __init__(self, raw, pairs, landed, low, manifest):
        self.raw, self.pairs, self.landed, self.low, self.manifest = raw, pairs, landed, low, manifest
        self.pieces = []
        self.split = []
        self.count = [0] * len(landed)

    def size(self, name):
        return self.manifest[name][0]

    def load(self, name):
        slot = len(self.pieces) % len(self.landed)
        self.count[slot] += 16 * len(self.manifest[name][1])
        self.pieces.append([name, slot, self.count[slot], None])
        return self.landed[slot], self.count[slot]

    def plain(self):
        name, slot = self.pieces[-1][:2]
        return self.raw[:, slot, 0:self.size(name)]

    def release(self, sem, value):
        self.pieces[-1][3] = (sem, value)

    def parts(self, name):
        self.load(name)
        self.split.append([len(self.pieces) - 1, None])
        self.release(self.low, len(self.split))
        return self.low, len(self.split)

    def pair(self, k=-1):
        k = k % len(self.split)
        n = self.size(self.pieces[self.split[k][0]][0])
        return [self.pairs[:, k % self.pairs.shape[1], h, 0:n] for h in range(2)]

    def used(self, sem, value):
        self.split[-1][1] = (sem, value)

    def source(self, k):
        name, slot = self.pieces[self.split[k][0]][:2]
        return self.raw[:, slot, 0:self.size(name)]

    def loaded(self, k):
        name, slot, value, _ = self.pieces[self.split[k][0]]
        return self.landed[slot], value

    def emptied(self, k):
        return self.split[k - self.pairs.shape[1]][1]


def build(nc, a, out):
    ctx = ExitStack()
    with ctx:
        def sb(name, shape, dt=F32):
            return ctx.enter_context(nc.sbuf_tensor(name, shape, dt))

        def sem(name):
            return ctx.enter_context(nc.semaphore(name))

        bias_line = nc.dram_tensor("bias_line", [NH, P, LINE], F32, kind="Internal")

        x = sb("x", [P, NT, D])
        rows = sb("rows", [P, NT, D])
        hTh = sb("hTh", [P, KC, T], F32R)
        hTl = sb("hTl", [P, KC, T], F32R)
        NRAW, NPAIR, PIECE = 3, 3, 2048
        wraw = sb("wraw", [P, NRAW, PIECE])
        wpair = sb("wpair", [P, NPAIR, 2, PIECE], F32R)
        ident = sb("ident", [P, P])
        triu = sb("triu", [P, P])
        tri64 = sb("tri64", [P, HC])
        causal = sb("causal", [P, T])
        rope = sb("rope", [P, NT, 2, HD // 2])
        cmask = sb("cmask", [P, NT, NCMP])
        gmask = sb("gmask", [P, 2])
        freq = sb("freq", [P, MR // 2])
        NVEC = 97
        vecs = sb("vecs", [P, 3, NVEC])
        V_ATTN, V_FFN, V_MIX2, V_FFN2, V_MQ, V_MKV, V_GLU, V_SD, V_LB, V_GMB, V_HG = 0, 16, 32, 48, 64, 67, 69, 73, 77, 85, 93
        relb = sb("relb", [NBUCKET + 1, NH])
        mhalf = sb("mhalf", [P, 64])
        halfpi = sb("halfpi", [P, 1])
        ss = sb("ss", [P, 64])
        rs = sb("rs", [P, 64])
        sg = sb("sg", [P, 4, T])
        stage = sg[:].rearrange("p (b k) n -> p b (k n)", b=2)
        lbt = sb("lbt", [P, 16])
        posi = sb("posi", [P, NT], I32)
        hidh = sb("hidh", [P, 4, T], F32R)
        hidl = sb("hidl", [P, 4, T], F32R)

        ARENA = 22144
        arena = sb("arena", [P, ARENA])

        class Carve:
            def __init__(self):
                self.at = 0

            def __call__(self, pattern=None, n=0, rows=P, **dims):
                v = arena[0:rows, self.at:self.at + n]
                self.at += n
                assert self.at <= ARENA, self.at
                return v.rearrange(pattern, **dims) if pattern else v

        c1 = Carve()
        proj = c1("p (t n) -> p t n", NT * IN_W, t=NT)
        decay = c1("p (h n) -> p h n", NH * T, h=NH)
        bias = c1("p (h n) -> p h n", NH * 3 * P, h=NH)
        peT = c1("p (j k) -> p j k", 2 * DEPTH * CMP_LEN, rows=HD, j=2 * DEPTH)
        gains = c1("p (l k d) -> p l k d", DEPTH * 4 * HD, l=DEPTH, k=4)
        gmws = c1("p (l g n) -> p l g n", DEPTH * 4 * P, l=DEPTH, g=4)
        cw2 = c1("p (j n) -> p j n", DEPTH * 2 * HD, rows=HD, j=2 * DEPTH)
        qk = c1(None, 6 * T)
        qTr, kTr = (qk[:, k * 3 * T:(k + 1) * 3 * T].rearrange("p (b n) -> p b n", b=3) for k in range(2))
        p_sb = qk[:, 0:1024].rearrange("p (b n) -> p b n", b=2)
        qTn = c1("p (b n) -> p b n", 3 * T, b=3)
        kTn = c1("p (b n) -> p b n", 2 * T, b=2)
        kTc = c1(None, 16)
        blocks = c1(None, 2 * CMP_LEN * 30)
        blk = blocks[0:HD].rearrange("p (j l n) -> p j l n", j=2, l=CMP_LEN)
        pcT = blocks[0:16, 0:NT * NH * P].rearrange("p (q n) -> p q n", q=NT * NH)
        onehot, line = blocks[0:NBUCKET + 1, 0:LINE], blocks[0:NH, LINE:2 * LINE]
        aT = proj[0:HD, :, 0:512].rearrange("p j (g n) -> p j g n", g=2)
        s_sb = proj[:, :, 0:512]
        turned = c1(None, 1024)
        sT = turned[:, 0:768].rearrange("p (b n) -> p b n", b=2)
        pT = turned.rearrange("p (b n) -> p b n", b=2)
        qn = c1("p (t n) -> p t n", NT * RET_W, t=NT)
        kn = c1("p (t n) -> p t n", NT * 256, t=NT)
        wsT = c1("p (g n) -> p g n", 4 * P, g=4)
        vn = c1("p (t n) -> p t n", NT * GM_W, t=NT)
        h1 = c1("p (j n) -> p j n", 2 * 30, rows=HD, j=2)
        kc = c1(None, 256, rows=16)
        kcn = c1(None, P, rows=16)
        s_c = c1("p (q n) -> p q n", NT * NH * NCMP, q=NT * NH)
        nmax = c1(None, 32)
        lsum = c1("p (t h b) -> p t h b", 36, t=NT, h=NH)
        gate = c1("p (t h b) -> p t h b", 36, t=NT, h=NH)
        rsq = osum = qn
        free_rows = rows[:].rearrange("p t n -> p (t n)")
        rtmp = [free_rows[:, 0:768], free_rows[:, 768:1536], qk[:, 0:768], qk[:, 768:1536]]
        nsq = free_rows[:, 0:768]
        sk = free_rows[:, 1536:2048]
        vraw = qn.rearrange("p t n -> p (t n)")[:, 0:3 * P].rearrange("p (k n) -> p k n", k=3)

        c2 = Carve()
        cosT = c2("p (i n) -> p i n", ST * T, i=ST)
        sinT = c2("p (i n) -> p i n", ST * T, i=ST)
        eg = c2("p (t n) -> p t n", NT * 1024, t=NT)
        qTe = c2("p (h n) -> p h n", HG * T, h=HG)
        lf = c2("p (h n) -> p h n", HG * T, h=HG)
        key = c2("p (h n) -> p h n", HG * T, h=HG)
        bcum = c2("p (h n) -> p h n", HG * T, h=HG)
        eb = c2("p (h n) -> p h n", HG * T, h=HG)
        ukk = c2(None, HG * T + NT * HG * P)
        uT = ukk[:, 0:HG * T].rearrange("p (h n) -> p h n", h=HG)
        kk = ukk[:, HG * T:].rearrange("p (t h n) -> p t h n", t=NT, h=HG)
        late = c2(None, 1536)
        state = late.rearrange("p (c h n) -> p c h n", c=3, h=HG)
        att = sg[:, 0:2, :].rearrange("p a n -> p (a n)").rearrange("p (q n) -> p q n", q=NT * HG)
        bbT = c2("p (r i n) -> p r i n", 2 * 4 * P, r=2, i=4)
        cT = c2("p (r i n) -> p r i n", 2 * 4 * P, r=2, i=4)
        mag = c2(None, ST)
        ones = c2(None, HC)
        small2 = c2(None, 32)
        bu = qTe, lf
        m1, m2, m3, m4 = key, bcum, eb, late[:, 0:1024].rearrange("p (j n) -> p j n", j=4)
        wre, wim = (eg[:, k, :].rearrange("p (j n) -> p j n", j=4) for k in range(2))
        zT = kk.rearrange("p t h n -> p (t h n)").rearrange("p (h n) -> p h n", h=4)
        braw = [key[:, 0, :].rearrange("p (i h) -> p i h", i=ST), key[:, 1, :].rearrange("p (i h) -> p i h", i=ST)]
        bpad = [qTe[:, 0:2, :].rearrange("p a n -> p (a n)").rearrange("p (i n) -> p i n", i=ST),
                qTe[:, 2:4, :].rearrange("p a n -> p (a n)").rearrange("p (i n) -> p i n", i=ST)]
        craw = [lf[:, 0, :].rearrange("p (i n) -> p i n", i=4), lf[:, 1, :].rearrange("p (i n) -> p i n", i=4)]
        cpad = [bcum[:, 0:2, :].rearrange("p a n -> p (a n)").rearrange("p (i n) -> p i n", i=4),
                bcum[:, 2:4, :].rearrange("p a n -> p (a n)").rearrange("p (i n) -> p i n", i=4)]
        bx = [key[:, 2, :].rearrange("p (i h) -> p i h", i=ST), key[:, 3, :].rearrange("p (i h) -> p i h", i=ST)]
        prm = eb.rearrange("p h n -> p (h n)")[:, 0:20 * ST].rearrange("p (k i) -> p k i", i=ST)
        etmp = [e.rearrange("p (i n) -> p i n", i=ST) for e in
                (eg.rearrange("p t n -> p (t n)"), ukk)]

        c3 = Carve()
        oin = c3("p (t n) -> p t n", NT * 704, t=NT)
        osq = c3("p (t n) -> p t n", NT * 640, t=NT)
        kr = c3("p (t n) -> p t n", NT * P, t=NT)
        cqT = c3("p (c n) -> p c n", 3 * T, c=3)
        ckvT = c3("p (c n) -> p c n", 2 * T, c=2)
        krT = c3(None, T)
        qnT = c3("p (h n) -> p h n", MH * T, h=MH)
        knT = c3("p (h n) -> p h n", MH * T, h=MH)
        qr = c3("p (t n) -> p t n", NT * MH * MR, t=NT)
        qrT = c3("p (b n) -> p b n", 4 * T, b=4)
        vt = c3("p (t n) -> p t n", NT * MH * MV, t=NT)
        mtmp = c3("p (k n) -> p k n", 4 * 512, k=4)
        ms = c3("p (b n) -> p b n", 2 * T, b=2)
        mp = c3("p (b n) -> p b n", 2 * T, b=2)
        mpT = c3("p (b n) -> p b n", 2 * T, b=2)
        mang = c3("p (k t n) -> p k t n", 4 * NT * 32, k=4, t=NT)
        mst = c3(None, 64)
        fg = c3(None, D)

        accum = ctx.enter_context(nc.psum_tensor("accum", [P, 4, COLS], F32))
        work = ctx.enter_context(nc.psum_tensor("work", [P, 4, COLS], F32))
        acc = Banks(accum, [sem(f"acc_full{i}") for i in range(4)], [sem(f"acc_free{i}") for i in range(4)])
        wk = Banks(work, [sem(f"work_full{i}") for i in range(4)], [sem(f"work_free{i}") for i in range(4)])

        man = {}

        def piece(name, w, n, pattern="p (c n) -> p c n", **dims):
            man[name] = (n, [(lambda s: s.rearrange(pattern, **dims), w)])

        def panel(name, w, k, cols):
            c0, c1_ = cols
            n, kc = c1_ - c0, k // P
            v = w[:, c0:c1_].rearrange("(c p) n -> p c n", p=P)
            per = min(kc, PIECE // n)
            for h in range(0, kc, per):
                piece((name, h // per), v[:, h:h + per, :], per * n, c=per)

        def ffn_panels(tag, w_in, w_out):
            wv = w_in.rearrange("(c p) n -> p c n", p=P)
            dv = w_out.rearrange("(c p) n -> p c n", p=P)
            for f in range(FC):
                man["gu", tag, f] = (PIECE, [
                    (lambda s, h=h: s.rearrange("p (c h n) -> p c h n", c=KC, h=2)[:, :, h, :],
                     wv[:, :, h * FF + f * P:h * FF + (f + 1) * P]) for h in range(2)])
            for j in range(NSTEP):
                piece(("dn", tag, j), dv[:, j * FSTEP:(j + 1) * FSTEP, :], PIECE, c=FSTEP)

        IN_COLS = [(c, min(c + COLS, IN_W)) for c in range(0, IN_W, COLS)]
        OUT_COLS = [(0, COLS), (COLS, D)]
        for l in range(DEPTH):
            for g, c in enumerate(IN_COLS):
                panel(("in", l, g), a["w_in"][l], D, c)
            for j in range(2):
                man["w1", l, j] = (PIECE, [(lambda s: s[0:HD].rearrange("p (l h) -> p l h", l=CMP_LEN),
                                            a["cmp_w1"][l, j].rearrange("(l d) h -> d l h", d=HD))])
            for g, c in enumerate(OUT_COLS):
                panel(("out", l, g), a["w_out"][l], D, c)
            ffn_panels(l, a["w_gate_up"][l], a["w_down"][l])
            ffn_panels(2 + l, a["ffn_w_in_2"][l], a["ffn_w_out_2"][l])
        for g in range(5):
            if g in (2, 3):
                panel(("even", g), a["even_w_in_2"][0], D, (g * COLS, (g + 1) * COLS))
            else:
                for q in range(2):
                    c = g * COLS + q * T
                    piece((("even", g), q), a["even_w_in_2"][0][:, c:c + T].rearrange("(c p) n -> p c n", p=P), PIECE, c=KC)
        panel("glu", a["s5_w_glu_2"][0], SD, (0, SD))
        ODD_COLS = [(0, 512), (512, 704)]
        for g in range(2):
            panel(("out", 2, g), a["even_w_out_2"][0], D, OUT_COLS[g])
            panel(("out", 3, g), a["odd_w_out_2"][0], D, OUT_COLS[g])
            panel(("odd", g), a["odd_w_in_2"][0], D, ODD_COLS[g])
        for q in range(4):
            panel(("uq", q), a["mla_w_uq_2"][0], MQ, (q * 384, (q + 1) * 384))
        for q in range(2):
            panel(("ukv", q), a["mla_w_ukv_2"][0], MKV, (q * 1024, (q + 1) * 1024))

        names = """x_in params_in setup_ready vec_ready consts2_in s5_params_in line_ready line_out bias_in mla_in
          pe_chain act_chain dve_chain pool_chain
          x_ready norm_sums norm_scale normed hT_high hT_ready w_high w_low piece_used
          proj_ready rotated turned_ret decayed ret_mixed
          head_sums head_scale nsa_rows nsa_turned blocks_ready blocks_read gelu_ready
          h1_ready kc_raw kc_rows kTc_ready scores_ready probs_ready probsT_ready pv_done
          cmp_scores cmp_exp cmp_probs cmp_turned gates_ready gm_rows silu_ready mixed
          act_silu hid_high hid_ready down_done conv_in conv_done
          s5_dt s5_arg s5_trig lb_arg lb_exp s5_tables s5_pad s5_wT table_done
          hg_tanh hg_forget hg_ln hg_cum hg_exp hg_q hg_kk hg_kkT hg_att hg_state hg_out
          drive_ready states_ready states_used s5_y s5_z glu_tanh z_gated
          odd_ready odd_rows odd_T qrope_rows qrope_T
          m_scores m_probs m_norm m_probsT m_pv pos_ready pos_arg pos_trig out_rows stored""".split()
        S = {n: sem(n) for n in names}
        W = Weights(wraw, wpair, [sem(f"raw_in{i}") for i in range(NRAW)], S["w_low"], man)

        P1 = [(ident[:], a["const_ident"]), (triu[:], a["const_triu"]), (tri64[:], a["const_tri64"]),
              (causal[:], a["const_causal"]), (rope[:], a["const_rope"]), (cmask[:], a["const_cmask"]),
              (gmask[:], a["const_gmask"]), (freq[:], a["const_freq"]),
              (onehot, a["const_onehot"]), (relb[0:NBUCKET, :], a["rel_bias"])]

        def vec(at, n, src, slot=0):
            P1.append((vraw[at:at + n, slot, :], src))

        vec(V_ATTN, 16, a["attn_norm"].rearrange("l (c p) -> (l c) p", p=P))
        vec(V_FFN, 16, a["ffn_norm"].rearrange("l (c p) -> (l c) p", p=P))
        vec(V_MIX2, 16, a["norm_mix_g_2"].rearrange("l (c p) -> (l c) p", p=P))
        vec(V_FFN2, 16, a["norm_ffn_g_2"].rearrange("l (c p) -> (l c) p", p=P))
        vec(V_MQ, 3, a["mla_q_norm_g_2"].rearrange("l (c p) -> (l c) p", p=P))
        vec(V_MKV, 2, a["mla_kv_norm_g_2"].rearrange("l (c p) -> (l c) p", p=P))
        vec(V_GLU, 4, a["s5_b_glu_2"].rearrange("l (c p) -> (l c) p", p=P))
        vec(V_SD, 4, a["s5_d_2"].rearrange("l (c p) -> (l c) p", p=P))
        vec(V_LB, 8, a["hgrn_lb_logits_2"].rearrange("l (c p) -> (l c) p", p=P))
        vec(V_GMB, 8, a["gm_b"].rearrange("l g p -> (l g) p"))
        vec(V_HG, 4, a["hgrn_norm_g_2"].rearrange("l (c p) -> (l c) p", p=P))
        for l in range(DEPTH):
            vec(0, 66, a["ffn_conv_w_2"][l].rearrange("w (c p) -> (w c) p", p=P), 1 + l)
            vec(66, 22, a["ffn_conv_b_2"][l:l + 1].rearrange("l (c p) -> (l c) p", p=P), 1 + l)
        peraw = rows[:, 0, 0:HD]
        P1.append((peraw, a["cmp_pe"].rearrange("l j k d -> (l j k) d")))
        P1.append((gains[:, :, 0, :].rearrange("p l d -> p l d"), a["nsa_q_gain"].partition_broadcast(P)))
        for l in range(DEPTH):
            P1.append((gains[:, l, 1:4, :], a["nsa_k_gain"][l].partition_broadcast(P)))
            P1.append((gmws[:, l, :, :], a["gm_ws"][l].rearrange("g t s -> t g s")))
            P1.append((cw2[:, 2 * l:2 * l + 2, :], a["cmp_w2"][l].rearrange("j d h -> d j h")))
        P1.append((decay, a["const_decay"]))
        P1.append((posi[:], a["positions_2"].rearrange("b (t p) -> p (b t)", p=P)))

        pview = lambda n: a[n][0].rearrange("(i g) p -> (g p) i", g=2)
        P2 = [(braw[r], a[n][0].rearrange("(i g) p h -> (g p) i h", g=2)) for r, n in enumerate(("s5_b_re_2", "s5_b_im_2"))]
        P2 += [(craw[r], a[n][0].rearrange("(i g) h p -> (g h) i p", i=4)) for r, n in enumerate(("s5_c_re_2", "s5_c_im_2"))]
        P2 += [(prm[:, 0, :], pview("s5_a_re_2")), (prm[:, 1, :], pview("s5_a_im_2"))]
        for g in range(2):
            P2.append((prm[64 * g:64 * g + 64, 2, :],
                       a["s5_log_dt_2"][0].rearrange("(i g) -> g i", g=2)[g].partition_broadcast(64)))

        block = ctx.enter_context(nc.Block())

        @block.tensor
        def _(pe):
            ln, own = Counts(), S["pe_chain"]
            mm = nc.tensor.matmul
            tr = nc.tensor.transpose

            def turn_rows(n, src, blocks):
                for t in range(NT):
                    for q in range(blocks // 4):
                        pe.wait_ge(*wk.turn())
                        b = wk.fill(("T", n, t, q))
                        for k in range(4):
                            c = (4 * q + k) * P
                            i = tr(b[:, k * P:(k + 1) * P], src[:, t, c:c + P], ident[:])
                        i.then_inc(*wk.fills(("T", n, t, q)))

            def mm3(dst, still, move, start, stop):
                mm(dst, still[0], move[0], start=start, stop=False)
                mm(dst, still[0], move[1], start=False, stop=False)
                return mm(dst, still[1], move[0], start=False, stop=stop)

            def hT_at(c, tokens):
                return hTh[:, c, tokens], hTl[:, c, tokens]

            used = [0]

            def piece_used(i):
                i.then_inc(S["piece_used"], 1)
                used[0] += 1
                W.used(S["piece_used"], used[0])

            def rows_by(name, width):
                b = []
                for t in range(NT):
                    pe.wait_ge(*acc.turn())
                    b.append(acc.fill(name + (t,)))
                per = min(KC, PIECE // width)
                for u in range(KC // per):
                    pe.wait_ge(*W.parts((name, u)))
                    w = [m.rearrange("p (c n) -> p c n", c=per) for m in W.pair()]
                    for t in range(NT):
                        for k in range(per):
                            c = u * per + k
                            i = mm3(b[t][:, 0:width], hT_at(c, slice(t * P, (t + 1) * P)), [m[:, k, :] for m in w], c == 0, c == KC - 1)
                        if u == KC // per - 1:
                            i.then_inc(*acc.fills(name + (t,)))
                    if u < KC // per - 1:
                        piece_used(i)
                    else:
                        W.used(*acc.filled(name + (NT - 1,)))

            def hT_of(n):
                pe.wait_ge(S["normed"], ln.next(S["normed"]))
                turn_rows(n, rows, KC)
                pe.wait_ge(S["hT_ready"], ln.next(S["hT_ready"], 4))

            def out_product(l):
                for g in range(2):
                    rows_by(("out", l, g), COLS)

            def ffn(n, tag):
                hT_of(n)
                y = []
                for q in range(4):
                    pe.wait_ge(*acc.turn())
                    y.append(acc.fill(("y", tag, q)))

                def gate_up(f):
                    pe.wait_ge(*wk.turn())
                    b = wk.fill(("gu", tag, f))
                    pe.wait_ge(*W.parts(("gu", tag, f)))
                    w = [m.rearrange("p (c h n) -> p c h n", c=KC, h=2) for m in W.pair()]
                    for h in range(2):
                        for c in range(KC):
                            i = mm3(b[:, h * T:(h + 1) * T], [m[:, c, h, :] for m in w], hT_at(c, slice(0, T)), c == 0, c == KC - 1)
                    i.then_inc(*wk.fills(("gu", tag, f)))
                    W.used(*wk.filled(("gu", tag, f)))

                def down(s):
                    pe.wait_ge(*W.parts(("dn", tag, s)))
                    w = [m.rearrange("p (c n) -> p c n", c=FSTEP) for m in W.pair()]
                    pe.wait_ge(S["hid_ready"], ln.next(S["hid_ready"], FSTEP))
                    for k in range(FSTEP):
                        f = FSTEP * s + k
                        for t in range(NT):
                            x_ = slice(t * P, (t + 1) * P)
                            for h in range(2):
                                i = mm3(y[2 * t + h], (hidh[:, f % 4, x_], hidl[:, f % 4, x_]), [m[:, k, h * COLS:(h + 1) * COLS] for m in w],
                                        f == 0, f == FC - 1)
                                if f == FC - 1:
                                    i.then_inc(*acc.fills(("y", tag, 2 * t + h)))
                    if s < NSTEP - 1:
                        i.then_inc(S["down_done"], 1)
                        W.used(S["down_done"], (NSTEP - 1) * tag + s + 1)
                    else:
                        W.used(*acc.filled(("y", tag, 3)))

                for s in range(NSTEP):
                    for f in range(FSTEP * s, FSTEP * s + FSTEP):
                        gate_up(f)
                    if s >= 1:
                        down(s - 1)
                down(NSTEP - 1)

            pe.wait_ge(S["params_in"], 16 * len(P1))
            pe.wait_ge(S["setup_ready"], ln.next(S["setup_ready"]))
            for k, n in enumerate((NVEC, 88, 88)):
                pe.wait_ge(*wk.turn())
                b = wk.fill(("vec", k))
                tr(b[:, 0:n], vraw[0:n, k, :], ident[0:n, 0:n]).then_inc(*wk.fills(("vec", k)))
            pe.wait_ge(*wk.turn())
            b = wk.fill(("pe",))
            tr(b[0:HD, 0:P], peraw, ident[:]).then_inc(*wk.fills(("pe",)))
            pe.wait_ge(*wk.turn())
            b = wk.fill(("line",))
            mm(b[0:NH, :], relb[:], onehot, start=True, stop=True).then_inc(*wk.fills(("line",)))

            for l in range(DEPTH):
                hT_of(("mix", l))
                for g, (c0, c1_) in enumerate(IN_COLS):
                    rows_by(("in", l, g), c1_ - c0)
                pe.wait_ge(S["rotated"], ln.next(S["rotated"]))
                for t in range(NT):
                    for k, off in enumerate((O_RQ, O_RK)):
                        pe.wait_ge(*wk.turn())
                        b = wk.fill(("rT", l, t, k))
                        for q in range(3):
                            i = tr(b[:, q * P:(q + 1) * P], proj[:, t, off + q * P:off + (q + 1) * P], ident[:])
                        i.then_inc(*wk.fills(("rT", l, t, k)))
                pe.wait_ge(S["turned_ret"], ln.next(S["turned_ret"], 4))
                o = []
                for t in range(NT):
                    pe.wait_ge(*acc.turn())
                    o.append(acc.fill(("ro", l, t)))

                def ret_out(h):
                    pe.wait_ge(S["decayed"], ln.next(S["decayed"]))
                    s = sT[:, h % 2, :]
                    e = slice(h * HD, (h + 1) * HD)
                    v = [proj[:, t, O_RV + h * HD:O_RV + (h + 1) * HD] for t in range(NT)]
                    i = mm(o[0][:, e], s[:, 0:P], v[0], start=True, stop=True)
                    if h == NH - 1:
                        i.then_inc(*acc.fills(("ro", l, 0)))
                    mm(o[1][:, e], s[:, P:2 * P], v[0], start=True, stop=False)
                    i = mm(o[1][:, e], s[:, 2 * P:3 * P], v[1], start=False, stop=True)
                    if h == NH - 1:
                        i.then_inc(*acc.fills(("ro", l, 1)))
                    else:
                        i.then_inc(S["ret_mixed"], 1)

                for h in range(NH):
                    pe.wait_ge(*wk.turn())
                    b = wk.fill(("rs", l, h))
                    r = slice(HD * (h % 2), HD * (h % 2) + HD)
                    mm(b[:, 0:T], kTr[r, h // 2, 0:P], qTr[r, h // 2, :], start=True, stop=True)
                    mm(b[:, T:T + P], kTr[r, h // 2, P:T], qTr[r, h // 2, P:T], start=True, stop=True).then_inc(*wk.fills(("rs", l, h)))
                    if h >= 1:
                        ret_out(h - 1)
                ret_out(NH - 1)
                for j in range(2):
                    pe.wait_ge(*wk.turn())
                    b = wk.fill(("aT", l, j))
                    for g in range(2):
                        for t in range(NT):
                            c = O_KV + j * P + g * HD
                            i = tr(b[0:HD, (g * NT + t) * P:(g * NT + t + 1) * P], proj[:, t, c:c + HD], ident[:])
                    i.then_inc(*wk.fills(("aT", l, j)))
                pe.wait_ge(S["nsa_rows"], ln.next(S["nsa_rows"]))
                for t in range(NT):
                    pe.wait_ge(*wk.turn())
                    b = wk.fill(("nqT", l, t))
                    for q in range(3):
                        i = tr(b[:, q * P:(q + 1) * P], qn[:, t, q * P:(q + 1) * P], ident[:])
                    i.then_inc(*wk.fills(("nqT", l, t)))
                pe.wait_ge(*wk.turn())
                b = wk.fill(("nkT", l))
                for br in range(2):
                    for t in range(NT):
                        i = tr(b[:, (br * NT + t) * P:(br * NT + t + 1) * P], kn[:, t, br * P:(br + 1) * P], ident[:])
                i.then_inc(*wk.fills(("nkT", l)))
                pe.wait_ge(*wk.turn())
                b = wk.fill(("wsT", l))
                for g in range(4):
                    i = tr(b[:, g * P:(g + 1) * P], gmws[:, l, g, :], ident[:])
                i.then_inc(*wk.fills(("wsT", l)))
                pe.wait_ge(S["blocks_ready"], ln.next(S["blocks_ready"]))
                pe.wait_ge(*wk.turn())
                b = wk.fill(("h1", l))
                for j in range(2):
                    pe.wait_ge(*W.load(("w1", l, j)))
                    w1 = W.plain()[0:HD].rearrange("p (l h) -> p l h", l=CMP_LEN)
                    for k in range(CMP_LEN):
                        i = mm(b[0:HD, j * 32:j * 32 + 30], w1[:, k, :], blk[:, j, k, :], start=(k == 0), stop=(k == CMP_LEN - 1))
                    W.release(*wk.filled(("h1", l)))
                i.then_inc(*wk.fills(("h1", l)))
                pe.wait_ge(S["h1_ready"], ln.next(S["h1_ready"]))
                pe.wait_ge(*wk.turn())
                b = wk.fill(("kc", l))
                for j in range(2):
                    for g in range(2):
                        c = (j * 2 + g) * HD
                        i = mm(b[0:NCMP, c:c + HD], h1[:, j, g * NCMP:(g + 1) * NCMP], cw2[:, 2 * l + j, :], start=True, stop=True)
                i.then_inc(*wk.fills(("kc", l)))
                pe.wait_ge(S["gm_rows"], ln.next(S["gm_rows"]))
                pe.wait_ge(*acc.turn())
                b = acc.fill(("gm", l))
                for g in range(4):
                    i = mm(b[:, g * P:(g + 1) * P].rearrange("p (t n) -> p t n", t=NT), wsT[:, g, :],
                           vn[:, :, g * HD:(g + 1) * HD], start=True, stop=True)
                i.then_inc(*acc.fills(("gm", l)))
                pe.wait_ge(S["kc_rows"], ln.next(S["kc_rows"]))
                pe.wait_ge(*wk.turn())
                b = wk.fill(("kcT", l))
                tr(b[:, 0:NCMP], kcn[0:NCMP, :], ident[0:NCMP, 0:NCMP]).then_inc(*wk.fills(("kcT", l)))
                pe.wait_ge(S["nsa_turned"], ln.next(S["nsa_turned"], 3))
                pe.wait_ge(S["kTc_ready"], ln.next(S["kTc_ready"]))
                for g in range(2):
                    pe.wait_ge(*wk.turn())
                    b = wk.fill(("sc", l, g))
                    r = slice(HD * g, HD * g + HD)
                    for t in range(NT):
                        for q in range(HPG):
                            c = (t * HPG + q) * 16
                            i = mm(b[:, c:c + NCMP], qTn[r, q, t * P:(t + 1) * P], kTc[r, 0:NCMP], start=True, stop=True)
                    i.then_inc(*wk.fills(("sc", l, g)))
                steps = [(t, h) for t in range(NT) for h in range(NH)]
                banks = {}

                def score(n):
                    t, h = steps[n]
                    g, q = h // HPG, h % HPG
                    r = slice(HD * g, HD * g + HD)
                    K = P * (t + 1)
                    pe.wait_ge(*wk.turn())
                    b = wk.fill(("s", l, n))
                    for br in range(2):
                        i = mm(b[:, br * T:br * T + K], qTn[r, q, t * P:(t + 1) * P], kTn[r, br, 0:K], start=True, stop=True)
                    i.then_inc(*wk.fills(("s", l, n)))

                def turn_probs(n):
                    t, h = steps[n]
                    pe.wait_ge(S["probs_ready"], ln.next(S["probs_ready"]))
                    pe.wait_ge(*wk.turn())
                    b = wk.fill(("pT", l, n))
                    for br in range(2):
                        for k in range(t + 1):
                            c = (br * (t + 1) + k) * P
                            i = tr(b[:, c:c + P], p_sb[:, n % 2, br * T + k * P:br * T + (k + 1) * P], ident[:])
                    i.then_inc(*wk.fills(("pT", l, n)))

                def weigh(n):
                    t, h = steps[n]
                    if h == 0:
                        for br in range(3):
                            pe.wait_ge(*acc.turn())
                            banks[br] = acc.fill(("no", l, t, br))
                        if t == 0:
                            pe.wait_ge(S["cmp_turned"], ln.next(S["cmp_turned"], 3))
                    g = h // HPG
                    e = slice(h * HD, (h + 1) * HD)
                    i = mm(banks[0][:, e], pcT[0:NCMP, t * NH + h, :], kc[0:NCMP, P + g * HD:P + (g + 1) * HD], start=True, stop=True)
                    if h == NH - 1:
                        i.then_inc(*acc.fills(("no", l, t, 0)))
                    pe.wait_ge(S["probsT_ready"], ln.next(S["probsT_ready"]))
                    for br in range(2):
                        c = O_KV + (1 + br) * 256 + P + g * HD
                        for k in range(t + 1):
                            i = mm(banks[1 + br][:, e], pT[:, n % 2, (br * (t + 1) + k) * P:(br * (t + 1) + k + 1) * P],
                                   proj[:, k, c:c + HD], start=(k == 0), stop=(k == t))
                        if h == NH - 1:
                            i.then_inc(*acc.fills(("no", l, t, 1 + br)))
                    if h < NH - 1:
                        i.then_inc(S["pv_done"], 1)

                for n in range(len(steps) + 2):
                    if n < len(steps):
                        score(n)
                    if n == 1:
                        pe.wait_ge(S["cmp_probs"], ln.next(S["cmp_probs"]))
                        for k in range(3):
                            pe.wait_ge(*wk.turn())
                            b = wk.fill(("pcT", l, k))
                            for q in range(4):
                                i = tr(b[0:NCMP, q * P:(q + 1) * P], s_c[:, 4 * k + q, :], ident[:])
                            i.then_inc(*wk.fills(("pcT", l, k)))
                    if 1 <= n <= len(steps):
                        turn_probs(n - 1)
                    if n >= 2:
                        weigh(n - 2)
                pe.wait_ge(S["mixed"], ln.next(S["mixed"]))
                turn_rows(("mixed", l), rows, KC)
                for t in range(NT):
                    for q in range(2):
                        pe.wait_ge(*wk.freed(("T", ("mixed", l), t, q)))
                out_product(l)
                ffn(("ffn", l), l)
                if l == DEPTH - 1:
                    pe.wait_ge(S["s5_pad"], ln.next(S["s5_pad"]))
                    for r in range(2):
                        pe.wait_ge(*wk.turn())
                        b = wk.fill(("bbT", r))
                        for k in range(4):
                            i = tr(b[:, k * P:(k + 1) * P], bpad[r][:, 4 * k:4 * k + 4, :].rearrange("p i n -> p (i n)"), ident[:])
                        i.then_inc(*wk.fills(("bbT", r)))
                        pe.wait_ge(*wk.turn())
                        b = wk.fill(("cT", r))
                        for k in range(4):
                            i = tr(b[:, k * P:(k + 1) * P], cpad[r][:, k, :], ident[:])
                        i.then_inc(*wk.fills(("cT", r)))

            hT_of(("mix", 2))
            for g in (1, 0, 2, 3, 4):
                if g in (2, 3):
                    rows_by(("even", g), COLS)
                    continue
                for q in range(2):
                    pe.wait_ge(*acc.turn())
                    b = acc.fill(("even", g, q))
                    pe.wait_ge(*W.parts((("even", g), q)))
                    w = [m.rearrange("p (c n) -> p c n", c=KC) for m in W.pair()]
                    for k in range(2):
                        for c in range(KC):
                            i = mm3(b[:, k * T:(k + 1) * T], [m[:, c, k * P:(k + 1) * P] for m in w], hT_at(c, slice(0, T)), c == 0, c == KC - 1)
                    i.then_inc(*acc.fills(("even", g, q)))
                    W.used(*acc.filled(("even", g, q)))
            pe.wait_ge(S["hg_q"], ln.next(S["hg_q"]))
            pe.wait_ge(*wk.turn())
            b = wk.fill(("att",))
            for n in range(NCH):
                t, po = n // 2, HC * (n % 2)
                for h in range(HG):
                    c = (t * HG + h) * HC
                    i = mm(b[po:po + HC, c:c + HC], bcum[:, h, n * HC:(n + 1) * HC], eb[:, h, n * HC:(n + 1) * HC], start=True, stop=True)
            i.then_inc(*wk.fills(("att",)))
            pe.wait_ge(S["hg_kk"], ln.next(S["hg_kk"]))
            for t in range(NT):
                pe.wait_ge(*wk.turn())
                b = wk.fill(("kkT", t))
                for h in range(HG):
                    i = tr(b[:, h * P:(h + 1) * P], key[:, h, t * P:(t + 1) * P], ident[:])
                i.then_inc(*wk.fills(("kkT", t)))
            pe.wait_ge(S["hg_kkT"], ln.next(S["hg_kkT"], 2))
            for n in range(NCH - 1):
                t, po = n // 2, HC * (n % 2)
                pe.wait_ge(*wk.turn())
                b = wk.fill(("ds", n))
                for h in range(HG):
                    i = mm(b[:, h * P:(h + 1) * P], kk[po:po + HC, t, h, :], eg[po:po + HC, t, h * P:(h + 1) * P], start=True, stop=True)
                i.then_inc(*wk.fills(("ds", n)))
            pe.wait_ge(S["hg_att"], ln.next(S["hg_att"]))
            o = []
            for t in range(NT):
                pe.wait_ge(*acc.turn())
                o.append(acc.fill(("eo", t)))
            for n in range(NCH):
                t, po = n // 2, HC * (n % 2)
                if n:
                    pe.wait_ge(S["hg_state"], ln.next(S["hg_state"]))
                for h in range(HG):
                    dst = o[t][po:po + HC, h * P:(h + 1) * P]
                    i = mm(dst, att[po:po + HC, t * HG + h, :], eg[po:po + HC, t, h * P:(h + 1) * P], start=True, stop=(n == 0))
                    if n:
                        i = mm(dst, eb[:, h, n * HC:(n + 1) * HC], state[:, n - 1, h, :], start=False, stop=True)
                if n % 2:
                    i.then_inc(*acc.fills(("eo", t)))
            for q in range(4):
                for j in range(4):
                    pe.wait_ge(*wk.turn())
                    b = wk.fill(("bu", q, j))
                    r = slice(32 * j, 32 * j + 32)
                    mm(b[:, 0:T], bbT[r, 0, q, :], uT[r, q, :], start=True, stop=True, tile_position=(32 * j, 0))
                    mm(b[:, T:2 * T], bbT[r, 1, q, :], uT[r, q, :], start=True, stop=True, tile_position=(32 * j, 0)).then_inc(*wk.fills(("bu", q, j)))
                pe.wait_ge(S["states_ready"], ln.next(S["states_ready"]))
                pe.wait_ge(*acc.turn())
                b = acc.fill(("sy", q))
                for j in range(4):
                    r = slice(32 * j, 32 * j + 32)
                    mm(b[r, 0:T], cT[:, 0, q, r], m1[:, j, :], start=True, stop=False)
                    i = mm(b[r, 0:T], cT[:, 1, q, r], m3[:, j, :], start=False, stop=True)
                i.then_inc(*acc.fills(("sy", q)))
            pe.wait_ge(*W.load(("glu", 0)))
            w = W.plain().rearrange("p (c n) -> p c n", c=4)
            pe.wait_ge(S["s5_z"], ln.next(S["s5_z"], 4))
            for q in range(2):
                pe.wait_ge(*acc.turn())
                b = acc.fill(("glu", q))
                for k in range(2):
                    for c in range(4):
                        i = mm(b[:, k * T:(k + 1) * T], w[:, c, (2 * q + k) * P:(2 * q + k + 1) * P], zT[:, c, :], start=(c == 0), stop=(c == 3))
                i.then_inc(*acc.fills(("glu", q)))
            W.release(*acc.filled(("glu", 1)))
            pe.wait_ge(S["mixed"], ln.next(S["mixed"]))
            for t in range(NT):
                pe.wait_ge(*wk.turn())
                b = wk.fill(("eT", t))
                for h in range(HG):
                    i = tr(b[:, h * P:(h + 1) * P], rows[:, t, h * P:(h + 1) * P], ident[:])
                i.then_inc(*wk.fills(("eT", t)))
            pe.wait_ge(S["hT_ready"], ln.next(S["hT_ready"], 4))
            out_product(2)
            ffn(("ffn", 2), 2)

            hT_of(("mix", 3))
            for g, (c0, c1_) in enumerate(ODD_COLS):
                rows_by(("odd", g), c1_ - c0)
            pe.wait_ge(S["odd_rows"], ln.next(S["odd_rows"]))
            for t in range(NT):
                pe.wait_ge(*wk.turn())
                b = wk.fill(("oT", t, 0))
                for c in range(3):
                    i = tr(b[:, c * P:(c + 1) * P], oin[:, t, c * P:(c + 1) * P], ident[:])
                i.then_inc(*wk.fills(("oT", t, 0)))
                pe.wait_ge(*wk.turn())
                b = wk.fill(("oT", t, 1))
                for c in range(2):
                    tr(b[:, c * P:(c + 1) * P], oin[:, t, MQ + c * P:MQ + (c + 1) * P], ident[:])
                tr(b[:, 2 * P:3 * P], kr[:, t, :], ident[:]).then_inc(*wk.fills(("oT", t, 1)))
            pe.wait_ge(S["odd_T"], ln.next(S["odd_T"], 4))
            for q in range(4):
                pe.wait_ge(*W.load((("uq", q), 0)))
                w = W.plain().rearrange("p (c h n) -> p c h n", c=3, h=2)
                pe.wait_ge(*acc.turn())
                b = acc.fill(("qn", q))
                for k in range(2):
                    for c in range(3):
                        i = mm(b[:, k * T:(k + 1) * T], w[:, c, k, 0:MN], cqT[:, c, :], start=(c == 0), stop=(c == 2))
                i.then_inc(*acc.fills(("qn", q)))
                pe.wait_ge(*acc.turn())
                b = acc.fill(("qr", q))
                for t in range(NT):
                    for c in range(3):
                        i = mm(b[:, t * P:(t + 1) * P].rearrange("p (h n) -> p h n", h=2), cqT[:, c, t * P:(t + 1) * P], w[:, c, :, MN:MQK],
                               start=(c == 0), stop=(c == 2))
                i.then_inc(*acc.fills(("qr", q)))
                W.release(*acc.filled(("qr", q)))
            for g in range(2):
                pe.wait_ge(*W.load((("ukv", g), 0)))
                w = W.plain().rearrange("p (c h n) -> p c h n", c=2, h=4)
                for q in range(2):
                    pe.wait_ge(*acc.turn())
                    b = acc.fill(("kn", 2 * g + q))
                    for k in range(2):
                        for c in range(2):
                            i = mm(b[:, k * T:(k + 1) * T], w[:, c, 2 * q + k, 0:MN], ckvT[:, c, :], start=(c == 0), stop=(c == 1))
                    i.then_inc(*acc.fills(("kn", 2 * g + q)))
                for t in range(NT):
                    pe.wait_ge(*acc.turn())
                    b = acc.fill(("v", t, g))
                    for c in range(2):
                        i = mm(b.rearrange("p (h n) -> p h n", h=4), ckvT[:, c, t * P:(t + 1) * P], w[:, c, :, MN:MN + MV],
                               start=(c == 0), stop=(c == 1))
                    i.then_inc(*acc.fills(("v", t, g)))
                W.release(*acc.filled(("v", NT - 1, g)))
            pe.wait_ge(S["qrope_rows"], ln.next(S["qrope_rows"]))
            for t in range(NT):
                pe.wait_ge(*wk.turn())
                b = wk.fill(("qrT", t))
                for q in range(4):
                    i = tr(b[:, q * P:(q + 1) * P], qr[:, t, q * P:(q + 1) * P], ident[:])
                i.then_inc(*wk.fills(("qrT", t)))
            pe.wait_ge(S["qrope_T"], ln.next(S["qrope_T"], 2))
            for q in range(4):
                pe.wait_ge(*acc.freed(("qn", q)))
                pe.wait_ge(*acc.freed(("kn", q)))
                pe.wait_ge(*acc.freed(("v", q % 2, q // 2)))
            steps = [(t, h) for t in range(NT) for h in range(MH)]
            for n in range(len(steps) + 2):
                if n < len(steps):
                    t, h = steps[n]
                    K = P * (t + 1)
                    r = slice(HD * (h % 2), HD * (h % 2) + HD)
                    pe.wait_ge(*wk.turn())
                    b = wk.fill(("ms", n))
                    mm(b[:, 0:K], qnT[:, h, t * P:(t + 1) * P], knT[:, h, 0:K], start=True, stop=False)
                    mm(b[:, 0:K], qrT[r, h // 2, t * P:(t + 1) * P], krT[r, 0:K], start=False, stop=True).then_inc(*wk.fills(("ms", n)))
                if 1 <= n <= len(steps):
                    t, h = steps[n - 1]
                    pe.wait_ge(S["m_norm"], ln.next(S["m_norm"]))
                    pe.wait_ge(*wk.turn())
                    b = wk.fill(("mpT", n - 1))
                    for k in range(t + 1):
                        i = tr(b[:, k * P:(k + 1) * P], mp[:, (n - 1) % 2, k * P:(k + 1) * P], ident[:])
                    i.then_inc(*wk.fills(("mpT", n - 1)))
                if n >= 2:
                    t, h = steps[n - 2]
                    if h % 4 == 0:
                        pe.wait_ge(*acc.turn())
                        b2 = acc.fill(("mo", t, h // 4))
                    pe.wait_ge(S["m_probsT"], ln.next(S["m_probsT"]))
                    for k in range(t + 1):
                        i = mm(b2[:, (h % 4) * P:(h % 4 + 1) * P], vt[:, k, h * MV:(h + 1) * MV], mpT[:, n % 2, k * P:(k + 1) * P],
                               start=(k == 0), stop=(k == t))
                    if h % 4 == 3:
                        i.then_inc(*acc.fills(("mo", t, h // 4)))
                    else:
                        i.then_inc(S["m_pv"], 1)
            for t in range(NT):
                for q in range(2):
                    pe.wait_ge(*acc.freed(("mo", t, q)))
            out_product(3)
            ffn(("ffn", 3), 3)

        @block.scalar
        def _(act):
            ln, own = Counts(), S["act_chain"]
            fn = nc.scalar.activation

            def norm():
                for t in range(NT):
                    act.wait_ge(S["x_ready"], ln.next(S["x_ready"]))
                    fn(rows[:, t, :], x[:, t, :], ACT.Square, accum_out=ss[:, t:t + 1]).then_inc(S["norm_sums"], 1)
                    act.wait_ge(S["norm_sums"], ln.made(S["norm_sums"]))
                act.wait_ge(S["norm_scale"], ln.next(S["norm_scale"]))
                fn(rows[:, 0, :], x[:, 0, :], ACT.Copy, scale=rs[:, 0:1]).then_inc(own, 1)
                act.wait_ge(own, ln.made(own))
                fn(rows[:, 1, :], x[:, 1, :], ACT.Copy, scale=rs[:, 1:2]).then_inc(S["normed"], 1)
                act.wait_ge(S["normed"], ln.made(S["normed"]))

            highs = [0]

            def split_high(n):
                for k in range(highs[0], min(highs[0] + n, len(W.split))):
                    act.wait_ge(*W.loaded(k))
                    if k >= NPAIR:
                        act.wait_ge(*W.emptied(k))
                    fn(W.pair(k)[0], W.source(k), ACT.Copy).then_inc(S["w_high"], 1)
                    highs[0] = k + 1

            def hT_high(n, t, q):
                act.wait_ge(*wk.freed(("T", n, t, q)))
                fn(hTh[:, 4 * q:4 * q + 4, t * P:(t + 1) * P], stage[:, q, :].rearrange("p (k n) -> p k n", k=4), ACT.Copy).then_inc(S["hT_high"], 1)

            def normed_high(n):
                for t in range(NT):
                    for q in range(2):
                        hT_high(n, t, q)
                split_high(1)

            def mixed_high(l):
                for t in range(NT):
                    for q in range(2):
                        act.wait_ge(*wk.filled(("T", ("mixed", l), t, q)))
                        b = wk.bank(("T", ("mixed", l), t, q)).rearrange("p (k n) -> p k n", k=4)
                        fn(hTh[:, 4 * q:4 * q + 4, t * P:(t + 1) * P], b, ACT.Copy).then_inc(S["hT_high"], 1)

            def s5_steps(s):
                if s == 2:
                    act.wait_ge(S["s5_params_in"], 16 * len(P2))
                    fn(prm[:, 3, :], prm[:, 2, :], ACT.Exp).then_inc(S["s5_dt"], 1)
                    act.wait_ge(S["s5_dt"], ln.made(S["s5_dt"]))
                if s == 4:
                    act.wait_ge(S["s5_arg"], ln.next(S["s5_arg"]))
                    fn(mag, prm[:, 4, :], ACT.Exp).then_inc(own, 1)
                    act.wait_ge(own, ln.made(own))
                    fn(prm[:, 6, :], prm[:, 5, :], ACT.Abs).then_inc(own, 1)
                    act.wait_ge(own, ln.made(own))
                    fn(prm[:, 6, :], prm[:, 6, :], ACT.Sin, scale=-1.0, bias=halfpi[:]).then_inc(own, 1)
                    act.wait_ge(own, ln.made(own))
                    fn(prm[:, 7, :], prm[:, 5, :], ACT.Sin).then_inc(S["s5_trig"], 1)
                    act.wait_ge(S["s5_trig"], ln.made(S["s5_trig"]))

            def ffn(n, tag):
                normed_high(n)
                v = vecs[:, tag - 1, :] if tag >= 2 else None
                for s in range(NSTEP):
                    chunks = range(FSTEP * s, FSTEP * s + FSTEP)
                    if tag == DEPTH - 1:
                        s5_steps(s)
                    split_high(1)
                    for f in chunks:
                        act.wait_ge(*wk.filled(("gu", tag, f)))
                        b = wk.bank(("gu", tag, f))
                        if f >= 4:
                            act.wait_ge(S["hid_ready"], FC * tag + f - 3)
                        if tag < 2:
                            fn(sg[:, f % 4, :], b[:, 0:T], ACT.Silu).then_inc(S["act_silu"], 1)
                        else:
                            fn(sg[:, f % 4, :], b[:, 0:T], ACT.Identity, scale=v[:, 44 + f:45 + f], bias=v[:, 66 + f:67 + f]).then_inc(S["conv_in"], 1)
                    if tag >= 2:
                        for f in chunks:
                            act.wait_ge(S["conv_done"], ln.next(S["conv_done"]))
                            fn(sg[:, f % 4, :], sg[:, f % 4, :], ACT.Silu).then_inc(S["act_silu"], 1)
                    split_high(1)
                    for f in chunks:
                        act.wait_ge(*wk.freed(("gu", tag, f)))
                        if s >= 2:
                            act.wait_ge(S["down_done"], (NSTEP - 1) * tag + s - 1)
                        fn(hidh[:, f % 4, :], sg[:, f % 4, :], ACT.Copy).then_inc(S["hid_high"], 1)
                    if s:
                        split_high(1)

            for dst, src in P1:
                act.dma_start(dst, src, allow_slow_non_contiguous=True).then_inc(S["params_in"], 16)
            act.wait_ge(*wk.filled(("line",)))
            b = wk.bank(("line",))
            fn(line, b[0:NH, :], ACT.Copy).then_inc(*wk.frees(("line",)))
            act.wait_ge(*wk.freed(("line",)))
            act.dma_start(bias_line.ap(), line.unsqueeze(1).to_broadcast([NH, P, LINE])).then_inc(S["line_out"], 16)
            act.wait_ge(S["line_out"], 16)
            for h in range(NH):
                act.dma_start(bias[:, h, :], bass.AP(bias_line, h * P * LINE + P - 1, [[LINE - 1, P], [1, 3 * P]])).then_inc(S["bias_in"], 16)

            split_high(NPAIR - 1)
            act.wait_ge(S["lb_arg"], ln.next(S["lb_arg"]))
            fn(lbt[:, 0:8], lbt[:, 0:8], ACT.Exp).then_inc(S["lb_exp"], 1)
            act.wait_ge(S["lb_exp"], ln.made(S["lb_exp"]))

            for l in range(DEPTH):
                norm()
                normed_high(("mix", l))
                for g, (c0, c1_) in enumerate(IN_COLS):
                    if g < 5:
                        split_high(1)
                    for t in range(NT):
                        act.wait_ge(*acc.filled(("in", l, g, t)))
                        b = acc.bank(("in", l, g, t))
                        fn(proj[:, t, c0:c1_], b[:, 0:c1_ - c0], ACT.Copy).then_inc(*acc.frees(("in", l, g, t)))
                        act.wait_ge(*acc.freed(("in", l, g, t)))
                        act.sem_inc(S["proj_ready"], 1)
                    if g < 5:
                        split_high(1)
                split_high(1)
                for t in range(NT):
                    for k, dst in enumerate((qTr, kTr)):
                        act.wait_ge(*wk.filled(("rT", l, t, k)))
                        b = wk.bank(("rT", l, t, k))
                        fn(dst[:, :, t * P:(t + 1) * P], b[:, 0:384].rearrange("p (b n) -> p b n", b=3), ACT.Copy).then_inc(*wk.frees(("rT", l, t, k)))
                        act.wait_ge(*wk.freed(("rT", l, t, k)))
                        act.sem_inc(S["turned_ret"], 1)
                fn(proj[:, :, O_GM:IN_W], proj[:, :, O_GM:IN_W], ACT.Gelu_apprx_tanh).then_inc(S["gelu_ready"], 1)
                act.wait_ge(S["gelu_ready"], ln.made(S["gelu_ready"]))
                fn(gate.rearrange("p t h b -> p t (h b)"), proj[:, :, O_NG:O_GM], ACT.Tanh, scale=0.5).then_inc(S["gates_ready"], 1)
                act.wait_ge(S["gates_ready"], ln.made(S["gates_ready"]))
                for j in range(2):
                    act.wait_ge(*wk.filled(("aT", l, j)))
                    b = wk.bank(("aT", l, j))
                    fn(aT[:, j].rearrange("p g n -> p (g n)"), b[0:HD, :], ACT.Copy).then_inc(*wk.frees(("aT", l, j)))
                    act.wait_ge(*wk.freed(("aT", l, j)))
                    act.sem_inc(S["blocks_read"], 1)
                for t in range(NT):
                    act.wait_ge(*wk.filled(("nqT", l, t)))
                    b = wk.bank(("nqT", l, t))
                    fn(qTn[:, :, t * P:(t + 1) * P], b[:, 0:384].rearrange("p (b n) -> p b n", b=3), ACT.Copy).then_inc(*wk.frees(("nqT", l, t)))
                    act.wait_ge(*wk.freed(("nqT", l, t)))
                    act.sem_inc(S["nsa_turned"], 1)
                act.wait_ge(*wk.filled(("nkT", l)))
                b = wk.bank(("nkT", l))
                fn(kTn.rearrange("p b n -> p (b n)"), b, ACT.Copy).then_inc(*wk.frees(("nkT", l)))
                act.wait_ge(*wk.freed(("nkT", l)))
                act.sem_inc(S["nsa_turned"], 1)
                act.wait_ge(*wk.filled(("h1", l)))
                b = wk.bank(("h1", l))
                fn(h1, b[0:HD, 0:64].rearrange("p (j n) -> p j n", j=2)[:, :, 0:30], ACT.Gelu_apprx_tanh).then_inc(*wk.frees(("h1", l)))
                act.wait_ge(*wk.freed(("h1", l)))
                act.sem_inc(S["h1_ready"], 1)
                fn(proj[:, :, O_RG:O_NQ], proj[:, :, O_RG:O_NQ], ACT.Silu).then_inc(S["silu_ready"], 1)
                act.wait_ge(S["silu_ready"], ln.made(S["silu_ready"]))
                act.wait_ge(S["cmp_scores"], ln.next(S["cmp_scores"]))
                fn(s_c, s_c, ACT.Exp).then_inc(S["cmp_exp"], 1)
                act.wait_ge(S["cmp_exp"], ln.made(S["cmp_exp"]))

                def exps(n):
                    t, h = n // NH, n % NH
                    K = P * (t + 1)
                    act.wait_ge(S["scores_ready"], ln.next(S["scores_ready"]))
                    for br in range(2):
                        i = fn(p_sb[:, n % 2, br * T:br * T + K], s_sb[:, n % 2, br * T:br * T + K], ACT.Exp,
                               bias=nmax[:, 2 * (n % 2) + br:2 * (n % 2) + br + 1], accum_out=lsum[:, t, h, 1 + br:2 + br])
                        to = S["probs_ready"] if br else own
                        i.then_inc(to, 1)
                        act.wait_ge(to, ln.made(to))

                def probsT(n):
                    t = n // NH
                    w = 2 * (t + 1) * P
                    if n >= 2 and (n - 2) % NH < NH - 1:
                        act.wait_ge(S["pv_done"], (NH - 1) * (NT * l + (n - 2) // NH) + (n - 2) % NH + 1)
                    elif n >= 2:
                        act.wait_ge(*acc.filled(("no", l, (n - 2) // NH, 2)))
                    act.wait_ge(*wk.filled(("pT", l, n)))
                    b = wk.bank(("pT", l, n))
                    fn(pT[:, n % 2, 0:w], b[:, 0:w], ACT.Copy).then_inc(*wk.frees(("pT", l, n)))
                    act.wait_ge(*wk.freed(("pT", l, n)))
                    act.sem_inc(S["probsT_ready"], 1)

                for n in range(NT * NH + 1):
                    if n < NT * NH:
                        exps(n)
                    if n == 0:
                        for k in range(3):
                            act.wait_ge(*wk.filled(("pcT", l, k)))
                            b = wk.bank(("pcT", l, k))
                            fn(pcT[0:NCMP, 4 * k:4 * k + 4, :], b[0:NCMP, :].rearrange("p (q n) -> p q n", q=4), ACT.Copy).then_inc(*wk.frees(("pcT", l, k)))
                            act.wait_ge(*wk.freed(("pcT", l, k)))
                            act.sem_inc(S["cmp_turned"], 1)
                    if n >= 1:
                        probsT(n - 1)
                    if n in (6, 8):
                        split_high(1)
                mixed_high(l)
                split_high(3)
                if l == DEPTH - 1:
                    act.wait_ge(S["mixed"], ln.next(S["mixed"], DEPTH))
                    for dst, src in P2:
                        act.dma_start(dst, src, allow_slow_non_contiguous=True).then_inc(S["s5_params_in"], 16)
                norm()
                ffn(("ffn", l), l)

            norm()
            normed_high(("mix", 2))
            for g in (1, 0, 2, 3, 4):
                if g < 4:
                    split_high(1)
                for q in range(2):
                    act.wait_ge(*acc.filled(("even", g, q)))
                    b = acc.bank(("even", g, q))
                    if g == 1:
                        fn(lf[:, 2 * q:2 * q + 2, :].rearrange("p h n -> p (h n)"), b, ACT.Tanh, scale=0.5).then_inc(*acc.frees(("even", g, q)))
                        act.wait_ge(*acc.freed(("even", g, q)))
                        act.sem_inc(S["hg_tanh"], 1)
                    elif g in (0, 4):
                        dst = qTe if g == 0 else uT
                        fn(dst[:, 2 * q:2 * q + 2, :].rearrange("p h n -> p (h n)"), b, ACT.Copy).then_inc(*acc.frees(("even", g, q)))
                        act.wait_ge(*acc.freed(("even", g, q)))
                        act.sem_inc(S["proj_ready"], 1)
                    else:
                        fn(eg[:, q, (g - 2) * 512:(g - 1) * 512], b, ACT.Copy).then_inc(*acc.frees(("even", g, q)))
                        act.wait_ge(*acc.freed(("even", g, q)))
                        act.sem_inc(S["proj_ready"], 1)
                if g in (0, 1, 2):
                    split_high(1)
            split_high(2)
            act.wait_ge(S["hg_forget"], ln.next(S["hg_forget"]))
            fn(lf, lf, ACT.Ln).then_inc(S["hg_ln"], 1)
            act.wait_ge(S["hg_ln"], ln.made(S["hg_ln"]))
            act.wait_ge(S["hg_cum"], ln.next(S["hg_cum"]))
            fn(eb, bcum, ACT.Exp).then_inc(own, 1)
            act.wait_ge(own, ln.made(own))
            act.wait_ge(S["hg_cum"], ln.next(S["hg_cum"]))
            fn(bcum, bcum, ACT.Exp, scale=-1.0).then_inc(S["hg_exp"], 1)
            act.wait_ge(S["hg_exp"], ln.made(S["hg_exp"]))
            fn(lf, lf, ACT.Exp).then_inc(S["hg_exp"], 1)
            act.wait_ge(S["hg_exp"], ln.made(S["hg_exp"]))
            for t in range(NT):
                act.wait_ge(*wk.filled(("kkT", t)))
                b = wk.bank(("kkT", t))
                fn(kk[:, t].rearrange("p h n -> p (h n)"), b, ACT.Copy).then_inc(*wk.frees(("kkT", t)))
                act.wait_ge(*wk.freed(("kkT", t)))
                act.sem_inc(S["hg_kkT"], 1)
            fn(eg[:, :, 512:1024], eg[:, :, 512:1024], ACT.Silu).then_inc(S["silu_ready"], 1)
            act.wait_ge(S["silu_ready"], ln.made(S["silu_ready"]))
            for q in range(4):
                if q:
                    act.wait_ge(S["states_used"], q)
                else:
                    act.wait_ge(S["hg_out"], ln.next(S["hg_out"]))
                for j in range(4):
                    act.wait_ge(*wk.filled(("bu", q, j)))
                    b = wk.bank(("bu", q, j))
                    fn(bu[0][:, j, :], b[:, 0:T], ACT.Copy).then_inc(own, 1)
                    act.wait_ge(own, ln.made(own))
                    fn(bu[1][:, j, :], b[:, T:2 * T], ACT.Copy).then_inc(*wk.frees(("bu", q, j)))
                    act.wait_ge(*wk.freed(("bu", q, j)))
                act.sem_inc(S["drive_ready"], 1)
            for q in range(4):
                act.wait_ge(S["s5_y"], ln.next(S["s5_y"]))
                fn(zT[:, q, :], uT[:, q, :], ACT.Gelu_apprx_tanh).then_inc(S["s5_z"], 1)
                act.wait_ge(S["s5_z"], ln.made(S["s5_z"]))
            for q in range(2):
                act.wait_ge(*acc.filled(("glu", q)))
                b = acc.bank(("glu", q))
                for k in range(2):
                    i = fn(qTe[:, 2 * q + k, :], b[:, k * T:(k + 1) * T], ACT.Tanh, scale=0.5, bias=small2[:, 8 + 2 * q + k:9 + 2 * q + k])
                    if k:
                        i.then_inc(*acc.frees(("glu", q)))
                        act.wait_ge(*acc.freed(("glu", q)))
                    else:
                        i.then_inc(own, 1)
                        act.wait_ge(own, ln.made(own))
                act.sem_inc(S["glu_tanh"], 1)
            split_high(1)
            for t in range(NT):
                act.wait_ge(*wk.freed(("eT", t)))
                fn(hTh[:, 0:4, t * P:(t + 1) * P], stage[:, t, :].rearrange("p (k n) -> p k n", k=4), ACT.Copy).then_inc(S["hT_high"], 1)
            for q in range(2):
                act.wait_ge(S["z_gated"], ln.next(S["z_gated"]))
                fn(hTh[:, 4 + 2 * q:6 + 2 * q, :], zT[:, 2 * q:2 * q + 2, :], ACT.Copy).then_inc(S["hT_high"], 1)
            split_high(3)
            norm()
            ffn(("ffn", 2), 2)

            act.wait_ge(S["pos_arg"], ln.next(S["pos_arg"]))
            act.dma_start(fg, a["final_norm_g_2"].partition_broadcast(P)).then_inc(S["mla_in"], 16)
            fn(mang[:, 1], mang[:, 0], ACT.Abs).then_inc(own, 1)
            act.wait_ge(own, ln.made(own))
            fn(mang[:, 2], mang[:, 1], ACT.Sin, scale=-1.0, bias=halfpi[:]).then_inc(own, 1)
            act.wait_ge(own, ln.made(own))
            fn(mang[:, 3], mang[:, 0], ACT.Sin).then_inc(S["pos_trig"], 1)
            act.wait_ge(S["pos_trig"], ln.made(S["pos_trig"]))
            norm()
            normed_high(("mix", 3))
            for g, (c0, c1_) in enumerate(ODD_COLS):
                for t in range(NT):
                    act.wait_ge(*acc.filled(("odd", g, t)))
                    b = acc.bank(("odd", g, t))
                    fn(oin[:, t, c0:c1_], b[:, 0:c1_ - c0], ACT.Copy).then_inc(*acc.frees(("odd", g, t)))
                    act.wait_ge(*acc.freed(("odd", g, t)))
                    act.sem_inc(S["odd_ready"], 1)
            for q in range(4):
                act.wait_ge(*acc.filled(("qn", q)))
                b = acc.bank(("qn", q))
                fn(qnT[:, 2 * q:2 * q + 2, :].rearrange("p h n -> p (h n)"), b, ACT.Copy).then_inc(*acc.frees(("qn", q)))
                act.wait_ge(*acc.filled(("qr", q)))
                b = acc.bank(("qr", q))
                fn(qr[:, :, q * P:(q + 1) * P], b[:, 0:T].rearrange("p (t n) -> p t n", t=NT), ACT.Copy).then_inc(*acc.frees(("qr", q)))
            for g in range(2):
                for q in range(2 * g, 2 * g + 2):
                    act.wait_ge(*acc.filled(("kn", q)))
                    b = acc.bank(("kn", q))
                    fn(knT[:, 2 * q:2 * q + 2, :].rearrange("p h n -> p (h n)"), b, ACT.Copy).then_inc(*acc.frees(("kn", q)))
                for t in range(NT):
                    act.wait_ge(*acc.filled(("v", t, g)))
                    b = acc.bank(("v", t, g))
                    fn(vt[:, t, g * 512:(g + 1) * 512], b, ACT.Copy).then_inc(*acc.frees(("v", t, g)))
            for t in range(NT):
                act.wait_ge(*wk.filled(("qrT", t)))
                b = wk.bank(("qrT", t))
                fn(qrT[:, :, t * P:(t + 1) * P], b.rearrange("p (b n) -> p b n", b=4), ACT.Copy).then_inc(*wk.frees(("qrT", t)))
                act.wait_ge(*wk.freed(("qrT", t)))
                act.sem_inc(S["qrope_T"], 1)
            for n in range(NT * MH + 1):
                if n < NT * MH:
                    K = P * (n // MH + 1)
                    act.wait_ge(S["m_scores"], ln.next(S["m_scores"]))
                    fn(mp[:, n % 2, 0:K], ms[:, n % 2, 0:K], ACT.Exp, bias=mst[:, n:n + 1], accum_out=mst[:, 16 + n:17 + n]).then_inc(S["m_probs"], 1)
                    act.wait_ge(S["m_probs"], ln.made(S["m_probs"]))
                if n >= 1:
                    m = n - 1
                    K = P * (m // MH + 1)
                    if m >= 2 and (m - 2) % 4 < 3:
                        act.wait_ge(S["m_pv"], 3 * ((m - 2) // 4) + (m - 2) % 4 + 1)
                    elif m >= 2:
                        act.wait_ge(*acc.filled(("mo", (m - 2) // MH, ((m - 2) % MH) // 4)))
                    act.wait_ge(*wk.filled(("mpT", m)))
                    b = wk.bank(("mpT", m))
                    fn(mpT[:, m % 2, 0:K], b[:, 0:K], ACT.Copy).then_inc(*wk.frees(("mpT", m)))
                    act.wait_ge(*wk.freed(("mpT", m)))
                    act.sem_inc(S["m_probsT"], 1)
                if n in (6, 8, 10):
                    split_high(1)
            for t in range(NT):
                for q in range(2):
                    act.wait_ge(*acc.filled(("mo", t, q)))
                    b = acc.bank(("mo", t, q)).rearrange("p (k n) -> p k n", k=4)
                    fn(hTh[:, 4 * q:4 * q + 4, t * P:(t + 1) * P], b, ACT.Copy).then_inc(S["hT_high"], 1)
            split_high(3)
            norm()
            ffn(("ffn", 3), 3)
            norm()

        @block.gpsimd
        def _(pool):
            ln, own = Counts(), S["pool_chain"]
            tt, ts = nc.gpsimd.tensor_tensor, nc.gpsimd.tensor_scalar
            nc.gpsimd.memset(mhalf[:], -0.5).then_inc(own, 1)
            pool.wait_ge(own, ln.made(own))
            nc.gpsimd.memset(halfpi[:], float(np.pi / 2)).then_inc(own, 1)
            pool.wait_ge(own, ln.made(own))
            nc.gpsimd.memset(relb[NBUCKET:NBUCKET + 1, :], NEG).then_inc(S["setup_ready"], 1)
            pool.wait_ge(S["setup_ready"], ln.made(S["setup_ready"]))

            def inverse_root(parts, c0, n, width, sem_):
                ts(rs[0:parts, c0:c0 + n], ss[0:parts, c0:c0 + n], 1.0 / width, EPS, ALU.mult, ALU.add).then_inc(own, 1)
                pool.wait_ge(own, ln.made(own))
                tt(rs[0:parts, c0:c0 + n], rs[0:parts, c0:c0 + n], mhalf[0:parts, 0:n], ALU.pow).then_inc(sem_, 1)
                pool.wait_ge(sem_, ln.made(sem_))

            def norm():
                pool.wait_ge(S["norm_sums"], ln.next(S["norm_sums"], 2))
                inverse_root(P, 0, NT, D, S["norm_scale"])

            def heads(c0, n, width, parts=P):
                pool.wait_ge(S["head_sums"], ln.next(S["head_sums"]))
                inverse_root(parts, c0, n, width, S["head_scale"])

            def s5_tables():
                K = lambda k: prm[:, k, :]
                ar, ai, arg, th, co, si, den, xr, xi, k1, k2 = (K(k) for k in (0, 1, 4, 5, 6, 7, 8, 9, 10, 11, 12))
                pool.wait_ge(S["s5_dt"], ln.next(S["s5_dt"]))
                tt(arg, ar, K(3), ALU.mult).then_inc(own, 1)
                pool.wait_ge(own, ln.made(own))
                tt(th, ai, K(3), ALU.mult).then_inc(own, 1)
                pool.wait_ge(own, ln.made(own))
                ts(k1, th, 1.0 / TWO_PI, MAGIC, ALU.mult, ALU.add).then_inc(own, 1)
                pool.wait_ge(own, ln.made(own))
                ts(k1, k1, -MAGIC, None, ALU.add).then_inc(own, 1)
                pool.wait_ge(own, ln.made(own))
                for c in (CW1, CW2, CW3):
                    ts(k2, k1, -c, None, ALU.mult).then_inc(own, 1)
                    pool.wait_ge(own, ln.made(own))
                    tt(th, th, k2, ALU.add).then_inc(own, 1)
                    pool.wait_ge(own, ln.made(own))
                ts(th, th, PI_SAFE, -PI_SAFE, ALU.min, ALU.max).then_inc(S["s5_arg"], 1)
                pool.wait_ge(S["s5_arg"], ln.made(S["s5_arg"]))
                tt(den, ar, ar, ALU.mult).then_inc(own, 1)
                pool.wait_ge(own, ln.made(own))
                tt(k2, ai, ai, ALU.mult).then_inc(own, 1)
                pool.wait_ge(own, ln.made(own))
                tt(den, den, k2, ALU.add).then_inc(own, 1)
                pool.wait_ge(own, ln.made(own))
                nc.gpsimd.memset(k1, -1.0).then_inc(own, 1)
                pool.wait_ge(own, ln.made(own))
                tt(den, den, k1, ALU.pow).then_inc(own, 1)
                pool.wait_ge(own, ln.made(own))
                for m in bpad:
                    nc.gpsimd.memset(m, 0.0).then_inc(own, 1)
                    pool.wait_ge(own, ln.made(own))
                for g in range(2):
                    ts(cpad[0][:, :, 64 * g:64 * g + 64], craw[0], gmask[:, g:g + 1], None, ALU.mult).then_inc(own, 1)
                    pool.wait_ge(own, ln.made(own))
                    ts(cpad[1][:, :, 64 * g:64 * g + 64], craw[1], gmask[:, g:g + 1], -1.0, ALU.mult, ALU.mult).then_inc(own, 1)
                    pool.wait_ge(own, ln.made(own))
                pool.wait_ge(S["s5_trig"], ln.next(S["s5_trig"]))
                tt(xr, mag, co, ALU.mult).then_inc(own, 1)
                pool.wait_ge(own, ln.made(own))
                ts(xr, xr, -1.0, None, ALU.add).then_inc(own, 1)
                pool.wait_ge(own, ln.made(own))
                tt(xi, mag, si, ALU.mult).then_inc(own, 1)
                pool.wait_ge(own, ln.made(own))
                cr, ci = K(13), K(14)
                tt(cr, xr, ar, ALU.mult).then_inc(own, 1)
                pool.wait_ge(own, ln.made(own))
                tt(k2, xi, ai, ALU.mult).then_inc(own, 1)
                pool.wait_ge(own, ln.made(own))
                tt(cr, cr, k2, ALU.add).then_inc(own, 1)
                pool.wait_ge(own, ln.made(own))
                tt(cr, cr, den, ALU.mult).then_inc(own, 1)
                pool.wait_ge(own, ln.made(own))
                tt(ci, xi, ar, ALU.mult).then_inc(own, 1)
                pool.wait_ge(own, ln.made(own))
                tt(k2, xr, ai, ALU.mult).then_inc(own, 1)
                pool.wait_ge(own, ln.made(own))
                tt(ci, ci, k2, ALU.subtract).then_inc(own, 1)
                pool.wait_ge(own, ln.made(own))
                tt(ci, ci, den, ALU.mult).then_inc(own, 1)
                pool.wait_ge(own, ln.made(own))

                def each(ap, n):
                    return ap.unsqueeze(2).to_broadcast([ap.shape[0], ST, n])

                for r, (f1, f2, op) in enumerate(((cr, ci, ALU.subtract), (ci, cr, ALU.add))):
                    tt(bx[0], braw[0], each(f1, 16), ALU.mult).then_inc(own, 1)
                    pool.wait_ge(own, ln.made(own))
                    tt(bx[1], braw[1], each(f2, 16), ALU.mult).then_inc(own, 1)
                    pool.wait_ge(own, ln.made(own))
                    for g in range(2):
                        p_ = slice(64 * g, 64 * g + 64)
                        to = S["s5_pad"] if r and g else own
                        tt(bpad[r][p_, :, 16 * g:16 * g + 16], bx[0][p_], bx[1][p_], op).then_inc(to, 1)
                        pool.wait_ge(to, ln.made(to))
                nc.gpsimd.memset(cosT[:, :, 0:1], 1.0).then_inc(own, 1)
                pool.wait_ge(own, ln.made(own))
                nc.gpsimd.memset(sinT[:, :, 0:1], 0.0).then_inc(own, 1)
                pool.wait_ge(own, ln.made(own))
                n = 1
                while n < T:
                    A, B = etmp[0][:, :, 0:n], etmp[1][:, :, 0:n]
                    tt(A, cosT[:, :, 0:n], each(co, n), ALU.mult).then_inc(own, 1)
                    pool.wait_ge(own, ln.made(own))
                    tt(B, sinT[:, :, 0:n], each(si, n), ALU.mult).then_inc(own, 1)
                    pool.wait_ge(own, ln.made(own))
                    tt(cosT[:, :, n:2 * n], A, B, ALU.subtract).then_inc(own, 1)
                    pool.wait_ge(own, ln.made(own))
                    tt(A, sinT[:, :, 0:n], each(co, n), ALU.mult).then_inc(own, 1)
                    pool.wait_ge(own, ln.made(own))
                    tt(B, cosT[:, :, 0:n], each(si, n), ALU.mult).then_inc(own, 1)
                    pool.wait_ge(own, ln.made(own))
                    to = S["table_done"] if 2 * n == T else own
                    tt(sinT[:, :, n:2 * n], A, B, ALU.add).then_inc(to, 1)
                    pool.wait_ge(to, ln.made(to))
                    tt(k1, co, co, ALU.mult).then_inc(own, 1)
                    pool.wait_ge(own, ln.made(own))
                    tt(k2, si, si, ALU.mult).then_inc(own, 1)
                    pool.wait_ge(own, ln.made(own))
                    tt(si, co, si, ALU.mult).then_inc(own, 1)
                    pool.wait_ge(own, ln.made(own))
                    ts(si, si, 2.0, None, ALU.mult).then_inc(own, 1)
                    pool.wait_ge(own, ln.made(own))
                    tt(co, k1, k2, ALU.subtract).then_inc(own, 1)
                    pool.wait_ge(own, ln.made(own))
                    n *= 2

            for l in range(DEPTH):
                norm()
                heads(4, 20, HD)
                heads(24, 8, HD)
                heads(36, 12, HD)
                heads(32, 2, HD, NCMP)
                norm()
            s5_tables()
            norm()
            heads(4, 8, 128)
            norm()
            norm()
            heads(4, 2, MQ)
            heads(6, 2, MKV)
            norm()
            norm()

        @block.vector
        def _(dve):
            ln, own = Counts(), S["dve_chain"]
            v = nc.vector
            tt, ts, stt = v.tensor_tensor, v.tensor_scalar, v.scalar_tensor_tensor

            def over(ap, n):
                return ap.unsqueeze(len(ap.shape)).to_broadcast(list(ap.shape) + [n])

            def across(ap, at, n):
                s = list(ap.shape)
                return ap.unsqueeze(at).to_broadcast(s[:at] + [n] + s[at:])

            lows = [0]

            def split_low(n):
                for k in range(lows[0], min(lows[0] + n, len(W.split))):
                    dve.wait_ge(S["w_high"], k + 1)
                    hi, lo = W.pair(k)
                    tt(lo, W.source(k), hi, ALU.subtract).then_inc(S["w_low"], 1)
                    lows[0] = k + 1

            def into_hT(n, gain):
                def low(t, q):
                    c = (slice(None), slice(4 * q, 4 * q + 4), slice(t * P, (t + 1) * P))
                    dve.wait_ge(S["hT_high"], ln.next(S["hT_high"]))
                    tt(hTl[c], stage[:, q, :].rearrange("p (k n) -> p k n", k=4), hTh[c], ALU.subtract).then_inc(S["hT_ready"], 1)

                for t in range(NT):
                    for q in range(2):
                        if t:
                            low(t - 1, q)
                            dve.wait_ge(S["hT_ready"], ln.made(S["hT_ready"]))
                        dve.wait_ge(*wk.filled(("T", n, t, q)))
                        b = wk.bank(("T", n, t, q)).rearrange("p (k n) -> p k n", k=4)
                        tt(stage[:, q, :].rearrange("p (k n) -> p k n", k=4), b, over(vecs[:, 0, gain + 4 * q:gain + 4 * q + 4], P), ALU.mult).then_inc(*wk.frees(("T", n, t, q)))
                for q in range(2):
                    low(NT - 1, q)
                    dve.wait_ge(S["hT_ready"], ln.made(S["hT_ready"]))
                split_low(1)

            def mixed_low(l):
                for t in range(NT):
                    for q in range(2):
                        c = (slice(None), slice(4 * q, 4 * q + 4), slice(t * P, (t + 1) * P))
                        b = wk.bank(("T", ("mixed", l), t, q)).rearrange("p (k n) -> p k n", k=4)
                        dve.wait_ge(S["hT_high"], ln.next(S["hT_high"]))
                        tt(hTl[c], b, hTh[c], ALU.subtract).then_inc(*wk.frees(("T", ("mixed", l), t, q)))

            def add_out(names):
                for t in range(NT):
                    for g in range(2):
                        dve.wait_ge(*acc.filled(names(g, t)))
                        b = acc.bank(names(g, t))
                        xs = x[:, t, g * COLS:(g + 1) * COLS]
                        tt(xs, xs, b, ALU.add).then_inc(*acc.frees(names(g, t)))
                        dve.wait_ge(*acc.freed(names(g, t)))
                    dve.sem_inc(S["x_ready"], 1)

            def add_mix(l):
                for g in range(2):
                    for t in range(NT):
                        dve.wait_ge(*acc.filled(("out", l, g, t)))
                        b = acc.bank(("out", l, g, t))
                        xs = x[:, t, g * COLS:(g + 1) * COLS]
                        tt(xs, xs, b, ALU.add).then_inc(*acc.frees(("out", l, g, t)))
                        dve.wait_ge(*acc.freed(("out", l, g, t)))
                        if g == 1:
                            dve.sem_inc(S["x_ready"], 1)

            def ffn(n, tag, gain):
                into_hT(n, gain)
                w = vecs[:, tag - 1, :] if tag >= 2 else None
                for s in range(NSTEP):
                    chunks = range(FSTEP * s, FSTEP * s + FSTEP)
                    split_low(1)
                    if tag >= 2:
                        for f in chunks:
                            c, b = sg[:, f % 4, :], wk.bank(("gu", tag, f))
                            dve.wait_ge(S["conv_in"], ln.next(S["conv_in"]))
                            stt(c[:, 1:T], b[:, 0:T - 1], w[:, 22 + f:23 + f], c[:, 1:T], ALU.mult, ALU.add).then_inc(own, 1)
                            dve.wait_ge(own, ln.made(own))
                            stt(c[:, 2:T], b[:, 0:T - 2], w[:, f:f + 1], c[:, 2:T], ALU.mult, ALU.add).then_inc(S["conv_done"], 1)
                    for f in chunks:
                        b = wk.bank(("gu", tag, f))
                        dve.wait_ge(S["act_silu"], ln.next(S["act_silu"]))
                        tt(sg[:, f % 4, :], sg[:, f % 4, :], b[:, T:2 * T], ALU.mult).then_inc(*wk.frees(("gu", tag, f)))
                    split_low(1)
                    for f in chunks:
                        dve.wait_ge(S["hid_high"], ln.next(S["hid_high"]))
                        tt(hidl[:, f % 4, :], sg[:, f % 4, :], hidh[:, f % 4, :], ALU.subtract).then_inc(S["hid_ready"], 1)
                    if s:
                        split_low(1)
                add_out(lambda g, t: ("y", tag, 2 * t + g))

            def rotate(src, cos, sin, heads, tmp):
                lo, hi = src[:, :, :, 0:32], src[:, :, :, 32:64]
                c, s = across(cos, 2, heads), across(sin, 2, heads)
                tmp = [tmp[k].rearrange("p (t h d) -> p t h d", t=NT, h=heads) for k in range(4)]
                for k, (p_, q_) in enumerate(((lo, c), (hi, s), (hi, c), (lo, s))):
                    tt(tmp[k], p_, q_, ALU.mult).then_inc(own, 1)
                    dve.wait_ge(own, ln.made(own))
                tt(lo, tmp[0], tmp[1], ALU.subtract).then_inc(own, 1)
                dve.wait_ge(own, ln.made(own))
                tt(hi, tmp[2], tmp[3], ALU.add).then_inc(own, 1)
                dve.wait_ge(own, ln.made(own))

            def combine(l, t):
                dve.wait_ge(S["probs_ready"], NT * NH * l + NH * (t + 1))
                v.reciprocal(lsum[:, t], lsum[:, t]).then_inc(own, 1)
                dve.wait_ge(own, ln.made(own))
                tt(gate[:, t], gate[:, t], lsum[:, t], ALU.mult).then_inc(own, 1)
                dve.wait_ge(own, ln.made(own))
                dst = rows[:, t, RET_W:2 * RET_W].rearrange("p (h d) -> p h d", d=HD)
                for br in range(3):
                    dve.wait_ge(*acc.filled(("no", l, t, br)))
                    b = acc.bank(("no", l, t, br))[:, 0:RET_W].rearrange("p (h d) -> p h d", d=HD)
                    o = dst if br == 0 else osum[:, t, :].rearrange("p (h d) -> p h d", d=HD)
                    tt(o, b, over(gate[:, t, :, br], HD), ALU.mult).then_inc(*acc.frees(("no", l, t, br)))
                    dve.wait_ge(*acc.freed(("no", l, t, br)))
                    if br:
                        to = S["mixed"] if t and br == 2 else own
                        tt(dst, dst, o, ALU.add).then_inc(to, 1)
                        dve.wait_ge(to, ln.made(to))

            for k, n in enumerate((NVEC, 88, 88)):
                dve.wait_ge(*wk.filled(("vec", k)))
                b = wk.bank(("vec", k))
                v.tensor_copy(vecs[:, k, 0:n], b[:, 0:n]).then_inc(*wk.frees(("vec", k)))
                dve.wait_ge(*wk.freed(("vec", k)))
            dve.wait_ge(*wk.filled(("pe",)))
            b = wk.bank(("pe",))
            v.tensor_copy(peT[:].rearrange("p j k -> p (j k)"), b[0:HD, 0:P]).then_inc(*wk.frees(("pe",)))
            dve.wait_ge(*wk.freed(("pe",)))
            dve.wait_ge(S["x_in"], 16)
            dve.sem_inc(S["x_ready"], 2)
            l0, l1 = vecs[:, 0, V_LB:V_LB + 4], vecs[:, 0, V_LB + 4:V_LB + 8]
            tt(lbt[:, 8:12], l0, l1, ALU.max).then_inc(own, 1)
            dve.wait_ge(own, ln.made(own))
            tt(lbt[:, 0:4], l0, lbt[:, 8:12], ALU.subtract).then_inc(own, 1)
            dve.wait_ge(own, ln.made(own))
            tt(lbt[:, 4:8], l1, lbt[:, 8:12], ALU.subtract).then_inc(S["lb_arg"], 1)
            dve.wait_ge(S["lb_arg"], ln.made(S["lb_arg"]))
            dve.wait_ge(S["lb_exp"], ln.next(S["lb_exp"]))
            tt(lbt[:, 12:16], lbt[:, 0:4], lbt[:, 4:8], ALU.add).then_inc(own, 1)
            dve.wait_ge(own, ln.made(own))
            v.reciprocal(lbt[:, 12:16], lbt[:, 12:16]).then_inc(own, 1)
            dve.wait_ge(own, ln.made(own))
            tt(lbt[:, 8:12], lbt[:, 0:4], lbt[:, 12:16], ALU.mult).then_inc(own, 1)
            dve.wait_ge(own, ln.made(own))
            ts(lbt[:, 12:16], lbt[:, 8:12], -1.0, 1.0, ALU.mult, ALU.add).then_inc(own, 1)
            dve.wait_ge(own, ln.made(own))

            split_low(NPAIR - 1)
            for l in range(DEPTH):
                into_hT(("mix", l), V_ATTN + KC * l)
                split_low(5)
                dve.wait_ge(S["proj_ready"], ln.next(S["proj_ready"], 4))
                rotate(proj[:, :, 0:2 * RET_W].rearrange("p t (h d) -> p t h d", d=HD), rope[:, :, 0, :], rope[:, :, 1, :], 2 * NH, rtmp)
                dve.sem_inc(S["rotated"], 1)
                split_low(6)
                dve.wait_ge(S["proj_ready"], ln.next(S["proj_ready"], 8))
                q3 = proj[:, :, O_NQ:O_KV]
                k4 = proj[:, :, O_KV + 256:O_KV + 768].rearrange("p t (b n) -> p t b n", b=2)[:, :, :, 0:P]
                sq = nsq.rearrange("p (t n) -> p t n", t=NT)
                tt(sq, q3, q3, ALU.mult).then_inc(own, 1)
                dve.wait_ge(own, ln.made(own))
                ssv = ss[:, 4:24].rearrange("p (t n) -> p t n", t=NT)
                v.tensor_reduce(ss[:, 4:16].rearrange("p (t h) -> p t h", t=NT), sq.rearrange("p t (h d) -> p t h d", d=HD), AX_X, ALU.add).then_inc(own, 1)
                dve.wait_ge(own, ln.made(own))
                sk4 = sk.rearrange("p (t b n) -> p t b n", t=NT, b=2)
                for t in range(NT):
                    tt(sk4[:, t], k4[:, t], k4[:, t], ALU.mult).then_inc(own, 1)
                    dve.wait_ge(own, ln.made(own))
                v.tensor_reduce(ss[:, 16:24], sk.rearrange("p (q d) -> p q d", d=HD), AX_X, ALU.add).then_inc(S["head_sums"], 1)
                dve.wait_ge(S["head_sums"], ln.made(S["head_sums"]))
                dve.wait_ge(S["head_scale"], ln.next(S["head_scale"]))
                for t in range(NT):
                    qv = qn[:, t, :].rearrange("p (q g d) -> p g q d", q=HPG, g=2)
                    src = proj[:, t, O_NQ:O_KV].rearrange("p (g q d) -> p g q d", q=HPG, g=2)
                    tt(qv, src, over(rs[:, 4 + t * NH:4 + (t + 1) * NH].rearrange("p (g q) -> p g q", g=2), HD), ALU.mult).then_inc(own, 1)
                    dve.wait_ge(own, ln.made(own))
                    stt(qn[:, t, :].rearrange("p (h d) -> p h d", d=HD), qn[:, t, :].rearrange("p (h d) -> p h d", d=HD), HD ** -0.5,
                                across(gains[:, l, 0, :], 1, NH), ALU.mult, ALU.mult).then_inc(own, 1)
                    dve.wait_ge(own, ln.made(own))
                    kv_ = kn[:, t, :].rearrange("p (b g d) -> p b g d", b=2, g=2)
                    tt(kv_, k4[:, t].rearrange("p b (g d) -> p b g d", g=2),
                               over(rs[:, 16 + 4 * t:20 + 4 * t].rearrange("p (b g) -> p b g", b=2), HD), ALU.mult).then_inc(own, 1)
                    dve.wait_ge(own, ln.made(own))
                    to = S["nsa_rows"] if t else own
                    tt(kv_, kv_, across(gains[:, l, 2:4, :], 2, 2), ALU.mult).then_inc(to, 1)
                    dve.wait_ge(to, ln.made(to))
                for h in range(NH):
                    dve.wait_ge(*wk.filled(("rs", l, h)))
                    b = wk.bank(("rs", l, h))
                    if h >= 2:
                        dve.wait_ge(S["ret_mixed"], (NH - 1) * l + h - 1)
                    tt(sT[:, h % 2, 0:T], b[:, 0:T], decay[:, h, :], ALU.mult).then_inc(own, 1)
                    dve.wait_ge(own, ln.made(own))
                    tt(sT[:, h % 2, T:T + P], b[:, T:T + P], decay[:, h, 0:P], ALU.mult).then_inc(*wk.frees(("rs", l, h)))
                    dve.wait_ge(*wk.freed(("rs", l, h)))
                    dve.sem_inc(S["decayed"], 1)
                dve.wait_ge(S["proj_ready"], ln.next(S["proj_ready"], 2))
                dve.wait_ge(S["gelu_ready"], ln.next(S["gelu_ready"]))
                zv = proj[:, :, O_GM + GM_W:IN_W]
                tt(vn, zv, zv, ALU.mult).then_inc(own, 1)
                dve.wait_ge(own, ln.made(own))
                v.tensor_reduce(ss[:, 24:32].rearrange("p (t h) -> p t h", t=NT), vn.rearrange("p t (h d) -> p t h d", d=HD), AX_X, ALU.add).then_inc(S["head_sums"], 1)
                dve.wait_ge(S["head_sums"], ln.made(S["head_sums"]))
                dve.wait_ge(S["blocks_read"], ln.next(S["blocks_read"], 2))
                for j in range(2):
                    for g in range(2):
                        src = aT[:, j, g, :]
                        win = bass.AP(src.tensor, src.offset, [list(src.ap[0]), [1, CMP_LEN], [CMP_STRIDE, NCMP]])
                        to = S["blocks_ready"] if j and g else own
                        tt(blk[:, j, :, g * NCMP:(g + 1) * NCMP], win, over(peT[:, 2 * l + j, :], NCMP), ALU.add).then_inc(to, 1)
                        dve.wait_ge(to, ln.made(to))
                dve.wait_ge(S["head_scale"], ln.next(S["head_scale"]))
                for t in range(NT):
                    tt(vn[:, t, :].rearrange("p (h d) -> p h d", d=HD), zv[:, t, :].rearrange("p (h d) -> p h d", d=HD),
                               over(rs[:, 24 + 4 * t:28 + 4 * t], HD), ALU.mult).then_inc(own, 1)
                    dve.wait_ge(own, ln.made(own))
                dve.wait_ge(*wk.filled(("wsT", l)))
                b = wk.bank(("wsT", l)).rearrange("p (g n) -> p g n", g=4)
                tt(wsT, b, across(triu[:], 1, 4), ALU.mult).then_inc(*wk.frees(("wsT", l)))
                dve.wait_ge(*wk.freed(("wsT", l)))
                dve.sem_inc(S["gm_rows"], 1)
                for t in range(NT):
                    dve.wait_ge(*acc.filled(("ro", l, t)))
                    b = acc.bank(("ro", l, t))
                    v.tensor_copy(rows[:, t, 0:RET_W], b[:, 0:RET_W]).then_inc(*acc.frees(("ro", l, t)))
                    dve.wait_ge(*acc.freed(("ro", l, t)))
                ro = rows[:, :, 0:RET_W]
                tt(rsq, ro, ro, ALU.mult).then_inc(own, 1)
                dve.wait_ge(own, ln.made(own))
                v.tensor_reduce(ss[:, 36:48].rearrange("p (t h) -> p t h", t=NT), rsq.rearrange("p t (h d) -> p t h d", d=HD), AX_X, ALU.add).then_inc(S["head_sums"], 1)
                dve.wait_ge(S["head_sums"], ln.made(S["head_sums"]))
                dve.wait_ge(*wk.filled(("kc", l)))
                b = wk.bank(("kc", l))
                v.tensor_copy(kc[0:NCMP, :], b[0:NCMP, 0:256]).then_inc(*wk.frees(("kc", l)))
                dve.wait_ge(*wk.freed(("kc", l)))
                tt(kcn[0:NCMP, :], kc[0:NCMP, 0:P], kc[0:NCMP, 0:P], ALU.mult).then_inc(own, 1)
                dve.wait_ge(own, ln.made(own))
                v.tensor_reduce(ss[0:NCMP, 32:34], kcn[0:NCMP, :].rearrange("p (g d) -> p g d", g=2), AX_X, ALU.add).then_inc(S["head_sums"], 1)
                dve.wait_ge(S["head_sums"], ln.made(S["head_sums"]))
                dve.wait_ge(S["head_scale"], ln.next(S["head_scale"], 2))
                kc3 = kcn[0:NCMP, :].rearrange("p (g d) -> p g d", g=2)
                tt(kc3, kc[0:NCMP, 0:P].rearrange("p (g d) -> p g d", g=2), over(rs[0:NCMP, 32:34], HD), ALU.mult).then_inc(own, 1)
                dve.wait_ge(own, ln.made(own))
                tt(kc3, kc3, across(gains[0:NCMP, l, 1, :], 1, 2), ALU.mult).then_inc(S["kc_rows"], 1)
                dve.wait_ge(S["kc_rows"], ln.made(S["kc_rows"]))
                dve.wait_ge(*wk.filled(("kcT", l)))
                b = wk.bank(("kcT", l))
                v.tensor_copy(kTc[:, 0:NCMP], b[:, 0:NCMP]).then_inc(*wk.frees(("kcT", l)))
                dve.wait_ge(*wk.freed(("kcT", l)))
                dve.sem_inc(S["kTc_ready"], 1)
                if l == 0:
                    dve.wait_ge(S["bias_in"], 16 * NH)
                for g in range(2):
                    dve.wait_ge(*wk.filled(("sc", l, g)))
                    b = wk.bank(("sc", l, g))[:, 0:NT * HPG * 16].rearrange("p (q n) -> p q n", n=16)
                    for t in range(NT):
                        at = (1 - t) * P + CMP_LEN - 1
                        i = tt(s_c[:, t * NH + g * HPG:t * NH + (g + 1) * HPG], b[:, t * HPG:(t + 1) * HPG, 0:NCMP],
                               bias[:, g * HPG:(g + 1) * HPG, at:at + 14 * CMP_STRIDE + 1:CMP_STRIDE], ALU.add)
                        if t == 0:
                            i.then_inc(own, 1)
                            dve.wait_ge(own, ln.made(own))
                        else:
                            i.then_inc(*wk.frees(("sc", l, g)))
                            dve.wait_ge(*wk.freed(("sc", l, g)))
                v.tensor_reduce(nmax[:, 8:20], s_c, AX_X, ALU.max).then_inc(own, 1)
                dve.wait_ge(own, ln.made(own))
                tt(s_c, s_c, over(nmax[:, 8:20], NCMP), ALU.subtract).then_inc(S["cmp_scores"], 1)
                dve.wait_ge(S["cmp_scores"], ln.made(S["cmp_scores"]))
                dve.wait_ge(S["cmp_exp"], ln.next(S["cmp_exp"]))
                v.tensor_reduce(lsum[:, :, :, 0], s_c, AX_X, ALU.add).then_inc(own, 1)
                dve.wait_ge(own, ln.made(own))
                sc4 = s_c.rearrange("p (t h) n -> p t h n", t=NT)
                tt(sc4, sc4, across(cmask[:], 2, NH), ALU.mult).then_inc(S["cmp_probs"], 1)
                dve.wait_ge(S["cmp_probs"], ln.made(S["cmp_probs"]))
                for n in range(NT * NH):
                    t, h = n // NH, n % NH
                    K = P * (t + 1)
                    dve.wait_ge(*wk.filled(("s", l, n)))
                    b = wk.bank(("s", l, n)).rearrange("p (b n) -> p b n", b=2)[:, :, 0:K]
                    if n >= 2:
                        dve.wait_ge(S["probs_ready"], NT * NH * l + n - 1)
                    s = s_sb[:, n % 2, :].rearrange("p (b n) -> p b n", b=2)[:, :, 0:K]
                    tt(s, b, across(bias[:, h, (1 - t) * P:(1 - t) * P + K], 1, 2), ALU.add).then_inc(*wk.frees(("s", l, n)))
                    dve.wait_ge(*wk.freed(("s", l, n)))
                    v.tensor_reduce(nmax[:, 2 * (n % 2):2 * (n % 2) + 2], s, AX_X, ALU.max, negate=True).then_inc(S["scores_ready"], 1)
                    dve.wait_ge(S["scores_ready"], ln.made(S["scores_ready"]))
                    if n == 1:
                        dve.wait_ge(*acc.filled(("gm", l)))
                        g_ = acc.bank(("gm", l)).rearrange("p (g t n) -> p g t n", g=4, t=NT)
                        for g in range(4):
                            dst = rows[:, :, 2 * RET_W + g * HD:2 * RET_W + (g + 1) * HD]
                            i = stt(dst, g_[:, g], vecs[:, 0, V_GMB + 4 * l + g:V_GMB + 4 * l + g + 1], proj[:, :, O_GM + g * HD:O_GM + (g + 1) * HD], ALU.add, ALU.mult)
                            if g < 3:
                                i.then_inc(own, 1)
                                dve.wait_ge(own, ln.made(own))
                            else:
                                i.then_inc(*acc.frees(("gm", l)))
                                dve.wait_ge(*acc.freed(("gm", l)))
                    if n == 2:
                        dve.wait_ge(S["silu_ready"], ln.next(S["silu_ready"]))
                        for t_ in range(NT):
                            r3 = ro[:, t_, :].rearrange("p (h d) -> p h d", d=HD)
                            tt(r3, r3, over(rs[:, 36 + NH * t_:36 + NH * (t_ + 1)], HD), ALU.mult).then_inc(own, 1)
                            dve.wait_ge(own, ln.made(own))
                        tt(ro, ro, proj[:, :, O_RG:O_NQ], ALU.mult).then_inc(own, 1)
                        dve.wait_ge(own, ln.made(own))
                    if n == 3:
                        dve.wait_ge(S["gates_ready"], ln.next(S["gates_ready"]))
                        ts(gate, gate, 0.5, 0.5, ALU.mult, ALU.add).then_inc(own, 1)
                        dve.wait_ge(own, ln.made(own))
                    if n == NH + 2:
                        combine(l, 0)
                    if n in (6, 8):
                        split_low(1)
                combine(l, 1)
                mixed_low(l)
                split_low(3)
                add_mix(l)
                ffn(("ffn", l), l, V_FFN + KC * l)
            for r in range(2):
                for key_, dst in (("bbT", bbT), ("cT", cT)):
                    dve.wait_ge(*wk.filled((key_, r)))
                    b = wk.bank((key_, r))
                    v.tensor_copy(dst[:, r].rearrange("p i n -> p (i n)"), b).then_inc(*wk.frees((key_, r)))
                    dve.wait_ge(*wk.freed((key_, r)))

            into_hT(("mix", 2), V_MIX2)
            split_low(3)
            v.memset(ones, 1.0).then_inc(own, 1)
            dve.wait_ge(own, ln.made(own))
            ts(small2[:, 8:12], vecs[:, 0, V_GLU:V_GLU + 4], 0.5, None, ALU.mult).then_inc(own, 1)
            dve.wait_ge(own, ln.made(own))
            dve.wait_ge(S["hg_tanh"], ln.next(S["hg_tanh"], 2))
            ts(lf, lf, 0.5, 0.5, ALU.mult, ALU.add).then_inc(own, 1)
            dve.wait_ge(own, ln.made(own))
            for h in range(HG):
                ts(lf[:, h, :], lf[:, h, :], lbt[:, 12 + h:13 + h], lbt[:, 8 + h:9 + h], ALU.mult, ALU.add).then_inc(own, 1)
                dve.wait_ge(own, ln.made(own))
            ts(key, lf, -1.0, 1.0, ALU.mult, ALU.add).then_inc(S["hg_forget"], 1)
            dve.wait_ge(S["hg_forget"], ln.made(S["hg_forget"]))
            split_low(4)
            dve.wait_ge(S["hg_ln"], ln.next(S["hg_ln"]))
            for h in range(HG):
                for n in range(NCH):
                    c = slice(n * HC, (n + 1) * HC)
                    to = S["hg_cum"] if (h, n) == (HG - 1, NCH - 1) else own
                    v.tensor_tensor_scan(bcum[:, h, c], ones, lf[:, h, c], 0.0, ALU.mult, ALU.add).then_inc(to, 1)
                    dve.wait_ge(to, ln.made(to))
            chunks = lambda m: m.rearrange("p h n -> p (h n)").rearrange("p (q c) -> p q c", c=HC)
            tt(chunks(lf), over(chunks(bcum)[:, :, HC - 1], HC), chunks(bcum), ALU.subtract).then_inc(S["hg_cum"], 1)
            dve.wait_ge(S["hg_cum"], ln.made(S["hg_cum"]))
            split_low(2)
            dve.wait_ge(S["proj_ready"], ln.next(S["proj_ready"], 8))
            dve.wait_ge(S["hg_exp"], ln.next(S["hg_exp"]))
            dec = small2[:, 16:32]
            v.tensor_copy(dec, chunks(eb)[:, :, HC - 1]).then_inc(own, 1)
            dve.wait_ge(own, ln.made(own))
            tt(eb, eb, qTe, ALU.mult).then_inc(own, 1)
            dve.wait_ge(own, ln.made(own))
            tt(bcum, bcum, key, ALU.mult).then_inc(S["hg_q"], 1)
            dve.wait_ge(S["hg_q"], ln.made(S["hg_q"]))
            dve.wait_ge(S["hg_exp"], ln.next(S["hg_exp"]))
            tt(key, key, lf, ALU.mult).then_inc(S["hg_kk"], 1)
            dve.wait_ge(S["hg_kk"], ln.made(S["hg_kk"]))
            dve.wait_ge(*wk.filled(("att",)))
            b = wk.bank(("att",)).rearrange("p (q n) -> p q n", n=HC)
            tt(att, b, across(tri64[:], 1, NT * HG), ALU.mult).then_inc(*wk.frees(("att",)))
            dve.wait_ge(*wk.freed(("att",)))
            dve.sem_inc(S["hg_att"], 1)
            for n in range(NCH - 1):
                dve.wait_ge(*wk.filled(("ds", n)))
                b = wk.bank(("ds", n)).rearrange("p (h n) -> p h n", h=HG)
                if n == 0:
                    v.tensor_copy(state[:, 0], b).then_inc(*wk.frees(("ds", n)))
                    dve.wait_ge(*wk.freed(("ds", n)))
                else:
                    for h in range(HG):
                        i = stt(state[:, n, h, :], state[:, n - 1, h, :], dec[:, h * NCH + n:h * NCH + n + 1], b[:, h, :], ALU.mult, ALU.add)
                        if h < HG - 1:
                            i.then_inc(own, 1)
                            dve.wait_ge(own, ln.made(own))
                        else:
                            i.then_inc(*wk.frees(("ds", n)))
                            dve.wait_ge(*wk.freed(("ds", n)))
                dve.sem_inc(S["hg_state"], 1)
            for t in range(NT):
                dve.wait_ge(*acc.filled(("eo", t)))
                b = acc.bank(("eo", t))
                v.tensor_copy(rows[:, t, 0:512], b).then_inc(*acc.frees(("eo", t)))
                dve.wait_ge(*acc.freed(("eo", t)))
            dve.sem_inc(S["hg_out"], 1)
            er = rows[:, :, 0:512]
            k2 = kk.rearrange("p t h n -> p t (h n)")
            tt(k2, er, er, ALU.mult).then_inc(own, 1)
            dve.wait_ge(own, ln.made(own))
            v.tensor_reduce(ss[:, 4:12], kk.rearrange("p t h n -> p (t h) n"), AX_X, ALU.add).then_inc(S["head_sums"], 1)
            dve.wait_ge(S["head_sums"], ln.made(S["head_sums"]))
            dve.wait_ge(S["head_scale"], ln.next(S["head_scale"]))
            for t in range(NT):
                r3 = rows[:, t, 0:512].rearrange("p (h d) -> p h d", h=HG)
                tt(r3, r3, over(rs[:, 4 + HG * t:4 + HG * (t + 1)], P), ALU.mult).then_inc(own, 1)
                dve.wait_ge(own, ln.made(own))
            dve.wait_ge(S["silu_ready"], ln.next(S["silu_ready"]))
            tt(er, er, eg[:, :, 512:1024], ALU.mult).then_inc(S["mixed"], 1)
            dve.wait_ge(S["mixed"], ln.made(S["mixed"]))

            dve.wait_ge(S["table_done"], ln.next(S["table_done"]))
            for q in range(4):
                co, si = cosT[:, 4 * q:4 * q + 4, :], sinT[:, 4 * q:4 * q + 4, :]
                dve.wait_ge(S["drive_ready"], ln.next(S["drive_ready"]))
                tt(m2, co, bu[0], ALU.mult).then_inc(own, 1)
                dve.wait_ge(own, ln.made(own))
                tt(m4, si, bu[1], ALU.mult).then_inc(own, 1)
                dve.wait_ge(own, ln.made(own))
                tt(wre, m2, m4, ALU.add).then_inc(own, 1)
                dve.wait_ge(own, ln.made(own))
                tt(m2, co, bu[1], ALU.mult).then_inc(own, 1)
                dve.wait_ge(own, ln.made(own))
                tt(m4, si, bu[0], ALU.mult).then_inc(own, 1)
                dve.wait_ge(own, ln.made(own))
                tt(wim, m2, m4, ALU.subtract).then_inc(S["states_used"], 1)
                dve.wait_ge(S["states_used"], ln.made(S["states_used"]))
                for j in range(4):
                    f = mag[:, 4 * q + j:4 * q + j + 1].to_broadcast([P, T])
                    v.tensor_tensor_scan(m2[:, j, :], f, wre[:, j, :], 0.0, ALU.mult, ALU.add).then_inc(own, 1)
                    dve.wait_ge(own, ln.made(own))
                    v.tensor_tensor_scan(m4[:, j, :], f, wim[:, j, :], 0.0, ALU.mult, ALU.add).then_inc(own, 1)
                    dve.wait_ge(own, ln.made(own))
                tt(wre, co, m2, ALU.mult).then_inc(own, 1)
                dve.wait_ge(own, ln.made(own))
                tt(wim, si, m4, ALU.mult).then_inc(own, 1)
                dve.wait_ge(own, ln.made(own))
                tt(m1, wre, wim, ALU.subtract).then_inc(own, 1)
                dve.wait_ge(own, ln.made(own))
                tt(wre, si, m2, ALU.mult).then_inc(own, 1)
                dve.wait_ge(own, ln.made(own))
                tt(wim, co, m4, ALU.mult).then_inc(own, 1)
                dve.wait_ge(own, ln.made(own))
                tt(m3, wre, wim, ALU.add).then_inc(S["states_ready"], 1)
                dve.wait_ge(S["states_ready"], ln.made(S["states_ready"]))
                dve.wait_ge(*acc.filled(("sy", q)))
                b = acc.bank(("sy", q))
                stt(uT[:, q, :], uT[:, q, :], vecs[:, 0, V_SD + q:V_SD + q + 1], b[:, 0:T], ALU.mult, ALU.add).then_inc(*acc.frees(("sy", q)))
                dve.wait_ge(*acc.freed(("sy", q)))
                dve.sem_inc(S["s5_y"], 1)
            for t in range(NT):
                dve.wait_ge(*wk.filled(("eT", t)))
                b = wk.bank(("eT", t)).rearrange("p (k n) -> p k n", k=4)
                tt(stage[:, t, :].rearrange("p (k n) -> p k n", k=4), b, over(vecs[:, 0, V_HG:V_HG + 4], P), ALU.mult).then_inc(*wk.frees(("eT", t)))
            for t in range(NT):
                c = (slice(None), slice(0, 4), slice(t * P, (t + 1) * P))
                dve.wait_ge(S["hT_high"], ln.next(S["hT_high"]))
                tt(hTl[c], stage[:, t, :].rearrange("p (k n) -> p k n", k=4), hTh[c], ALU.subtract).then_inc(S["hT_ready"], 1)
                dve.wait_ge(S["hT_ready"], ln.made(S["hT_ready"]))
            for q in range(2):
                dve.wait_ge(S["glu_tanh"], ln.next(S["glu_tanh"]))
                h = slice(2 * q, 2 * q + 2)
                ts(qTe[:, h], qTe[:, h], 0.5, 0.5, ALU.mult, ALU.add).then_inc(own, 1)
                dve.wait_ge(own, ln.made(own))
                tt(zT[:, h], zT[:, h], qTe[:, h], ALU.mult).then_inc(S["z_gated"], 1)
            for q in range(2):
                h, c = slice(2 * q, 2 * q + 2), slice(4 + 2 * q, 6 + 2 * q)
                dve.wait_ge(S["hT_high"], ln.next(S["hT_high"]))
                tt(hTl[:, c, :], zT[:, h], hTh[:, c, :], ALU.subtract).then_inc(S["hT_ready"], 1)
                dve.wait_ge(S["hT_ready"], ln.made(S["hT_ready"]))
            split_low(4)
            add_mix(2)
            v.tensor_copy(mst[:, 48:50], posi[:]).then_inc(own, 1)
            dve.wait_ge(own, ln.made(own))
            for t in range(NT):
                ts(mang[:, 0, t, :], freq[:], mst[:, 48 + t:49 + t], None, ALU.mult).then_inc(own, 1)
                dve.wait_ge(own, ln.made(own))
            ts(mang[:, 1], mang[:, 0], 1.0 / TWO_PI, MAGIC, ALU.mult, ALU.add).then_inc(own, 1)
            dve.wait_ge(own, ln.made(own))
            ts(mang[:, 1], mang[:, 1], -MAGIC, None, ALU.add).then_inc(own, 1)
            dve.wait_ge(own, ln.made(own))
            for c in (CW1, CW2, CW3):
                stt(mang[:, 0], mang[:, 1], -c, mang[:, 0], ALU.mult, ALU.add).then_inc(own, 1)
                dve.wait_ge(own, ln.made(own))
            ts(mang[:, 0], mang[:, 0], PI_SAFE, -PI_SAFE, ALU.min, ALU.max).then_inc(S["pos_arg"], 1)
            dve.wait_ge(S["pos_arg"], ln.made(S["pos_arg"]))
            ffn(("ffn", 2), 2, V_FFN2)

            into_hT(("mix", 3), V_MIX2 + KC)
            dve.wait_ge(S["odd_ready"], ln.next(S["odd_ready"], 4))
            lat = oin[:, :, 0:MQ + MKV]
            tt(osq, lat, lat, ALU.mult).then_inc(own, 1)
            dve.wait_ge(own, ln.made(own))
            v.tensor_reduce(ss[:, 4:6], osq[:, :, 0:MQ], AX_X, ALU.add).then_inc(S["head_sums"], 1)
            dve.wait_ge(S["head_sums"], ln.made(S["head_sums"]))
            v.tensor_reduce(ss[:, 6:8], osq[:, :, MQ:MQ + MKV], AX_X, ALU.add).then_inc(S["head_sums"], 1)
            dve.wait_ge(S["head_sums"], ln.made(S["head_sums"]))
            dve.wait_ge(S["pos_trig"], ln.next(S["pos_trig"]))
            cos, sin = mang[:, 2], mang[:, 3]
            rotate(oin[:, :, MQ + MKV:].rearrange("p t (h d) -> p t h d", h=1), cos, sin, 1, [mtmp[:, k, 0:NT * 32] for k in range(4)])
            for k in range(2):
                v.tensor_copy(kr[:, :, k * MR:(k + 1) * MR], oin[:, :, MQ + MKV:]).then_inc(own, 1)
                dve.wait_ge(own, ln.made(own))
            dve.wait_ge(S["head_scale"], ln.next(S["head_scale"], 2))
            for t in range(NT):
                ts(oin[:, t, 0:MQ], oin[:, t, 0:MQ], rs[:, 4 + t:5 + t], None, ALU.mult).then_inc(own, 1)
                dve.wait_ge(own, ln.made(own))
                to = S["odd_rows"] if t else own
                ts(oin[:, t, MQ:MQ + MKV], oin[:, t, MQ:MQ + MKV], rs[:, 6 + t:7 + t], None, ALU.mult).then_inc(to, 1)
                dve.wait_ge(to, ln.made(to))
            for t in range(NT):
                c = slice(t * P, (t + 1) * P)
                dve.wait_ge(*wk.filled(("oT", t, 0)))
                b = wk.bank(("oT", t, 0))[:, 0:MQ].rearrange("p (c n) -> p c n", c=3)
                tt(cqT[:, :, c], b, over(vecs[:, 0, V_MQ:V_MQ + 3], P), ALU.mult).then_inc(*wk.frees(("oT", t, 0)))
                dve.wait_ge(*wk.freed(("oT", t, 0)))
                dve.sem_inc(S["odd_T"], 1)
                dve.wait_ge(*wk.filled(("oT", t, 1)))
                b = wk.bank(("oT", t, 1))
                tt(ckvT[:, :, c], b[:, 0:MKV].rearrange("p (c n) -> p c n", c=2), over(vecs[:, 0, V_MKV:V_MKV + 2], P), ALU.mult).then_inc(own, 1)
                dve.wait_ge(own, ln.made(own))
                v.tensor_copy(krT[:, c], b[:, MKV:MKV + P]).then_inc(*wk.frees(("oT", t, 1)))
                dve.wait_ge(*wk.freed(("oT", t, 1)))
                dve.sem_inc(S["odd_T"], 1)
            for q in range(4):
                dve.wait_ge(*acc.freed(("qr", q)))
            rotate(qr.rearrange("p t (h d) -> p t h d", h=MH), cos, sin, MH, [mtmp[:, k, :] for k in range(4)])
            dve.sem_inc(S["qrope_rows"], 1)
            for n in range(NT * MH + 1):
                if n < NT * MH:
                    K = P * (n // MH + 1)
                    dve.wait_ge(*wk.filled(("ms", n)))
                    b = wk.bank(("ms", n))[:, 0:K]
                    if n >= 2:
                        dve.wait_ge(S["m_probs"], n - 1)
                    s_ = ms[:, n % 2, 0:K]
                    stt(s_, b, MQK ** -0.5, causal[:, T - K:T], ALU.mult, ALU.add).then_inc(*wk.frees(("ms", n)))
                    dve.wait_ge(*wk.freed(("ms", n)))
                    v.tensor_reduce(mst[:, n:n + 1], s_, AX_X, ALU.max, negate=True).then_inc(S["m_scores"], 1)
                    dve.wait_ge(S["m_scores"], ln.made(S["m_scores"]))
                if n >= 1:
                    m = n - 1
                    K = P * (m // MH + 1)
                    dve.wait_ge(S["m_probs"], ln.next(S["m_probs"]))
                    v.reciprocal(mst[:, 32:33], mst[:, 16 + m:17 + m]).then_inc(own, 1)
                    dve.wait_ge(own, ln.made(own))
                    ts(mp[:, m % 2, 0:K], mp[:, m % 2, 0:K], mst[:, 32:33], None, ALU.mult).then_inc(S["m_norm"], 1)
                    dve.wait_ge(S["m_norm"], ln.made(S["m_norm"]))
                if n in (6, 8, 10):
                    split_low(1)
            for t in range(NT):
                for q in range(2):
                    c = (slice(None), slice(4 * q, 4 * q + 4), slice(t * P, (t + 1) * P))
                    b = acc.bank(("mo", t, q)).rearrange("p (k n) -> p k n", k=4)
                    dve.wait_ge(S["hT_high"], ln.next(S["hT_high"]))
                    tt(hTl[c], b, hTh[c], ALU.subtract).then_inc(*acc.frees(("mo", t, q)))
            split_low(3)
            add_mix(3)
            ffn(("ffn", 3), 3, V_FFN2 + KC)
            dve.wait_ge(S["normed"], ln.next(S["normed"], 9))
            dve.wait_ge(S["mla_in"], 16)
            for t in range(NT):
                tt(rows[:, t, :], rows[:, t, :], fg, ALU.mult).then_inc(S["out_rows"], 1)
                dve.wait_ge(S["out_rows"], ln.made(S["out_rows"]))

        @block.sync
        def _(sp):
            xv = a["x"].rearrange("b (t p) d -> p (b t) d", p=P)
            sp.dma_start(x[:], xv).then_inc(S["x_in"], 16)
            for k, (name, slot, _, _) in enumerate(W.pieces):
                if k >= NRAW:
                    sp.wait_ge(*W.pieces[k - NRAW][3])
                n, loads = man[name]
                for dst, src in loads:
                    sp.dma_start(dst(wraw[:, slot, 0:n]), src).then_inc(W.landed[slot], 16)
            ov = out.rearrange("b (t p) d -> p (b t) d", p=P)
            for t in range(NT):
                sp.wait_ge(S["out_rows"], t + 1)
                sp.dma_start(ov[:, t, :], rows[:, t, :]).then_inc(S["stored"], 16)
            sp.wait_ge(S["stored"], 16 * NT)


_INS = """x attn_norm w_in w_out nsa_q_gain nsa_k_gain cmp_pe cmp_w1 cmp_w2 gm_ws gm_b ffn_norm w_gate_up w_down rel_bias
    positions_2 norm_mix_g_2 norm_ffn_g_2 final_norm_g_2 even_w_in_2 hgrn_lb_logits_2 hgrn_norm_g_2 s5_a_re_2 s5_a_im_2
    s5_log_dt_2 s5_b_re_2 s5_b_im_2 s5_c_re_2 s5_c_im_2 s5_d_2 s5_w_glu_2 s5_b_glu_2 even_w_out_2 odd_w_in_2 mla_q_norm_g_2
    mla_w_uq_2 mla_kv_norm_g_2 mla_w_ukv_2 odd_w_out_2 ffn_w_in_2 ffn_conv_w_2 ffn_conv_b_2 ffn_w_out_2""".split()


def kernel(**inputs):
    import concourse.bacc as bacc
    from concourse.bass_utils import run_bass_kernel_spmd

    nc = bacc.Bacc("TRN2", target_bir_lowering=False, num_devices=1)
    arrays, aps = {}, {}
    for name in _INS:
        v = np.ascontiguousarray(inputs[name])
        arrays["in_" + name] = v
        aps[name] = nc.dram_tensor("in_" + name, v.shape, mybir.dt.from_np(v.dtype), kind="ExternalInput").ap()
    for name, v in shape_constants().items():
        v = np.ascontiguousarray(v)
        arrays[name] = v
        aps[name] = nc.dram_tensor(name, v.shape, F32, kind="ExternalInput").ap()
    out = nc.dram_tensor("out", (1, T, D), F32, kind="ExternalOutput").ap()
    build(nc, aps, out)
    r = run_bass_kernel_spmd(nc, [arrays], core_ids=[0])
    return r.results[0]["out"]
```

```python
from contextlib import ExitStack

import numpy as np

import concourse.bass as bass
from concourse import mybir

F32 = mybir.dt.float32
F32R = mybir.dt.float32r
I32 = mybir.dt.int32
ALU = mybir.AluOpType
ACT = mybir.ActivationFunctionType
AX_X = mybir.AxisListType.X

P = 128
T = 256
NT = T // P
D = 1024
KC = D // P
DEPTH = 2
HD = 64
NH = 6
HPG = 3
RET_W = NH * HD
IN_W = 3218
O_RQ, O_RK, O_RV, O_RG = 0, RET_W, 2 * RET_W, 3 * RET_W
O_NQ = 4 * RET_W
O_KV = O_NQ + RET_W
O_NG = O_KV + 768
O_GM = O_NG + 18
GM_W = 256
NCMP = 15
CMP_LEN, CMP_STRIDE = 32, 16
FF = 2816
FC = FF // P
FSTEP = 2
NSTEP = FC // FSTEP
LAG = 3
COLS = 512
EPS = 1e-6
NEG = -1e30
NBUCKET = 32
LINE = 512
HG = 4
HC = 64
NCH = T // HC
SD = 512
ST = 16
MH = 8
MQ, MKV, MR, MN, MV = 384, 256, 64, 128, 128
MQK = MN + MR
TWO_PI = 2.0 * np.pi
MAGIC = 12582912.0
CW1 = 6.28125
CW2 = float(np.float32(0.0019350051879882812))
CW3 = float(TWO_PI - CW1 - CW2)
PI_SAFE = 3.1415925


def shape_constants():
    f = np.float32
    p = np.arange(P)
    ident = np.eye(P, dtype=f)
    triu = (p[:, None] <= p[None, :]).astype(f)
    tri64 = np.concatenate([triu[:HC, :HC], triu[:HC, :HC]], 0)
    causal = np.zeros((P, T), f)
    causal[:, P:] = np.where(p[None, :] > p[:, None], f(NEG), f(0))
    half = HD // 2
    inv = (f(10000.0) ** (-np.arange(half, dtype=f) / f(half))).astype(f)
    ang = np.arange(T, dtype=f)[:, None] * inv[None]
    rope = np.stack([np.cos(ang), np.sin(ang)], 1).astype(f)
    rope = rope.reshape(NT, P, 2, half).transpose(1, 0, 2, 3)
    log_gamma = np.log(1.0 - 2.0 ** (-5.0 - np.arange(NH)))
    m, n = np.arange(T)[:, None], np.arange(T)[None]
    dec = np.where(n >= m, np.exp(np.maximum(n - m, 0)[None] * log_gamma[:, None, None]), 0.0) * HD ** -0.5
    decay = dec[:, :P, :].transpose(1, 0, 2).astype(f)
    dist = 255 - np.arange(LINE)
    me = NBUCKET // 2
    nf = np.maximum(dist, 1).astype(f)
    large = me + (np.log(nf / f(me)) / f(np.log(128 / me)) * f(NBUCKET - me)).astype(np.int32)
    bucket = np.where(dist < me, np.maximum(dist, 0), np.minimum(large, NBUCKET - 1))
    onehot = np.zeros((NBUCKET + 1, LINE), f)
    onehot[np.where(dist >= 0, bucket, NBUCKET), np.arange(LINE)] = 1.0
    tok = np.arange(T)
    cend = np.arange(NCMP) * CMP_STRIDE + CMP_LEN - 1
    cmask = (tok[:, None] >= cend[None]).astype(f).reshape(NT, P, NCMP).transpose(1, 0, 2)
    gmask = (((p // 16) % 2)[:, None] == np.arange(2)[None]).astype(f)
    freq = (f(10000.0) ** (-np.arange(0, MR, 2, dtype=f) / f(MR))).astype(f)
    return {
        "const_ident": ident, "const_triu": triu, "const_tri64": tri64, "const_causal": causal,
        "const_rope": rope, "const_decay": decay, "const_onehot": onehot, "const_cmask": cmask,
        "const_gmask": gmask, "const_freq": np.tile(freq[None], (P, 1)),
    }


class Counts:

    def __init__(self):
        self.own, self.others = {}, {}

    def made(self, sem):
        self.own[sem.name] = self.own.get(sem.name, 0) + 1
        return self.own[sem.name]

    def next(self, sem, n=1):
        self.others[sem.name] = self.others.get(sem.name, 0) + n
        return self.others[sem.name]


class Banks:

    def __init__(self, tensor, full, free):
        self.t, self.full, self.free, self.at, self.n = tensor, full, free, {}, 0

    def turn(self):
        return self.free[self.n % len(self.free)], self.n // len(self.free)

    def fill(self, name):
        self.at[name] = self.n
        self.n += 1
        return self.bank(name)

    def bank(self, name):
        return self.t[:, self.at[name] % len(self.full), :]

    def fills(self, name):
        return self.full[self.at[name] % len(self.full)], 1

    def filled(self, name):
        return self.full[self.at[name] % len(self.full)], self.at[name] // len(self.full) + 1

    def frees(self, name):
        return self.free[self.at[name] % len(self.free)], 1

    def freed(self, name):
        return self.free[self.at[name] % len(self.free)], self.at[name] // len(self.free) + 1


class Weights:

    def __init__(self, raw, pairs, landed, low, manifest):
        self.raw, self.pairs, self.landed, self.low, self.manifest = raw, pairs, landed, low, manifest
        self.pieces = []
        self.split = []
        self.count = [0] * len(landed)

    def size(self, name):
        return self.manifest[name][0]

    def load(self, name):
        slot = len(self.pieces) % len(self.landed)
        self.count[slot] += 16 * len(self.manifest[name][1])
        self.pieces.append([name, slot, self.count[slot], None])
        return self.landed[slot], self.count[slot]

    def plain(self):
        name, slot = self.pieces[-1][:2]
        return self.raw[:, slot, 0:self.size(name)]

    def release(self, sem, value, k=-1):
        self.pieces[k][3] = (sem, value)

    def parts(self, name):
        self.load(name)
        self.split.append([len(self.pieces) - 1, None])
        self.release(self.low, len(self.split))
        return self.low, len(self.split)

    def pair(self, k=-1):
        k = k % len(self.split)
        n = self.size(self.pieces[self.split[k][0]][0])
        return [self.pairs[:, k % self.pairs.shape[1], h, 0:n] for h in range(2)]

    def used(self, sem, value):
        self.split[-1][1] = (sem, value)

    def source(self, k):
        name, slot = self.pieces[self.split[k][0]][:2]
        return self.raw[:, slot, 0:self.size(name)]

    def loaded(self, k):
        name, slot, value, _ = self.pieces[self.split[k][0]]
        return self.landed[slot], value

    def emptied(self, k):
        return self.split[k - self.pairs.shape[1]][1]


def build(nc, a, out):
    ctx = ExitStack()
    with ctx:
        def sb(name, shape, dt=F32):
            return ctx.enter_context(nc.sbuf_tensor(name, shape, dt))

        def sem(name):
            return ctx.enter_context(nc.semaphore(name))

        bias_line = nc.dram_tensor("bias_line", [NH, P, LINE], F32, kind="Internal")

        x = sb("x", [P, NT, D])
        rows = sb("rows", [P, NT, D])
        hTh = sb("hTh", [P, KC, T], F32R)
        hTl = sb("hTl", [P, KC, T], F32R)
        NRAW, NPAIR, PIECE = 3, 3, 2048
        wraw = sb("wraw", [P, NRAW, PIECE])
        wpair = sb("wpair", [P, NPAIR, 2, PIECE], F32R)
        ident = sb("ident", [P, P])
        triu = sb("triu", [P, P])
        tri64 = sb("tri64", [P, HC])
        causal = sb("causal", [P, T])
        rope = sb("rope", [P, NT, 2, HD // 2])
        cmask = sb("cmask", [P, NT, NCMP])
        gmask = sb("gmask", [P, 2])
        freq = sb("freq", [P, MR // 2])
        NVEC = 97
        vecs = sb("vecs", [P, 3, NVEC])
        V_ATTN, V_FFN, V_MIX2, V_FFN2, V_MQ, V_MKV, V_GLU, V_SD, V_LB, V_GMB, V_HG = 0, 16, 32, 48, 64, 67, 69, 73, 77, 85, 93
        relb = sb("relb", [NBUCKET + 1, NH])
        mhalf = sb("mhalf", [P, 64])
        diag = sb("diag", [P, NT, P])
        halfpi = sb("halfpi", [P, 1])
        ss = sb("ss", [P, 64])
        rs = sb("rs", [P, 64])
        sg = sb("sg", [P, 4, T])
        stage = sg[:].rearrange("p (b k) n -> p b (k n)", b=2)
        lbt = sb("lbt", [P, 16])
        posi = sb("posi", [P, NT], I32)
        hidh = sb("hidh", [P, 4, T], F32R)
        hidl = sb("hidl", [P, 4, T], F32R)

        ARENA = 21888
        arena = sb("arena", [P, ARENA])

        class Carve:
            def __init__(self):
                self.at = 0

            def __call__(self, pattern=None, n=0, rows=P, **dims):
                v = arena[0:rows, self.at:self.at + n]
                self.at += n
                assert self.at <= ARENA, self.at
                return v.rearrange(pattern, **dims) if pattern else v

        c1 = Carve()
        proj = c1("p (t n) -> p t n", NT * IN_W, t=NT)
        decay = c1("p (h n) -> p h n", NH * T, h=NH)
        bias = c1("p (h n) -> p h n", NH * 3 * P, h=NH)
        peT = c1("p (j k) -> p j k", 2 * DEPTH * CMP_LEN, rows=HD, j=2 * DEPTH)
        gains = c1("p (l k d) -> p l k d", DEPTH * 4 * HD, l=DEPTH, k=4)
        gmws = c1("p (l g n) -> p l g n", DEPTH * 4 * P, l=DEPTH, g=4)
        cw2 = c1("p (j n) -> p j n", DEPTH * 2 * HD, rows=HD, j=2 * DEPTH)
        qk = c1(None, 6 * T)
        qTr, kTr = (qk[:, k * 3 * T:(k + 1) * 3 * T].rearrange("p (b n) -> p b n", b=3) for k in range(2))
        probs = [qk[:, 0:512], qk[:, 512:1024], proj[:, 0, 0:512], proj[:, 1, 0:512]]
        qkn = c1(None, 5 * T)
        qTn = qkn[:, 0:3 * T].rearrange("p (b n) -> p b n", b=3)
        kTn = qkn[:, 3 * T:].rearrange("p (b n) -> p b n", b=2)
        aT = qkn[0:HD, 0:4 * T].rearrange("p (j g n) -> p j g n", j=2, g=2)
        kTc = c1(None, 16)
        blocks = c1(None, 2 * CMP_LEN * 30)
        blk = blocks[0:HD].rearrange("p (j l n) -> p j l n", j=2, l=CMP_LEN)
        pcT = blocks[0:16, 0:NT * NH * P].rearrange("p (q n) -> p q n", q=NT * NH)
        onehot, line = blocks[0:NBUCKET + 1, 0:LINE], blocks[0:NH, LINE:2 * LINE]
        turned = c1(None, 1536)
        sT = turned.rearrange("p (b n) -> p b n", b=4)
        pT = turned.rearrange("p (b n) -> p b n", b=3)
        qn = c1("p (t n) -> p t n", NT * RET_W, t=NT)
        kn = c1("p (t n) -> p t n", NT * 256, t=NT)
        wsT = c1("p (g n) -> p g n", 4 * P, g=4)
        vn = c1("p (t n) -> p t n", NT * GM_W, t=NT)
        h1 = c1("p (j n) -> p j n", 2 * 30, rows=HD, j=2)
        kc = c1(None, 256, rows=16)
        kcn = c1(None, P, rows=16)
        s_c = c1("p (q n) -> p q n", NT * NH * NCMP, q=NT * NH)
        nmax = c1(None, 32)
        lsum = c1("p (t h b) -> p t h b", 36, t=NT, h=NH)
        gate = c1("p (t h b) -> p t h b", 36, t=NT, h=NH)
        osum = qn
        rsq = rows[:, :, RET_W:2 * RET_W]
        free_rows = rows[:].rearrange("p t n -> p (t n)")
        rtmp = [free_rows[:, 0:768], free_rows[:, 768:1536], qk[:, 0:768], qk[:, 768:1536]]
        nsq = qn.rearrange("p t n -> p (t n)")
        sk = vn.rearrange("p t n -> p (t n)")
        vraw = qn.rearrange("p t n -> p (t n)")[:, 0:3 * P].rearrange("p (k n) -> p k n", k=3)

        c2 = Carve()
        cosT = c2("p (i n) -> p i n", ST * T, i=ST)
        sinT = c2("p (i n) -> p i n", ST * T, i=ST)
        eg = c2("p (t n) -> p t n", NT * 1024, t=NT)
        qTe = c2("p (h n) -> p h n", HG * T, h=HG)
        lf = c2("p (h n) -> p h n", HG * T, h=HG)
        key = c2("p (h n) -> p h n", HG * T, h=HG)
        bcum = c2("p (h n) -> p h n", HG * T, h=HG)
        eb = c2("p (h n) -> p h n", HG * T, h=HG)
        ukk = c2(None, HG * T + NT * HG * P)
        uT = ukk[:, 0:HG * T].rearrange("p (h n) -> p h n", h=HG)
        kk = ukk[:, HG * T:].rearrange("p (t h n) -> p t h n", t=NT, h=HG)
        late = c2(None, 1536)
        state = late.rearrange("p (c h n) -> p c h n", c=3, h=HG)
        att = sg[:, 0:2, :].rearrange("p a n -> p (a n)").rearrange("p (q n) -> p q n", q=NT * HG)
        bbT = c2("p (r i n) -> p r i n", 2 * 4 * P, r=2, i=4)
        cT = c2("p (r i n) -> p r i n", 3 * 4 * P, r=3, i=4)
        mag = c2(None, ST)
        ones = c2(None, HC)
        small2 = c2(None, 32)
        turns = ([m.rearrange("p h n -> p (h n)") for m in (key, bcum, eb, lf)],
                 [qTe.rearrange("p h n -> p (h n)"), eg[:, 0, :], eg[:, 1, :], late[:, 0:1024]])
        turns = [[m.rearrange("p (j n) -> p j n", j=4) for m in s] for s in turns]
        zT = kk.rearrange("p t h n -> p (t h n)").rearrange("p (h n) -> p h n", h=4)
        braw = [key[:, 0, :].rearrange("p (i h) -> p i h", i=ST), key[:, 1, :].rearrange("p (i h) -> p i h", i=ST)]
        bpad = [qTe[:, 0:2, :].rearrange("p a n -> p (a n)").rearrange("p (i n) -> p i n", i=ST),
                qTe[:, 2:4, :].rearrange("p a n -> p (a n)").rearrange("p (i n) -> p i n", i=ST)]
        craw = [lf[:, 0, :].rearrange("p (i n) -> p i n", i=4), lf[:, 1, :].rearrange("p (i n) -> p i n", i=4)]
        cpad = [bcum[:, 0:2, :].rearrange("p a n -> p (a n)").rearrange("p (i n) -> p i n", i=4),
                bcum[:, 2:4, :].rearrange("p a n -> p (a n)").rearrange("p (i n) -> p i n", i=4)]
        bx = [key[:, 2, :].rearrange("p (i h) -> p i h", i=ST), key[:, 3, :].rearrange("p (i h) -> p i h", i=ST)]
        prm = eb.rearrange("p h n -> p (h n)")[:, 0:20 * ST].rearrange("p (k i) -> p k i", i=ST)
        etmp = [e.rearrange("p (i n) -> p i n", i=ST) for e in
                (eg.rearrange("p t n -> p (t n)"), ukk)]

        c3 = Carve()
        oin = c3("p (t n) -> p t n", NT * 704, t=NT)
        osq = c3("p (t n) -> p t n", NT * 640, t=NT)
        kr = c3("p (t n) -> p t n", NT * P, t=NT)
        cqT = c3("p (c n) -> p c n", 3 * T, c=3)
        ckvT = c3("p (c n) -> p c n", 2 * T, c=2)
        krT = c3(None, T)
        qnT = c3("p (h n) -> p h n", MH * T, h=MH)
        knT = c3("p (h n) -> p h n", MH * T, h=MH)
        qr = c3("p (t n) -> p t n", NT * MH * MR, t=NT)
        qrT = c3("p (b n) -> p b n", 4 * T, b=4)
        vt = c3("p (t n) -> p t n", NT * MH * MV, t=NT)
        mtmp = c3("p (k n) -> p k n", 4 * 512, k=4)
        ms = c3("p (b n) -> p b n", 4 * T, b=4)
        mp = c3("p (b n) -> p b n", 4 * T, b=4)
        mpT = c3("p (b n) -> p b n", 4 * T, b=4)
        mang = c3("p (k t n) -> p k t n", 4 * NT * 32, k=4, t=NT)
        mst = c3(None, 64)
        fg = c3(None, D)

        accum = ctx.enter_context(nc.psum_tensor("accum", [P, 4, COLS], F32))
        work = ctx.enter_context(nc.psum_tensor("work", [P, 4, COLS], F32))
        acc = Banks(accum, [sem(f"acc_full{i}") for i in range(4)], [sem(f"acc_free{i}") for i in range(4)])
        wk = Banks(work, [sem(f"work_full{i}") for i in range(4)], [sem(f"work_free{i}") for i in range(4)])

        man = {}

        def piece(name, w, n, pattern="p (c n) -> p c n", **dims):
            man[name] = (n, [(lambda s: s.rearrange(pattern, **dims), w)])

        def panel(name, w, k, cols):
            c0, c1_ = cols
            n, kc = c1_ - c0, k // P
            v = w[:, c0:c1_].rearrange("(c p) n -> p c n", p=P)
            per = min(kc, PIECE // n)
            for h in range(0, kc, per):
                piece((name, h // per), v[:, h:h + per, :], per * n, c=per)

        def ffn_panels(tag, w_in, w_out):
            wv = w_in.rearrange("(c p) n -> p c n", p=P)
            dv = w_out.rearrange("(c p) n -> p c n", p=P)
            for f in range(FC):
                man["gu", tag, f] = (PIECE, [
                    (lambda s, h=h: s.rearrange("p (c h n) -> p c h n", c=KC, h=2)[:, :, h, :],
                     wv[:, :, h * FF + f * P:h * FF + (f + 1) * P]) for h in range(2)])
            for j in range(NSTEP):
                piece(("dn", tag, j), dv[:, j * FSTEP:(j + 1) * FSTEP, :], PIECE, c=FSTEP)

        IN_COLS = [(c, min(c + COLS, IN_W)) for c in range(0, IN_W, COLS)]
        OUT_COLS = [(0, COLS), (COLS, D)]
        for l in range(DEPTH):
            for g, c in enumerate(IN_COLS):
                panel(("in", l, g), a["w_in"][l], D, c)
            for j in range(2):
                man["w1", l, j] = (PIECE, [(lambda s: s[0:HD].rearrange("p (l h) -> p l h", l=CMP_LEN),
                                            a["cmp_w1"][l, j].rearrange("(l d) h -> d l h", d=HD))])
            for g, c in enumerate(OUT_COLS):
                panel(("out", l, g), a["w_out"][l], D, c)
            ffn_panels(l, a["w_gate_up"][l], a["w_down"][l])
            ffn_panels(2 + l, a["ffn_w_in_2"][l], a["ffn_w_out_2"][l])
        for g in range(5):
            if g in (2, 3):
                panel(("even", g), a["even_w_in_2"][0], D, (g * COLS, (g + 1) * COLS))
            else:
                for q in range(2):
                    c = g * COLS + q * T
                    piece((("even", g), q), a["even_w_in_2"][0][:, c:c + T].rearrange("(c p) n -> p c n", p=P), PIECE, c=KC)
        panel("glu", a["s5_w_glu_2"][0], SD, (0, SD))
        ODD_COLS = [(0, 512), (512, 704)]
        for g in range(2):
            panel(("out", 2, g), a["even_w_out_2"][0], D, OUT_COLS[g])
            panel(("out", 3, g), a["odd_w_out_2"][0], D, OUT_COLS[g])
            panel(("odd", g), a["odd_w_in_2"][0], D, ODD_COLS[g])
        for q in range(4):
            panel(("uq", q), a["mla_w_uq_2"][0], MQ, (q * 384, (q + 1) * 384))
        for q in range(2):
            panel(("ukv", q), a["mla_w_ukv_2"][0], MKV, (q * 1024, (q + 1) * 1024))

        names = """x_in ident_in vectors_in params_in tables_in setup_ready vec_ready consts2_in s5_params_in line_ready line_out bias_in mla_in
          pe_chain act_chain dve_chain pool_chain
          norm_sums norm_scale normed hT_high hT_ready w_high w_low piece_used
          proj_ready rotated turned_ret decayed ret_mixed
          head_sums head_scale hg_sums hg_scale lat_sums lat_scale cq_rows nsa_rows nsa_turned blocks_ready blocks_read gelu_ready
          h1_ready kc_raw kc_rows kTc_ready scores_ready probs_ready probsT_ready pv_done
          cmp_scores cmp_exp cmp_probs cmp_turned gates_ready gm_rows silu_ready mixed
          act_silu hid_high hid_ready down_done conv_in conv_done
          s5_dt s5_arg s5_trig lb_arg lb_exp s5_tables s5_pad s5_wT table_done
          hg_tanh hg_forget hg_ln hg_cum hg_exp hg_q hg_kk hg_kkT hg_att hg_state
          scanned last_turned states_ready s5_z z_gated
          odd_ready odd_rows odd_T qrope_rows qrope_T
          m_scores m_probs m_norm m_probsT m_pv pos_ready pos_arg pos_trig out_rows stored""".split()
        S = {n: sem(n) for n in names}
        W = Weights(wraw, wpair, [sem(f"raw_in{i}") for i in range(NRAW)], S["w_low"], man)

        VECTORS = []
        P1 = [(onehot, a["const_onehot"]), (relb[0:NBUCKET, :], a["rel_bias"])]
        TABLES = [(rope[:], a["const_rope"]),
                  (triu[:], a["const_triu"]), (tri64[:], a["const_tri64"]), (causal[:], a["const_causal"]), (cmask[:], a["const_cmask"]),
                  (gmask[:], a["const_gmask"]), (freq[:], a["const_freq"])]

        def vec(at, n, src, slot=0):
            (P1 if slot else VECTORS).append((vraw[at:at + n, slot, :], src))

        vec(V_ATTN, 16, a["attn_norm"].rearrange("l (c p) -> (l c) p", p=P))
        vec(V_FFN, 16, a["ffn_norm"].rearrange("l (c p) -> (l c) p", p=P))
        vec(V_MIX2, 16, a["norm_mix_g_2"].rearrange("l (c p) -> (l c) p", p=P))
        vec(V_FFN2, 16, a["norm_ffn_g_2"].rearrange("l (c p) -> (l c) p", p=P))
        vec(V_MQ, 3, a["mla_q_norm_g_2"].rearrange("l (c p) -> (l c) p", p=P))
        vec(V_MKV, 2, a["mla_kv_norm_g_2"].rearrange("l (c p) -> (l c) p", p=P))
        vec(V_GLU, 4, a["s5_b_glu_2"].rearrange("l (c p) -> (l c) p", p=P))
        vec(V_SD, 4, a["s5_d_2"].rearrange("l (c p) -> (l c) p", p=P))
        vec(V_LB, 8, a["hgrn_lb_logits_2"].rearrange("l (c p) -> (l c) p", p=P))
        vec(V_GMB, 8, a["gm_b"].rearrange("l g p -> (l g) p"))
        vec(V_HG, 4, a["hgrn_norm_g_2"].rearrange("l (c p) -> (l c) p", p=P))
        for l in range(DEPTH):
            vec(0, 66, a["ffn_conv_w_2"][l].rearrange("w (c p) -> (w c) p", p=P), 1 + l)
            vec(66, 22, a["ffn_conv_b_2"][l:l + 1].rearrange("l (c p) -> (l c) p", p=P), 1 + l)
        peraw = vn[:, 0, 0:HD]
        P1.append((peraw, a["cmp_pe"].rearrange("l j k d -> (l j k) d")))
        TABLES.append((gains[:, :, 0, :].rearrange("p l d -> p l d"), a["nsa_q_gain"].partition_broadcast(P)))
        for l in range(DEPTH):
            TABLES.append((gains[:, l, 1:4, :], a["nsa_k_gain"][l].partition_broadcast(P)))
            TABLES.append((gmws[:, l, :, :], a["gm_ws"][l].rearrange("g t s -> t g s")))
            TABLES.append((cw2[:, 2 * l:2 * l + 2, :], a["cmp_w2"][l].rearrange("j d h -> d j h")))
        TABLES.append((decay, a["const_decay"]))
        TABLES.append((posi[:], a["positions_2"].rearrange("b (t p) -> p (b t)", p=P)))

        pview = lambda n: a[n][0].rearrange("(i g) p -> (g p) i", g=2)
        P2 = [(braw[r], a[n][0].rearrange("(i g) p h -> (g p) i h", g=2)) for r, n in enumerate(("s5_b_re_2", "s5_b_im_2"))]
        P2 += [(craw[r], a[n][0].rearrange("(i g) h p -> (g h) i p", i=4)) for r, n in enumerate(("s5_c_re_2", "s5_c_im_2"))]
        P2 += [(prm[:, 0, :], pview("s5_a_re_2")), (prm[:, 1, :], pview("s5_a_im_2"))]
        for g in range(2):
            P2.append((prm[64 * g:64 * g + 64, 2, :],
                       a["s5_log_dt_2"][0].rearrange("(i g) -> g i", g=2)[g].partition_broadcast(64)))

        block = ctx.enter_context(nc.Block())

        @block.tensor
        def _(pe):
            ln, own = Counts(), S["pe_chain"]
            mm = nc.tensor.matmul
            tr = nc.tensor.transpose

            def turn_rows(n, src, blocks):
                for t in range(NT):
                    for q in range(blocks // 4):
                        pe.wait_ge(*wk.turn())
                        b = wk.fill(("T", n, t, q))
                        for k in range(4):
                            c = (4 * q + k) * P
                            i = tr(b[:, k * P:(k + 1) * P], src[:, t, c:c + P], ident[:])
                        i.then_inc(*wk.fills(("T", n, t, q)))

            def mm3(dst, still, move, start, stop):
                mm(dst, still[0], move[0], start=start, stop=False)
                mm(dst, still[0], move[1], start=False, stop=False)
                return mm(dst, still[1], move[0], start=False, stop=stop)

            second_half = []

            def hT_at(c, tokens):
                if c == KC // 2 and second_half:
                    pe.wait_ge(S["hT_ready"], second_half.pop())
                return hTh[:, c, tokens], hTl[:, c, tokens]

            used = [0]

            def piece_used(i):
                i.then_inc(S["piece_used"], 1)
                used[0] += 1
                W.used(S["piece_used"], used[0])

            def rows_by(name, width):
                b = []
                for t in range(NT):
                    pe.wait_ge(*acc.turn())
                    b.append(acc.fill(name + (t,)))
                per = min(KC, PIECE // width)
                for u in range(KC // per):
                    pe.wait_ge(*W.parts((name, u)))
                    w = [m.rearrange("p (c n) -> p c n", c=per) for m in W.pair()]
                    for t in range(NT):
                        for k in range(per):
                            c = u * per + k
                            i = mm3(b[t][:, 0:width], hT_at(c, slice(t * P, (t + 1) * P)), [m[:, k, :] for m in w], c == 0, c == KC - 1)
                        if u == KC // per - 1:
                            i.then_inc(*acc.fills(name + (t,)))
                    if u < KC // per - 1:
                        piece_used(i)
                    else:
                        W.used(*acc.filled(name + (NT - 1,)))

            def hT_of(n):
                for q in range(KC // 4):
                    for t in range(NT):
                        if q == 0:
                            pe.wait_ge(S["normed"], ln.next(S["normed"]))
                        pe.wait_ge(*wk.turn())
                        b = wk.fill(("T", n, t, q))
                        for k in range(4):
                            c = (4 * q + k) * P
                            i = mm(b[:, k * P:(k + 1) * P], x[:, t, c:c + P], diag[:, t, :], start=True, stop=True)
                        i.then_inc(*wk.fills(("T", n, t, q)))
                pe.wait_ge(S["hT_ready"], ln.next(S["hT_ready"], NT))
                second_half.append(ln.next(S["hT_ready"], NT))

            def out_product(l):
                for g in range(2):
                    rows_by(("out", l, g), COLS)

            def ffn(n, tag):
                hT_of(n)
                y = []
                for q in range(4):
                    pe.wait_ge(*acc.turn())
                    y.append(acc.fill(("y", tag, q)))

                def gate_up(f):
                    pe.wait_ge(*wk.turn())
                    b = wk.fill(("gu", tag, f))
                    pe.wait_ge(*W.parts(("gu", tag, f)))
                    w = [m.rearrange("p (c h n) -> p c h n", c=KC, h=2) for m in W.pair()]
                    for h in range(2):
                        for c in range(KC):
                            i = mm3(b[:, h * T:(h + 1) * T], [m[:, c, h, :] for m in w], hT_at(c, slice(0, T)), c == 0, c == KC - 1)
                    i.then_inc(*wk.fills(("gu", tag, f)))
                    W.used(*wk.filled(("gu", tag, f)))

                def down(s):
                    pe.wait_ge(*W.parts(("dn", tag, s)))
                    w = [m.rearrange("p (c n) -> p c n", c=FSTEP) for m in W.pair()]
                    pe.wait_ge(S["hid_ready"], ln.next(S["hid_ready"], FSTEP))
                    for t in range(NT):
                        x_ = slice(t * P, (t + 1) * P)
                        for k in range(FSTEP):
                            f = FSTEP * s + k
                            for h in range(2):
                                i = mm3(y[2 * t + h], (hidh[:, f % 4, x_], hidl[:, f % 4, x_]), [m[:, k, h * COLS:(h + 1) * COLS] for m in w],
                                        f == 0, f == FC - 1)
                                if f == FC - 1:
                                    i.then_inc(*acc.fills(("y", tag, 2 * t + h)))
                    if s < NSTEP - 1:
                        i.then_inc(S["down_done"], 1)
                        W.used(S["down_done"], (NSTEP - 1) * tag + s + 1)
                    else:
                        W.used(*acc.filled(("y", tag, 3)))

                for s in range(NSTEP):
                    for f in range(FSTEP * s, FSTEP * s + FSTEP):
                        gate_up(f)
                    if s >= 1:
                        down(s - 1)
                down(NSTEP - 1)

            pe.wait_ge(S["ident_in"], 16)
            pe.wait_ge(S["vectors_in"], 16 * len(VECTORS))
            pe.wait_ge(*wk.turn())
            b = wk.fill(("vec", 0))
            tr(b[:, 0:NVEC], vraw[0:NVEC, 0, :], ident[0:NVEC, 0:NVEC]).then_inc(*wk.fills(("vec", 0)))

            def other_vectors():
                pe.wait_ge(S["params_in"], 16 * len(P1))
                pe.wait_ge(S["setup_ready"], ln.next(S["setup_ready"]))
                for k in (1, 2):
                    pe.wait_ge(*wk.turn())
                    b = wk.fill(("vec", k))
                    tr(b[:, 0:88], vraw[0:88, k, :], ident[0:88, 0:88]).then_inc(*wk.fills(("vec", k)))
                pe.wait_ge(*wk.turn())
                b = wk.fill(("pe",))
                tr(b[0:HD, 0:P], peraw, ident[:]).then_inc(*wk.fills(("pe",)))
                pe.wait_ge(*wk.turn())
                b = wk.fill(("line",))
                mm(b[0:NH, :], relb[:], onehot, start=True, stop=True).then_inc(*wk.fills(("line",)))

            for l in range(DEPTH):
                hT_of(("mix", l))
                if l == 0:
                    other_vectors()
                def in_panel(g):
                    rows_by(("in", l, g), IN_COLS[g][1] - IN_COLS[g][0])

                def ret_score(h):
                    pe.wait_ge(*wk.turn())
                    b = wk.fill(("rs", l, h))
                    r = slice(HD * (h % 2), HD * (h % 2) + HD)
                    mm(b[:, 0:T], kTr[r, h // 2, 0:P], qTr[r, h // 2, :], start=True, stop=True)
                    mm(b[:, T:T + P], kTr[r, h // 2, P:T], qTr[r, h // 2, P:T], start=True, stop=True).then_inc(*wk.fills(("rs", l, h)))

                for g in (3, 4, 5):
                    in_panel(g)
                pe.wait_ge(*acc.freed(("in", l, 4, NT - 1)))
                for j in range(2):
                    pe.wait_ge(*wk.turn())
                    b = wk.fill(("aT", l, j))
                    for g in range(2):
                        for t in range(NT):
                            c = O_KV + j * P + g * HD
                            i = tr(b[0:HD, (g * NT + t) * P:(g * NT + t + 1) * P], proj[:, t, c:c + HD], ident[:])
                    i.then_inc(*wk.fills(("aT", l, j)))
                in_panel(0)
                in_panel(1)
                pe.wait_ge(S["nsa_rows"], ln.next(S["nsa_rows"]))
                for t in range(NT):
                    pe.wait_ge(*wk.turn())
                    b = wk.fill(("nqT", l, t))
                    for q in range(3):
                        i = tr(b[:, q * P:(q + 1) * P], qn[:, t, q * P:(q + 1) * P], ident[:])
                    i.then_inc(*wk.fills(("nqT", l, t)))
                pe.wait_ge(*wk.turn())
                b = wk.fill(("nkT", l))
                for br in range(2):
                    for t in range(NT):
                        i = tr(b[:, (br * NT + t) * P:(br * NT + t + 1) * P], kn[:, t, br * P:(br + 1) * P], ident[:])
                i.then_inc(*wk.fills(("nkT", l)))
                pe.wait_ge(S["blocks_ready"], ln.next(S["blocks_ready"]))
                pe.wait_ge(*wk.turn())
                b = wk.fill(("h1", l))
                for j in range(2):
                    pe.wait_ge(*W.load(("w1", l, j)))
                    w1 = W.plain()[0:HD].rearrange("p (l h) -> p l h", l=CMP_LEN)
                    for k in range(CMP_LEN):
                        i = mm(b[0:HD, j * 32:j * 32 + 30], w1[:, k, :], blk[:, j, k, :], start=(k == 0), stop=(k == CMP_LEN - 1))
                    W.release(*wk.filled(("h1", l)))
                i.then_inc(*wk.fills(("h1", l)))
                pe.wait_ge(*wk.freed(("h1", l)))
                pe.wait_ge(*wk.turn())
                b = wk.fill(("kc", l))
                for j in range(2):
                    for g in range(2):
                        c = (j * 2 + g) * HD
                        i = mm(b[0:NCMP, c:c + HD], h1[:, j, g * NCMP:(g + 1) * NCMP], cw2[:, 2 * l + j, :], start=True, stop=True)
                i.then_inc(*wk.fills(("kc", l)))
                in_panel(2)
                pe.wait_ge(S["rotated"], ln.next(S["rotated"]))
                for t in range(NT):
                    for k, off in enumerate((O_RQ, O_RK)):
                        pe.wait_ge(*wk.turn())
                        b = wk.fill(("rT", l, t, k))
                        for q in range(3):
                            i = tr(b[:, q * P:(q + 1) * P], proj[:, t, off + q * P:off + (q + 1) * P], ident[:])
                        i.then_inc(*wk.fills(("rT", l, t, k)))
                pe.wait_ge(*wk.freed(("rT", l, NT - 1, 1)))
                pe.wait_ge(S["kc_rows"], ln.next(S["kc_rows"]))
                pe.wait_ge(*wk.turn())
                b = wk.fill(("kcT", l))
                tr(b[:, 0:NCMP], kcn[0:NCMP, :], ident[0:NCMP, 0:NCMP]).then_inc(*wk.fills(("kcT", l)))
                pe.wait_ge(*wk.freed(("nkT", l)))
                pe.wait_ge(*wk.freed(("kcT", l)))
                for g in range(2):
                    pe.wait_ge(*wk.turn())
                    b = wk.fill(("sc", l, g))
                    r = slice(HD * g, HD * g + HD)
                    for t in range(NT):
                        for q in range(HPG):
                            c = (t * HPG + q) * 16
                            i = mm(b[:, c:c + NCMP], qTn[r, q, t * P:(t + 1) * P], kTc[r, 0:NCMP], start=True, stop=True)
                    i.then_inc(*wk.fills(("sc", l, g)))
                in_panel(6)
                o = []
                for t in range(NT):
                    pe.wait_ge(*acc.turn())
                    o.append(acc.fill(("ro", l, t)))

                def ret_out(h):
                    pe.wait_ge(*wk.freed(("rs", l, h)))
                    s = sT[:, h % 4, :]
                    e = slice(h * HD, (h + 1) * HD)
                    v = [proj[:, t, O_RV + h * HD:O_RV + (h + 1) * HD] for t in range(NT)]
                    i = mm(o[0][:, e], s[:, 0:P], v[0], start=True, stop=True)
                    if h == NH - 1:
                        i.then_inc(*acc.fills(("ro", l, 0)))
                    mm(o[1][:, e], s[:, P:2 * P], v[0], start=True, stop=False)
                    i = mm(o[1][:, e], s[:, 2 * P:3 * P], v[1], start=False, stop=True)
                    if h == NH - 1:
                        i.then_inc(*acc.fills(("ro", l, 1)))
                    else:
                        i.then_inc(S["ret_mixed"], 1)

                for h in range(NH + 3):
                    if h >= 3:
                        ret_out(h - 3)
                    if h < NH:
                        ret_score(h)
                pe.wait_ge(*wk.turn())
                b = wk.fill(("wsT", l))
                for g in range(4):
                    i = tr(b[:, g * P:(g + 1) * P], gmws[:, l, g, :], ident[:])
                i.then_inc(*wk.fills(("wsT", l)))
                pe.wait_ge(S["gm_rows"], ln.next(S["gm_rows"]))
                pe.wait_ge(*acc.turn())
                b = acc.fill(("gm", l))
                for g in range(4):
                    i = mm(b[:, g * P:(g + 1) * P].rearrange("p (t n) -> p t n", t=NT), wsT[:, g, :],
                           vn[:, :, g * HD:(g + 1) * HD], start=True, stop=True)
                i.then_inc(*acc.fills(("gm", l)))
                steps = [(t, h) for t in range(NT) for h in range(NH)]
                banks = {}

                def score(n):
                    t, h = steps[n]
                    g, q = h // HPG, h % HPG
                    r = slice(HD * g, HD * g + HD)
                    K = P * (t + 1)
                    pe.wait_ge(*wk.turn())
                    b = wk.fill(("s", l, n))
                    for br in range(2):
                        i = mm(b[:, br * T:br * T + K], qTn[r, q, t * P:(t + 1) * P], kTn[r, br, 0:K], start=True, stop=True)
                    i.then_inc(*wk.fills(("s", l, n)))

                def turn_probs(n):
                    t, h = steps[n]
                    pe.wait_ge(S["probs_ready"], ln.next(S["probs_ready"]))
                    pe.wait_ge(*wk.turn())
                    b = wk.fill(("pT", l, n))
                    for br in range(2):
                        for k in range(t + 1):
                            c = (br * (t + 1) + k) * P
                            i = tr(b[:, c:c + P], probs[n % 4][:, br * T + k * P:br * T + (k + 1) * P], ident[:])
                    i.then_inc(*wk.fills(("pT", l, n)))

                def weigh(n):
                    t, h = steps[n]
                    if h == 0:
                        for br in range(3):
                            pe.wait_ge(*acc.turn())
                            banks[br] = acc.fill(("no", l, t, br))
                        if t == 0:
                            pe.wait_ge(*wk.freed(("pcT", l, 2)))
                    g = h // HPG
                    e = slice(h * HD, (h + 1) * HD)
                    i = mm(banks[0][:, e], pcT[0:NCMP, t * NH + h, :], kc[0:NCMP, P + g * HD:P + (g + 1) * HD], start=True, stop=True)
                    if h == NH - 1:
                        i.then_inc(*acc.fills(("no", l, t, 0)))
                    pe.wait_ge(*wk.freed(("pT", l, n)))
                    for br in range(2):
                        c = O_KV + (1 + br) * 256 + P + g * HD
                        for k in range(t + 1):
                            i = mm(banks[1 + br][:, e], pT[:, n % 3, (br * (t + 1) + k) * P:(br * (t + 1) + k + 1) * P],
                                   proj[:, k, c:c + HD], start=(k == 0), stop=(k == t))
                        if h == NH - 1:
                            i.then_inc(*acc.fills(("no", l, t, 1 + br)))
                    if h < NH - 1:
                        i.then_inc(S["pv_done"], 1)

                for n in range(len(steps) + LAG + 1):
                    if n < len(steps):
                        score(n)
                    if n == 1:
                        pe.wait_ge(S["cmp_probs"], ln.next(S["cmp_probs"]))
                        for k in range(3):
                            pe.wait_ge(*wk.turn())
                            b = wk.fill(("pcT", l, k))
                            for q in range(4):
                                i = tr(b[0:NCMP, q * P:(q + 1) * P], s_c[:, 4 * k + q, :], ident[:])
                            i.then_inc(*wk.fills(("pcT", l, k)))
                    if LAG <= n < len(steps) + LAG:
                        turn_probs(n - LAG)
                    if n > LAG:
                        weigh(n - LAG - 1)
                pe.wait_ge(S["mixed"], ln.next(S["mixed"]))
                turn_rows(("mixed", l), rows, KC)
                for t in range(NT):
                    for q in range(2):
                        pe.wait_ge(*wk.freed(("T", ("mixed", l), t, q)))
                out_product(l)
                ffn(("ffn", l), l)
                if l == DEPTH - 1:
                    pe.wait_ge(S["s5_pad"], ln.next(S["s5_pad"]))
                    for r in range(2):
                        pe.wait_ge(*wk.turn())
                        b = wk.fill(("bbT", r))
                        for k in range(4):
                            i = tr(b[:, k * P:(k + 1) * P], bpad[r][:, 4 * k:4 * k + 4, :].rearrange("p i n -> p (i n)"), ident[:])
                        i.then_inc(*wk.fills(("bbT", r)))
                        pe.wait_ge(*wk.turn())
                        b = wk.fill(("cT", r))
                        for k in range(4):
                            i = tr(b[:, k * P:(k + 1) * P], cpad[r][:, k, :], ident[:])
                        i.then_inc(*wk.fills(("cT", r)))

            hT_of(("mix", 2))
            def even_panel(g):
                if g in (2, 3):
                    rows_by(("even", g), COLS)
                    return
                for q in range(2):
                    pe.wait_ge(*acc.turn())
                    b = acc.fill(("even", g, q))
                    pe.wait_ge(*W.parts((("even", g), q)))
                    w = [m.rearrange("p (c n) -> p c n", c=KC) for m in W.pair()]
                    for k in range(2):
                        for c in range(KC):
                            i = mm3(b[:, k * T:(k + 1) * T], [m[:, c, k * P:(k + 1) * P] for m in w], hT_at(c, slice(0, T)), c == 0, c == KC - 1)
                    i.then_inc(*acc.fills(("even", g, q)))
                    W.used(*acc.filled(("even", g, q)))

            for g in (1, 0, 2, 3):
                even_panel(g)
            pe.wait_ge(S["hg_q"], ln.next(S["hg_q"]))
            pe.wait_ge(*wk.turn())
            b = wk.fill(("att",))
            for n in range(NCH):
                t, po = n // 2, HC * (n % 2)
                for h in range(HG):
                    c = (t * HG + h) * HC
                    i = mm(b[po:po + HC, c:c + HC], bcum[:, h, n * HC:(n + 1) * HC], eb[:, h, n * HC:(n + 1) * HC], start=True, stop=True)
            i.then_inc(*wk.fills(("att",)))
            pe.wait_ge(S["hg_kk"], ln.next(S["hg_kk"]))
            for t in range(NT):
                pe.wait_ge(*wk.turn())
                b = wk.fill(("kkT", t))
                for h in range(HG):
                    i = tr(b[:, h * P:(h + 1) * P], key[:, h, t * P:(t + 1) * P], ident[:])
                i.then_inc(*wk.fills(("kkT", t)))
            even_panel(4)
            pe.wait_ge(*wk.freed(("kkT", NT - 1)))
            pe.wait_ge(*acc.freed(("even", 2, NT - 1)))
            for n in range(NCH - 1):
                t, po = n // 2, HC * (n % 2)
                pe.wait_ge(*wk.turn())
                b = wk.fill(("ds", n))
                for h in range(HG):
                    i = mm(b[:, h * P:(h + 1) * P], kk[po:po + HC, t, h, :], eg[po:po + HC, t, h * P:(h + 1) * P], start=True, stop=True)
                i.then_inc(*wk.fills(("ds", n)))
            pe.wait_ge(S["hg_att"], ln.next(S["hg_att"]))
            o = []
            for t in range(NT):
                pe.wait_ge(*acc.turn())
                o.append(acc.fill(("eo", t)))
            for n in range(NCH):
                t, po = n // 2, HC * (n % 2)
                if n:
                    pe.wait_ge(S["hg_state"], ln.next(S["hg_state"]))
                for h in range(HG):
                    dst = o[t][po:po + HC, h * P:(h + 1) * P]
                    i = mm(dst, att[po:po + HC, t * HG + h, :], eg[po:po + HC, t, h * P:(h + 1) * P], start=True, stop=(n == 0))
                    if n:
                        i = mm(dst, eb[:, h, n * HC:(n + 1) * HC], state[:, n - 1, h, :], start=False, stop=True)
                if n % 2:
                    i.then_inc(*acc.fills(("eo", t)))
            pe.wait_ge(*acc.freed(("even", 4, 1)))
            for q in range(5):
                if q < 4:
                    for k in range(4):
                        pe.wait_ge(*wk.turn())
                        j = wk.n % 4
                        b = wk.fill(("bu", q, j))
                        r = slice(32 * j, 32 * j + 32)
                        mm(b[:, 0:T], bbT[r, 0, q, :], uT[r, q, :], start=True, stop=True, tile_position=(32 * j, 0))
                        mm(b[:, T:2 * T], bbT[r, 1, q, :], uT[r, q, :], start=True, stop=True, tile_position=(32 * j, 0)).then_inc(*wk.fills(("bu", q, j)))
                if q == 2:
                    pe.wait_ge(S["mixed"], ln.next(S["mixed"]))
                    for t in range(NT):
                        pe.wait_ge(*wk.turn())
                        b = wk.fill(("eT", t))
                        for h in range(HG):
                            i = tr(b[:, h * P:(h + 1) * P], rows[:, t, h * P:(h + 1) * P], ident[:])
                        i.then_inc(*wk.fills(("eT", t)))
                if q:
                    cz, sz, cw, sw = turns[(q - 1) % 2]
                    pe.wait_ge(S["states_ready"], ln.next(S["states_ready"], 2 if q < 4 else 1))
                    if q == 4:
                        pe.wait_ge(S["last_turned"], 1)
                    pe.wait_ge(*acc.turn())
                    b = acc.fill(("sy", q - 1))
                    for j in range(4):
                        r = slice(32 * j, 32 * j + 32)
                        mm(b[r, 0:T], cT[:, 0, q - 1, r], cz[:, j, :], start=True, stop=False)
                        mm(b[r, 0:T], cT[:, 1, q - 1, r], sz[:, j, :], start=False, stop=False)
                        mm(b[r, 0:T], cT[:, 1, q - 1, r], cw[:, j, :], start=False, stop=False)
                        i = mm(b[r, 0:T], cT[:, 2, q - 1, r], sw[:, j, :], start=False, stop=True)
                    i.then_inc(*acc.fills(("sy", q - 1)))
            pe.wait_ge(*W.load(("glu", 0)))
            w = W.plain().rearrange("p (c n) -> p c n", c=4)
            b = []
            for o in range(4):
                pe.wait_ge(*wk.turn())
                b.append(wk.fill(("glu", o)))
            for c in range(4):
                pe.wait_ge(S["s5_z"], ln.next(S["s5_z"]))
                for o in range(4):
                    i = mm(b[o][:, 0:T], w[:, c, o * P:(o + 1) * P], zT[:, c, :], start=(c == 0), stop=(c == 3))
                    if c == 3:
                        i.then_inc(*wk.fills(("glu", o)))
            W.release(*wk.filled(("glu", 3)))
            pe.wait_ge(S["hT_ready"], ln.next(S["hT_ready"], 4))
            out_product(2)
            ffn(("ffn", 2), 2)

            hT_of(("mix", 3))
            for g, (c0, c1_) in enumerate(ODD_COLS):
                rows_by(("odd", g), c1_ - c0)
            pe.wait_ge(S["cq_rows"], ln.next(S["cq_rows"]))
            for t in range(NT):
                pe.wait_ge(*wk.turn())
                b = wk.fill(("oT", t, 0))
                for c in range(3):
                    i = tr(b[:, c * P:(c + 1) * P], oin[:, t, c * P:(c + 1) * P], ident[:])
                i.then_inc(*wk.fills(("oT", t, 0)))
            pe.wait_ge(S["odd_T"], ln.next(S["odd_T"], NT))
            for q in range(4):
                if q == 2:
                    pe.wait_ge(S["odd_rows"], ln.next(S["odd_rows"]))
                    for t in range(NT):
                        pe.wait_ge(*wk.turn())
                        b = wk.fill(("oT", t, 1))
                        for c in range(2):
                            tr(b[:, c * P:(c + 1) * P], oin[:, t, MQ + c * P:MQ + (c + 1) * P], ident[:])
                        tr(b[:, 2 * P:3 * P], kr[:, t, :], ident[:]).then_inc(*wk.fills(("oT", t, 1)))
                pe.wait_ge(*W.load((("uq", q), 0)))
                w = W.plain().rearrange("p (c h n) -> p c h n", c=3, h=2)
                pe.wait_ge(*acc.turn())
                b = acc.fill(("qn", q))
                for k in range(2):
                    for c in range(3):
                        i = mm(b[:, k * T:(k + 1) * T], w[:, c, k, 0:MN], cqT[:, c, :], start=(c == 0), stop=(c == 2))
                i.then_inc(*acc.fills(("qn", q)))
                pe.wait_ge(*acc.turn())
                b = acc.fill(("qr", q))
                for t in range(NT):
                    for c in range(3):
                        i = mm(b[:, t * P:(t + 1) * P].rearrange("p (h n) -> p h n", h=2), cqT[:, c, t * P:(t + 1) * P], w[:, c, :, MN:MQK],
                               start=(c == 0), stop=(c == 2))
                i.then_inc(*acc.fills(("qr", q)))
                W.release(*acc.filled(("qr", q)))
            pe.wait_ge(S["odd_T"], ln.next(S["odd_T"], NT))
            ukv = []
            for g in range(2):
                pe.wait_ge(*W.load((("ukv", g), 0)))
                w = W.plain().rearrange("p (c h n) -> p c h n", c=2, h=4)
                ukv.append(w)
                for q in range(2):
                    pe.wait_ge(*acc.turn())
                    b = acc.fill(("kn", 2 * g + q))
                    for k in range(2):
                        for c in range(2):
                            i = mm(b[:, k * T:(k + 1) * T], w[:, c, 2 * q + k, 0:MN], ckvT[:, c, :], start=(c == 0), stop=(c == 1))
                    i.then_inc(*acc.fills(("kn", 2 * g + q)))

            def mla_values():
                for g in range(2):
                    for t in range(NT):
                        pe.wait_ge(*acc.turn())
                        b = acc.fill(("v", t, g))
                        for c in range(2):
                            i = mm(b.rearrange("p (h n) -> p h n", h=4), ckvT[:, c, t * P:(t + 1) * P], ukv[g][:, c, :, MN:MN + MV],
                                   start=(c == 0), stop=(c == 1))
                        i.then_inc(*acc.fills(("v", t, g)))
                    W.release(*acc.filled(("v", NT - 1, g)), g - 2)

            pe.wait_ge(S["qrope_rows"], ln.next(S["qrope_rows"]))
            for t in range(NT):
                pe.wait_ge(*wk.turn())
                b = wk.fill(("qrT", t))
                for q in range(4):
                    i = tr(b[:, q * P:(q + 1) * P], qr[:, t, q * P:(q + 1) * P], ident[:])
                i.then_inc(*wk.fills(("qrT", t)))
            pe.wait_ge(*wk.freed(("qrT", NT - 1)))
            for q in range(4):
                pe.wait_ge(*acc.freed(("qn", q)))
                pe.wait_ge(*acc.freed(("kn", q)))
            steps = [(t, h) for t in range(NT) for h in range(MH)]
            for n in range(len(steps) + LAG + 1):
                if n == LAG:
                    mla_values()
                if n == LAG + 1:
                    for q in range(4):
                        pe.wait_ge(*acc.freed(("v", q % 2, q // 2)))
                if n < len(steps):
                    t, h = steps[n]
                    K = P * (t + 1)
                    r = slice(HD * (h % 2), HD * (h % 2) + HD)
                    pe.wait_ge(*wk.turn())
                    b = wk.fill(("ms", n))
                    mm(b[:, 0:K], qnT[:, h, t * P:(t + 1) * P], knT[:, h, 0:K], start=True, stop=False)
                    mm(b[:, 0:K], qrT[r, h // 2, t * P:(t + 1) * P], krT[r, 0:K], start=False, stop=True).then_inc(*wk.fills(("ms", n)))
                if LAG <= n < len(steps) + LAG:
                    m = n - LAG
                    t, h = steps[m]
                    pe.wait_ge(S["m_norm"], ln.next(S["m_norm"]))
                    pe.wait_ge(*wk.turn())
                    b = wk.fill(("mpT", m))
                    for k in range(t + 1):
                        i = tr(b[:, k * P:(k + 1) * P], mp[:, m % 4, k * P:(k + 1) * P], ident[:])
                    i.then_inc(*wk.fills(("mpT", m)))
                if n > LAG:
                    m = n - LAG - 1
                    t, h = steps[m]
                    if h % 4 == 0:
                        pe.wait_ge(*acc.turn())
                        b2 = acc.fill(("mo", t, h // 4))
                    pe.wait_ge(*wk.freed(("mpT", m)))
                    for k in range(t + 1):
                        i = mm(b2[:, (h % 4) * P:(h % 4 + 1) * P], vt[:, k, h * MV:(h + 1) * MV], mpT[:, m % 4, k * P:(k + 1) * P],
                               start=(k == 0), stop=(k == t))
                    if h % 4 == 3:
                        i.then_inc(*acc.fills(("mo", t, h // 4)))
                    else:
                        i.then_inc(S["m_pv"], 1)
            for t in range(NT):
                for q in range(2):
                    pe.wait_ge(*acc.freed(("mo", t, q)))
            out_product(3)
            ffn(("ffn", 3), 3)

        @block.scalar
        def _(act):
            ln, own = Counts(), S["act_chain"]
            fn = nc.scalar.activation

            def norm(after):
                for t in range(NT):
                    act.wait_ge(*after(t))
                    fn(rows[:, t, :], x[:, t, :], ACT.Square, accum_out=ss[:, t:t + 1]).then_inc(S["norm_sums"], 1)

            highs = [0]

            def split_high(n):
                for k in range(highs[0], min(highs[0] + n, len(W.split))):
                    act.wait_ge(*W.loaded(k))
                    if k >= NPAIR:
                        act.wait_ge(*W.emptied(k))
                    fn(W.pair(k)[0], W.source(k), ACT.Copy).then_inc(S["w_high"], 1)
                    highs[0] = k + 1

            def hT_high(n, t, q):
                act.wait_ge(*wk.freed(("T", n, t, q)))
                fn(hTh[:, 4 * q:4 * q + 4, t * P:(t + 1) * P], stage[:, t, :].rearrange("p (k n) -> p k n", k=4), ACT.Copy).then_inc(S["hT_high"], 1)

            def normed_high(n):
                for q in range(2):
                    for t in range(NT):
                        hT_high(n, t, q)
                split_high(1)

            def mixed_high(l):
                for t in range(NT):
                    for q in range(2):
                        act.wait_ge(*wk.filled(("T", ("mixed", l), t, q)))
                        b = wk.bank(("T", ("mixed", l), t, q)).rearrange("p (k n) -> p k n", k=4)
                        fn(hTh[:, 4 * q:4 * q + 4, t * P:(t + 1) * P], b, ACT.Copy).then_inc(S["hT_high"], 1)

            def s5_steps(s):
                if s == 2:
                    act.wait_ge(S["s5_params_in"], 16 * len(P2))
                    fn(prm[:, 3, :], prm[:, 2, :], ACT.Exp).then_inc(S["s5_dt"], 1)
                    act.wait_ge(S["s5_dt"], ln.made(S["s5_dt"]))
                if s == 4:
                    act.wait_ge(S["s5_arg"], ln.next(S["s5_arg"]))
                    fn(mag, prm[:, 4, :], ACT.Exp).then_inc(own, 1)
                    act.wait_ge(own, ln.made(own))
                    fn(prm[:, 6, :], prm[:, 5, :], ACT.Abs).then_inc(own, 1)
                    act.wait_ge(own, ln.made(own))
                    fn(prm[:, 6, :], prm[:, 6, :], ACT.Sin, scale=-1.0, bias=halfpi[:]).then_inc(own, 1)
                    act.wait_ge(own, ln.made(own))
                    fn(prm[:, 7, :], prm[:, 5, :], ACT.Sin).then_inc(S["s5_trig"], 1)
                    act.wait_ge(S["s5_trig"], ln.made(S["s5_trig"]))

            def ffn(n, tag):
                normed_high(n)
                v = vecs[:, tag - 1, :] if tag >= 2 else None
                for s in range(NSTEP):
                    chunks = range(FSTEP * s, FSTEP * s + FSTEP)
                    if tag == DEPTH - 1:
                        s5_steps(s)
                    split_high(1)
                    for f in chunks:
                        act.wait_ge(*wk.filled(("gu", tag, f)))
                        b = wk.bank(("gu", tag, f))
                        if f >= 4:
                            act.wait_ge(S["hid_ready"], FC * tag + f - 3)
                        if tag < 2:
                            fn(sg[:, f % 4, :], b[:, 0:T], ACT.Silu).then_inc(S["act_silu"], 1)
                        else:
                            fn(sg[:, f % 4, :], b[:, 0:T], ACT.Identity, scale=v[:, 44 + f:45 + f], bias=v[:, 66 + f:67 + f]).then_inc(S["conv_in"], 1)
                    if tag >= 2:
                        for f in chunks:
                            act.wait_ge(S["conv_done"], ln.next(S["conv_done"]))
                            fn(sg[:, f % 4, :], sg[:, f % 4, :], ACT.Silu).then_inc(S["act_silu"], 1)
                    split_high(1)
                    for f in chunks:
                        act.wait_ge(*wk.freed(("gu", tag, f)))
                        if s >= 2:
                            act.wait_ge(S["down_done"], (NSTEP - 1) * tag + s - 1)
                        fn(hidh[:, f % 4, :], sg[:, f % 4, :], ACT.Copy).then_inc(S["hid_high"], 1)
                    if s:
                        split_high(1)

            norm(lambda t: (S["x_in"], 16))

            def line_out():
                act.wait_ge(*wk.filled(("line",)))
                b = wk.bank(("line",))
                fn(line, b[0:NH, :], ACT.Copy).then_inc(*wk.frees(("line",)))
                act.wait_ge(*wk.freed(("line",)))
                act.dma_start(bias_line.ap(), line.unsqueeze(1).to_broadcast([NH, P, LINE])).then_inc(S["line_out"], 16)
                act.wait_ge(S["lb_arg"], ln.next(S["lb_arg"]))
                fn(lbt[:, 0:8], lbt[:, 0:8], ACT.Exp).then_inc(S["lb_exp"], 1)

            for l in range(DEPTH):
                if l:
                    norm(lambda t: acc.freed(("y", l - 1, 2 * t + 1)))
                normed_high(("mix", l))
                if l == 0:
                    split_high(NPAIR - 1)
                    line_out()
                for n, g in enumerate((3, 4, 5, 0, 1, 2, 6)):
                    c0, c1_ = IN_COLS[g]
                    if n < 4:
                        split_high(1)
                    for t in range(NT):
                        act.wait_ge(*acc.filled(("in", l, g, t)))
                        b = acc.bank(("in", l, g, t))
                        fn(proj[:, t, c0:c1_], b[:, 0:c1_ - c0], ACT.Copy).then_inc(*acc.frees(("in", l, g, t)))
                    if n < 4:
                        split_high(1)
                    if (l, g) == (0, 4):
                        act.wait_ge(S["line_out"], 16)
                        for h in range(NH):
                            act.dma_start(bias[:, h, :], bass.AP(bias_line, h * P * LINE + P - 1, [[LINE - 1, P], [1, 3 * P]])).then_inc(S["bias_in"], 16)
                    if g == 5:
                        for j in range(2):
                            act.wait_ge(*wk.filled(("aT", l, j)))
                            b = wk.bank(("aT", l, j))
                            fn(aT[:, j].rearrange("p g n -> p (g n)"), b[0:HD, :], ACT.Copy).then_inc(*wk.frees(("aT", l, j)))
                    if g == 1:
                        for t in range(NT):
                            act.wait_ge(*wk.filled(("nqT", l, t)))
                            b = wk.bank(("nqT", l, t))
                            fn(qTn[:, :, t * P:(t + 1) * P], b[:, 0:384].rearrange("p (b n) -> p b n", b=3), ACT.Copy).then_inc(*wk.frees(("nqT", l, t)))
                        act.wait_ge(*wk.filled(("nkT", l)))
                        b = wk.bank(("nkT", l))
                        fn(kTn.rearrange("p b n -> p (b n)"), b, ACT.Copy).then_inc(*wk.frees(("nkT", l)))
                        act.wait_ge(*wk.filled(("h1", l)))
                        b = wk.bank(("h1", l))
                        fn(h1, b[0:HD, 0:64].rearrange("p (j n) -> p j n", j=2)[:, :, 0:30], ACT.Gelu_apprx_tanh).then_inc(*wk.frees(("h1", l)))
                        split_high(2)
                    if g == 2:
                        for t in range(NT):
                            for k, dst in enumerate((qTr, kTr)):
                                act.wait_ge(*wk.filled(("rT", l, t, k)))
                                b = wk.bank(("rT", l, t, k))
                                fn(dst[:, :, t * P:(t + 1) * P], b[:, 0:384].rearrange("p (b n) -> p b n", b=3), ACT.Copy).then_inc(*wk.frees(("rT", l, t, k)))
                split_high(1)
                act.wait_ge(*acc.freed(("in", l, 6, NT - 1)))
                fn(proj[:, :, O_GM:IN_W], proj[:, :, O_GM:IN_W], ACT.Gelu_apprx_tanh).then_inc(S["gelu_ready"], 1)
                fn(gate.rearrange("p t h b -> p t (h b)"), proj[:, :, O_NG:O_GM], ACT.Tanh, scale=0.5).then_inc(S["gates_ready"], 1)
                fn(proj[:, :, O_RG:O_NQ], proj[:, :, O_RG:O_NQ], ACT.Silu).then_inc(S["silu_ready"], 1)
                act.wait_ge(S["cmp_scores"], ln.next(S["cmp_scores"]))
                fn(s_c, s_c, ACT.Exp).then_inc(S["cmp_exp"], 1)
                for t in range(NT):
                    act.wait_ge(*acc.filled(("ro", l, t)))
                    b = acc.bank(("ro", l, t))
                    fn(rows[:, t, 0:RET_W], b[:, 0:RET_W], ACT.Copy).then_inc(*acc.frees(("ro", l, t)))

                def exps(n):
                    t, h = n // NH, n % NH
                    K = P * (t + 1)
                    act.wait_ge(S["scores_ready"], ln.next(S["scores_ready"]))
                    for br in range(2):
                        s = probs[n % 4][:, br * T:br * T + K]
                        i = fn(s, s, ACT.Exp, bias=nmax[:, 2 * (n % 4) + br:2 * (n % 4) + br + 1], accum_out=lsum[:, t, h, 1 + br:2 + br])
                    i.then_inc(S["probs_ready"], 1)

                def probsT(n):
                    t = n // NH
                    w = 2 * (t + 1) * P
                    m = n - 3
                    if n >= 3 and m % NH < NH - 1:
                        act.wait_ge(S["pv_done"], (NH - 1) * (NT * l + m // NH) + m % NH + 1)
                    elif n >= 3:
                        act.wait_ge(*acc.filled(("no", l, m // NH, 2)))
                    act.wait_ge(*wk.filled(("pT", l, n)))
                    b = wk.bank(("pT", l, n))
                    fn(pT[:, n % 3, 0:w], b[:, 0:w], ACT.Copy).then_inc(*wk.frees(("pT", l, n)))

                for n in range(NT * NH + LAG):
                    if n < NT * NH:
                        exps(n)
                    if n == 0:
                        for k in range(3):
                            act.wait_ge(*wk.filled(("pcT", l, k)))
                            b = wk.bank(("pcT", l, k))
                            fn(pcT[0:NCMP, 4 * k:4 * k + 4, :], b[0:NCMP, :].rearrange("p (q n) -> p q n", q=4), ACT.Copy).then_inc(*wk.frees(("pcT", l, k)))
                    if n >= LAG:
                        probsT(n - LAG)
                    if n in (6, 8):
                        split_high(1)
                mixed_high(l)
                split_high(3)
                if l == DEPTH - 1:
                    act.wait_ge(S["mixed"], ln.next(S["mixed"], DEPTH))
                    for dst, src in P2:
                        act.dma_start(dst, src, allow_slow_non_contiguous=True).then_inc(S["s5_params_in"], 16)
                norm(lambda t: acc.freed(("out", l, 1, t)))
                ffn(("ffn", l), l)

            norm(lambda t: acc.freed(("y", 1, 2 * t + 1)))
            normed_high(("mix", 2))
            for n, g in enumerate((1, 0, 2, 3, 4)):
                split_high(1)
                for q in range(2):
                    act.wait_ge(*acc.filled(("even", g, q)))
                    b = acc.bank(("even", g, q))
                    if g == 1:
                        fn(lf[:, 2 * q:2 * q + 2, :].rearrange("p h n -> p (h n)"), b, ACT.Tanh, scale=0.5).then_inc(*acc.frees(("even", g, q)))
                    elif g in (0, 4):
                        dst = qTe if g == 0 else uT
                        fn(dst[:, 2 * q:2 * q + 2, :].rearrange("p h n -> p (h n)"), b, ACT.Copy).then_inc(*acc.frees(("even", g, q)))
                    else:
                        fn(eg[:, q, (g - 2) * 512:(g - 1) * 512], b, ACT.Copy).then_inc(*acc.frees(("even", g, q)))
                if n < 4:
                    split_high(1)
                if g == 0:
                    act.wait_ge(S["hg_forget"], ln.next(S["hg_forget"]))
                    fn(lf, lf, ACT.Ln).then_inc(S["hg_ln"], 1)
                if g == 2:
                    act.wait_ge(S["hg_cum"], ln.next(S["hg_cum"]))
                    fn(eb, bcum, ACT.Exp).then_inc(own, 1)
                    act.wait_ge(own, ln.made(own))
                    act.wait_ge(S["hg_cum"], ln.next(S["hg_cum"]))
                    fn(bcum, bcum, ACT.Exp, scale=-1.0).then_inc(S["hg_exp"], 1)
                    fn(lf, lf, ACT.Exp).then_inc(S["hg_exp"], 1)
                if g == 3:
                    for t in range(NT):
                        act.wait_ge(*wk.filled(("kkT", t)))
                        b = wk.bank(("kkT", t))
                        fn(kk[:, t].rearrange("p h n -> p (h n)"), b, ACT.Copy).then_inc(*wk.frees(("kkT", t)))
                    act.wait_ge(*acc.freed(("even", 3, 1)))
                    fn(eg[:, :, 512:1024], eg[:, :, 512:1024], ACT.Silu).then_inc(S["silu_ready"], 1)
            for t in range(NT):
                act.wait_ge(*acc.filled(("eo", t)))
                b = acc.bank(("eo", t))
                for h in range(HG):
                    i = fn(kk[:, t, h, :], b[:, h * P:(h + 1) * P], ACT.Square, accum_out=ss[:, 4 + HG * t + h:5 + HG * t + h])
            i.then_inc(S["hg_sums"], 1)
            act.wait_ge(S["hg_scale"], ln.next(S["hg_scale"]))
            for t in range(NT):
                b = acc.bank(("eo", t))
                for h in range(HG):
                    i = fn(rows[:, t, h * P:(h + 1) * P], b[:, h * P:(h + 1) * P], ACT.Identity, scale=rs[:, 4 + HG * t + h:5 + HG * t + h])
                i.then_inc(*acc.frees(("eo", t)))
            for t in range(NT):
                act.wait_ge(*wk.freed(("eT", t)))
                fn(hTh[:, 0:4, t * P:(t + 1) * P], stage[:, t, :].rearrange("p (k n) -> p k n", k=4), ACT.Copy).then_inc(S["hT_high"], 1)
            for q in range(4):
                act.wait_ge(*acc.freed(("sy", q)))
                fn(zT[:, q, :], uT[:, q, :], ACT.Gelu_apprx_tanh).then_inc(S["s5_z"], 1)
            for o in range(4):
                act.wait_ge(*wk.filled(("glu", o)))
                fn(qTe[:, o, :], wk.bank(("glu", o))[:, 0:T], ACT.Tanh, scale=0.5, bias=small2[:, 8 + o:9 + o]).then_inc(*wk.frees(("glu", o)))
            for q in range(2):
                act.wait_ge(S["z_gated"], ln.next(S["z_gated"]))
                fn(hTh[:, 4 + 2 * q:6 + 2 * q, :], zT[:, 2 * q:2 * q + 2, :], ACT.Copy, scale=0.5).then_inc(S["hT_high"], 1)
            split_high(4)
            norm(lambda t: acc.freed(("out", 2, 1, t)))
            ffn(("ffn", 2), 2)

            act.wait_ge(S["pos_arg"], ln.next(S["pos_arg"]))
            act.dma_start(fg, a["final_norm_g_2"].partition_broadcast(P)).then_inc(S["mla_in"], 16)
            fn(mang[:, 1], mang[:, 0], ACT.Abs).then_inc(own, 1)
            act.wait_ge(own, ln.made(own))
            fn(mang[:, 2], mang[:, 1], ACT.Sin, scale=-1.0, bias=halfpi[:]).then_inc(own, 1)
            act.wait_ge(own, ln.made(own))
            fn(mang[:, 3], mang[:, 0], ACT.Sin).then_inc(S["pos_trig"], 1)
            act.wait_ge(S["pos_trig"], ln.made(S["pos_trig"]))
            norm(lambda t: acc.freed(("y", 2, 2 * t + 1)))
            normed_high(("mix", 3))
            for g, (c0, c1_) in enumerate(ODD_COLS):
                for t in range(NT):
                    act.wait_ge(*acc.filled(("odd", g, t)))
                    b = acc.bank(("odd", g, t))
                    if g == 0:
                        fn(osq[:, t, 0:MQ], b[:, 0:MQ], ACT.Square, accum_out=ss[:, 4 + t:5 + t])
                    fn(oin[:, t, c0:c1_], b[:, 0:c1_ - c0], ACT.Copy).then_inc(*acc.frees(("odd", g, t)))
                if g == 1:
                    act.wait_ge(*acc.freed(("odd", g, NT - 1)))
                    for t in range(NT):
                        i = fn(osq[:, t, MQ:MQ + MKV], oin[:, t, MQ:MQ + MKV], ACT.Square, accum_out=ss[:, 6 + t:7 + t])
                    i.then_inc(S["lat_sums"], 1)
                else:
                    act.wait_ge(*acc.freed(("odd", g, NT - 1)))
                    act.sem_inc(S["lat_sums"], 1)
            for q in range(4):
                act.wait_ge(*acc.filled(("qn", q)))
                b = acc.bank(("qn", q))
                fn(qnT[:, 2 * q:2 * q + 2, :].rearrange("p h n -> p (h n)"), b, ACT.Copy).then_inc(*acc.frees(("qn", q)))
                act.wait_ge(*acc.filled(("qr", q)))
                b = acc.bank(("qr", q))
                fn(qr[:, :, q * P:(q + 1) * P], b[:, 0:T].rearrange("p (t n) -> p t n", t=NT), ACT.Copy).then_inc(*acc.frees(("qr", q)))
            for g in range(2):
                for q in range(2 * g, 2 * g + 2):
                    act.wait_ge(*acc.filled(("kn", q)))
                    b = acc.bank(("kn", q))
                    fn(knT[:, 2 * q:2 * q + 2, :].rearrange("p h n -> p (h n)"), b, ACT.Copy).then_inc(*acc.frees(("kn", q)))
            for t in range(NT):
                act.wait_ge(*wk.filled(("qrT", t)))
                b = wk.bank(("qrT", t))
                fn(qrT[:, :, t * P:(t + 1) * P], b.rearrange("p (b n) -> p b n", b=4), ACT.Copy).then_inc(*wk.frees(("qrT", t)))
            for n in range(NT * MH + LAG):
                if n == LAG:
                    for g in range(2):
                        for t in range(NT):
                            act.wait_ge(*acc.filled(("v", t, g)))
                            fn(vt[:, t, g * 512:(g + 1) * 512], acc.bank(("v", t, g)), ACT.Copy).then_inc(*acc.frees(("v", t, g)))
                if n < NT * MH:
                    K = P * (n // MH + 1)
                    act.wait_ge(S["m_scores"], ln.next(S["m_scores"]))
                    if n >= 4:
                        act.wait_ge(*wk.filled(("mpT", n - 4)))
                    fn(mp[:, n % 4, 0:K], ms[:, n % 4, 0:K], ACT.Exp, bias=mst[:, n:n + 1], accum_out=mst[:, 16 + n:17 + n]).then_inc(S["m_probs"], 1)
                if n >= LAG:
                    m = n - LAG
                    K = P * (m // MH + 1)
                    r = m - 4
                    if m >= 4 and r % 4 < 3:
                        act.wait_ge(S["m_pv"], 3 * (r // 4) + r % 4 + 1)
                    elif m >= 4:
                        act.wait_ge(*acc.filled(("mo", r // MH, (r % MH) // 4)))
                    act.wait_ge(*wk.filled(("mpT", m)))
                    b = wk.bank(("mpT", m))
                    fn(mpT[:, m % 4, 0:K], b[:, 0:K], ACT.Copy).then_inc(*wk.frees(("mpT", m)))
                if n in (6, 8, 10):
                    split_high(1)
            for t in range(NT):
                for q in range(2):
                    act.wait_ge(*acc.filled(("mo", t, q)))
                    b = acc.bank(("mo", t, q)).rearrange("p (k n) -> p k n", k=4)
                    fn(hTh[:, 4 * q:4 * q + 4, t * P:(t + 1) * P], b, ACT.Copy).then_inc(S["hT_high"], 1)
            split_high(3)
            norm(lambda t: acc.freed(("out", 3, 1, t)))
            ffn(("ffn", 3), 3)
            norm(lambda t: acc.freed(("y", 3, 2 * t + 1)))

        @block.gpsimd
        def _(pool):
            ln, own = Counts(), S["pool_chain"]
            tt, ts = nc.gpsimd.tensor_tensor, nc.gpsimd.tensor_scalar
            nc.gpsimd.memset(mhalf[:], -0.5).then_inc(own, 1)
            pool.wait_ge(own, ln.made(own))
            nc.gpsimd.memset(halfpi[:], float(np.pi / 2)).then_inc(own, 1)
            pool.wait_ge(own, ln.made(own))
            nc.gpsimd.memset(relb[NBUCKET:NBUCKET + 1, :], NEG).then_inc(S["setup_ready"], 1)
            pool.wait_ge(S["setup_ready"], ln.made(S["setup_ready"]))

            def inverse_root(parts, c0, n, width, sem_):
                ts(rs[0:parts, c0:c0 + n], ss[0:parts, c0:c0 + n], 1.0 / width, EPS, ALU.mult, ALU.add).then_inc(own, 1)
                pool.wait_ge(own, ln.made(own))
                tt(rs[0:parts, c0:c0 + n], rs[0:parts, c0:c0 + n], mhalf[0:parts, 0:n], ALU.pow).then_inc(sem_, 1)
                pool.wait_ge(sem_, ln.made(sem_))

            def norm():
                for t in range(NT):
                    pool.wait_ge(S["norm_sums"], ln.next(S["norm_sums"]))
                    inverse_root(P, t, 1, D, S["norm_scale"])

            def heads(c0, n, width, parts=P):
                pool.wait_ge(S["head_sums"], ln.next(S["head_sums"]))
                inverse_root(parts, c0, n, width, S["head_scale"])

            def s5_tables():
                K = lambda k: prm[:, k, :]
                ar, ai, arg, th, co, si, den, xr, xi, k1, k2 = (K(k) for k in (0, 1, 4, 5, 6, 7, 8, 9, 10, 11, 12))
                pool.wait_ge(S["s5_dt"], ln.next(S["s5_dt"]))
                tt(arg, ar, K(3), ALU.mult).then_inc(own, 1)
                pool.wait_ge(own, ln.made(own))
                tt(th, ai, K(3), ALU.mult).then_inc(own, 1)
                pool.wait_ge(own, ln.made(own))
                ts(k1, th, 1.0 / TWO_PI, MAGIC, ALU.mult, ALU.add).then_inc(own, 1)
                pool.wait_ge(own, ln.made(own))
                ts(k1, k1, -MAGIC, None, ALU.add).then_inc(own, 1)
                pool.wait_ge(own, ln.made(own))
                for c in (CW1, CW2, CW3):
                    ts(k2, k1, -c, None, ALU.mult).then_inc(own, 1)
                    pool.wait_ge(own, ln.made(own))
                    tt(th, th, k2, ALU.add).then_inc(own, 1)
                    pool.wait_ge(own, ln.made(own))
                ts(th, th, PI_SAFE, -PI_SAFE, ALU.min, ALU.max).then_inc(S["s5_arg"], 1)
                pool.wait_ge(S["s5_arg"], ln.made(S["s5_arg"]))
                tt(den, ar, ar, ALU.mult).then_inc(own, 1)
                pool.wait_ge(own, ln.made(own))
                tt(k2, ai, ai, ALU.mult).then_inc(own, 1)
                pool.wait_ge(own, ln.made(own))
                tt(den, den, k2, ALU.add).then_inc(own, 1)
                pool.wait_ge(own, ln.made(own))
                nc.gpsimd.memset(k1, -1.0).then_inc(own, 1)
                pool.wait_ge(own, ln.made(own))
                tt(den, den, k1, ALU.pow).then_inc(own, 1)
                pool.wait_ge(own, ln.made(own))
                for m in bpad:
                    nc.gpsimd.memset(m, 0.0).then_inc(own, 1)
                    pool.wait_ge(own, ln.made(own))
                for g in range(2):
                    ts(cpad[0][:, :, 64 * g:64 * g + 64], craw[0], gmask[:, g:g + 1], None, ALU.mult).then_inc(own, 1)
                    pool.wait_ge(own, ln.made(own))
                    ts(cpad[1][:, :, 64 * g:64 * g + 64], craw[1], gmask[:, g:g + 1], -1.0, ALU.mult, ALU.mult).then_inc(own, 1)
                    pool.wait_ge(own, ln.made(own))
                pool.wait_ge(S["s5_trig"], ln.next(S["s5_trig"]))
                tt(xr, mag, co, ALU.mult).then_inc(own, 1)
                pool.wait_ge(own, ln.made(own))
                ts(xr, xr, -1.0, None, ALU.add).then_inc(own, 1)
                pool.wait_ge(own, ln.made(own))
                tt(xi, mag, si, ALU.mult).then_inc(own, 1)
                pool.wait_ge(own, ln.made(own))
                cr, ci = K(13), K(14)
                tt(cr, xr, ar, ALU.mult).then_inc(own, 1)
                pool.wait_ge(own, ln.made(own))
                tt(k2, xi, ai, ALU.mult).then_inc(own, 1)
                pool.wait_ge(own, ln.made(own))
                tt(cr, cr, k2, ALU.add).then_inc(own, 1)
                pool.wait_ge(own, ln.made(own))
                tt(cr, cr, den, ALU.mult).then_inc(own, 1)
                pool.wait_ge(own, ln.made(own))
                tt(ci, xi, ar, ALU.mult).then_inc(own, 1)
                pool.wait_ge(own, ln.made(own))
                tt(k2, xr, ai, ALU.mult).then_inc(own, 1)
                pool.wait_ge(own, ln.made(own))
                tt(ci, ci, k2, ALU.subtract).then_inc(own, 1)
                pool.wait_ge(own, ln.made(own))
                tt(ci, ci, den, ALU.mult).then_inc(own, 1)
                pool.wait_ge(own, ln.made(own))

                def each(ap, n):
                    return ap.unsqueeze(2).to_broadcast([ap.shape[0], ST, n])

                for r, (f1, f2, op) in enumerate(((cr, ci, ALU.subtract), (ci, cr, ALU.add))):
                    tt(bx[0], braw[0], each(f1, 16), ALU.mult).then_inc(own, 1)
                    pool.wait_ge(own, ln.made(own))
                    tt(bx[1], braw[1], each(f2, 16), ALU.mult).then_inc(own, 1)
                    pool.wait_ge(own, ln.made(own))
                    for g in range(2):
                        p_ = slice(64 * g, 64 * g + 64)
                        to = S["s5_pad"] if r and g else own
                        tt(bpad[r][p_, :, 16 * g:16 * g + 16], bx[0][p_], bx[1][p_], op).then_inc(to, 1)
                        pool.wait_ge(to, ln.made(to))
                nc.gpsimd.memset(cosT[:, :, 0:1], 1.0).then_inc(own, 1)
                pool.wait_ge(own, ln.made(own))
                nc.gpsimd.memset(sinT[:, :, 0:1], 0.0).then_inc(own, 1)
                pool.wait_ge(own, ln.made(own))
                n = 1
                while n < T:
                    A, B = etmp[0][:, :, 0:n], etmp[1][:, :, 0:n]
                    tt(A, cosT[:, :, 0:n], each(co, n), ALU.mult).then_inc(own, 1)
                    pool.wait_ge(own, ln.made(own))
                    tt(B, sinT[:, :, 0:n], each(si, n), ALU.mult).then_inc(own, 1)
                    pool.wait_ge(own, ln.made(own))
                    tt(cosT[:, :, n:2 * n], A, B, ALU.subtract).then_inc(own, 1)
                    pool.wait_ge(own, ln.made(own))
                    tt(A, sinT[:, :, 0:n], each(co, n), ALU.mult).then_inc(own, 1)
                    pool.wait_ge(own, ln.made(own))
                    tt(B, cosT[:, :, 0:n], each(si, n), ALU.mult).then_inc(own, 1)
                    pool.wait_ge(own, ln.made(own))
                    to = S["table_done"] if 2 * n == T else own
                    tt(sinT[:, :, n:2 * n], A, B, ALU.add).then_inc(to, 1)
                    pool.wait_ge(to, ln.made(to))
                    tt(k1, co, co, ALU.mult).then_inc(own, 1)
                    pool.wait_ge(own, ln.made(own))
                    tt(k2, si, si, ALU.mult).then_inc(own, 1)
                    pool.wait_ge(own, ln.made(own))
                    tt(si, co, si, ALU.mult).then_inc(own, 1)
                    pool.wait_ge(own, ln.made(own))
                    ts(si, si, 2.0, None, ALU.mult).then_inc(own, 1)
                    pool.wait_ge(own, ln.made(own))
                    tt(co, k1, k2, ALU.subtract).then_inc(own, 1)
                    pool.wait_ge(own, ln.made(own))
                    n *= 2

            for l in range(DEPTH):
                norm()
                heads(4, 20, HD)
                heads(32, 2, HD, NCMP)
                heads(24, 8, HD)
                heads(36, 12, HD)
                norm()
            s5_tables()
            norm()
            pool.wait_ge(S["hg_sums"], ln.next(S["hg_sums"]))
            inverse_root(P, 4, 8, 128, S["hg_scale"])
            for q in range(4):
                co, si = cosT[:, 4 * q:4 * q + 4, :], sinT[:, 4 * q:4 * q + 4, :]
                A, B, C, E_ = turns[q % 2]
                pool.wait_ge(S["scanned"], 2 * q + 1)
                tt(A, co, B, ALU.mult).then_inc(own, 1)
                pool.wait_ge(own, ln.made(own))
                tt(B, si, B, ALU.mult).then_inc(S["states_ready"], 1)
                if q < 3:
                    pool.wait_ge(S["scanned"], 2 * q + 2)
                    tt(C, co, E_, ALU.mult).then_inc(own, 1)
                    pool.wait_ge(own, ln.made(own))
                    tt(E_, si, E_, ALU.mult).then_inc(S["states_ready"], 1)
            norm()
            norm()
            for c, width in ((4, MQ), (6, MKV)):
                pool.wait_ge(S["lat_sums"], ln.next(S["lat_sums"]))
                inverse_root(P, c, 2, width, S["lat_scale"])
            norm()
            norm()

        @block.vector
        def _(dve):
            ln, own = Counts(), S["dve_chain"]
            v = nc.vector
            tt, ts, stt = v.tensor_tensor, v.tensor_scalar, v.scalar_tensor_tensor

            def over(ap, n):
                return ap.unsqueeze(len(ap.shape)).to_broadcast(list(ap.shape) + [n])

            def across(ap, at, n):
                s = list(ap.shape)
                return ap.unsqueeze(at).to_broadcast(s[:at] + [n] + s[at:])

            lows = [0]

            def split_low(n):
                for k in range(lows[0], min(lows[0] + n, len(W.split))):
                    dve.wait_ge(S["w_high"], k + 1)
                    hi, lo = W.pair(k)
                    tt(lo, W.source(k), hi, ALU.subtract).then_inc(S["w_low"], 1)
                    lows[0] = k + 1

            def into_hT(n, gain):
                def low(t, q):
                    c = (slice(None), slice(4 * q, 4 * q + 4), slice(t * P, (t + 1) * P))
                    dve.wait_ge(S["hT_high"], ln.next(S["hT_high"]))
                    tt(hTl[c], stage[:, t, :].rearrange("p (k n) -> p k n", k=4), hTh[c], ALU.subtract).then_inc(S["hT_ready"], 1)

                for t in range(NT):
                    dve.wait_ge(S["norm_scale"], ln.next(S["norm_scale"]))
                    ts(diag[:, t, :], ident[:], rs[:, t:t + 1], None, ALU.mult).then_inc(S["normed"], 1)
                for q in range(2):
                    for t in range(NT):
                        if q:
                            low(t, q - 1)
                            dve.wait_ge(S["hT_ready"], ln.made(S["hT_ready"]))
                        dve.wait_ge(*wk.filled(("T", n, t, q)))
                        b = wk.bank(("T", n, t, q)).rearrange("p (k n) -> p k n", k=4)
                        tt(stage[:, t, :].rearrange("p (k n) -> p k n", k=4), b, over(vecs[:, 0, gain + 4 * q:gain + 4 * q + 4], P), ALU.mult).then_inc(*wk.frees(("T", n, t, q)))
                for t in range(NT):
                    low(t, 1)
                    dve.wait_ge(S["hT_ready"], ln.made(S["hT_ready"]))
                split_low(1)

            def mixed_low(l):
                for t in range(NT):
                    for q in range(2):
                        c = (slice(None), slice(4 * q, 4 * q + 4), slice(t * P, (t + 1) * P))
                        b = wk.bank(("T", ("mixed", l), t, q)).rearrange("p (k n) -> p k n", k=4)
                        dve.wait_ge(S["hT_high"], ln.next(S["hT_high"]))
                        tt(hTl[c], b, hTh[c], ALU.subtract).then_inc(*wk.frees(("T", ("mixed", l), t, q)))

            def add_out(tag):
                for t in range(NT):
                    for g in range(2):
                        name = "y", tag, 2 * t + g
                        dve.wait_ge(*acc.filled(name))
                        xs = x[:, t, g * COLS:(g + 1) * COLS]
                        tt(xs, xs, acc.bank(name), ALU.add).then_inc(*acc.frees(name))

            def add_mix(l, g):
                for t in range(NT):
                    dve.wait_ge(*acc.filled(("out", l, g, t)))
                    xs = x[:, t, g * COLS:(g + 1) * COLS]
                    tt(xs, xs, acc.bank(("out", l, g, t)), ALU.add).then_inc(*acc.frees(("out", l, g, t)))

            def ffn(n, tag, gain):
                into_hT(n, gain)
                w = vecs[:, tag - 1, :] if tag >= 2 else None
                for s in range(NSTEP):
                    chunks = range(FSTEP * s, FSTEP * s + FSTEP)
                    split_low(1)
                    if tag >= 2:
                        for f in chunks:
                            c, b = sg[:, f % 4, :], wk.bank(("gu", tag, f))
                            dve.wait_ge(S["conv_in"], ln.next(S["conv_in"]))
                            stt(c[:, 1:T], b[:, 0:T - 1], w[:, 22 + f:23 + f], c[:, 1:T], ALU.mult, ALU.add).then_inc(own, 1)
                            dve.wait_ge(own, ln.made(own))
                            stt(c[:, 2:T], b[:, 0:T - 2], w[:, f:f + 1], c[:, 2:T], ALU.mult, ALU.add).then_inc(S["conv_done"], 1)
                    for f in chunks:
                        b = wk.bank(("gu", tag, f))
                        dve.wait_ge(S["act_silu"], ln.next(S["act_silu"]))
                        tt(sg[:, f % 4, :], sg[:, f % 4, :], b[:, T:2 * T], ALU.mult).then_inc(*wk.frees(("gu", tag, f)))
                    split_low(1)
                    for f in chunks:
                        dve.wait_ge(S["hid_high"], ln.next(S["hid_high"]))
                        tt(hidl[:, f % 4, :], sg[:, f % 4, :], hidh[:, f % 4, :], ALU.subtract).then_inc(S["hid_ready"], 1)
                    if s:
                        split_low(1)
                add_out(tag)

            def rotate(src, cos, sin, heads, tmp):
                lo, hi = src[:, :, :, 0:32], src[:, :, :, 32:64]
                c, s = across(cos, 2, heads), across(sin, 2, heads)
                tmp = [tmp[k].rearrange("p (t h d) -> p t h d", t=NT, h=heads) for k in range(4)]
                for k, (p_, q_) in enumerate(((lo, c), (hi, s), (hi, c), (lo, s))):
                    tt(tmp[k], p_, q_, ALU.mult).then_inc(own, 1)
                    dve.wait_ge(own, ln.made(own))
                tt(lo, tmp[0], tmp[1], ALU.subtract).then_inc(own, 1)
                dve.wait_ge(own, ln.made(own))
                tt(hi, tmp[2], tmp[3], ALU.add).then_inc(own, 1)
                dve.wait_ge(own, ln.made(own))

            def combine(l, t):
                dve.wait_ge(S["probs_ready"], NT * NH * l + NH * (t + 1))
                v.reciprocal(lsum[:, t], lsum[:, t]).then_inc(own, 1)
                dve.wait_ge(own, ln.made(own))
                tt(gate[:, t], gate[:, t], lsum[:, t], ALU.mult).then_inc(own, 1)
                dve.wait_ge(own, ln.made(own))
                dst = rows[:, t, RET_W:2 * RET_W].rearrange("p (h d) -> p h d", d=HD)
                for br in range(3):
                    dve.wait_ge(*acc.filled(("no", l, t, br)))
                    b = acc.bank(("no", l, t, br))[:, 0:RET_W].rearrange("p (h d) -> p h d", d=HD)
                    o = dst if br == 0 else osum[:, t, :].rearrange("p (h d) -> p h d", d=HD)
                    tt(o, b, over(gate[:, t, :, br], HD), ALU.mult).then_inc(*acc.frees(("no", l, t, br)))
                    dve.wait_ge(*acc.freed(("no", l, t, br)))
                    if br:
                        to = S["mixed"] if t and br == 2 else own
                        tt(dst, dst, o, ALU.add).then_inc(to, 1)
                        dve.wait_ge(to, ln.made(to))

            dve.wait_ge(S["ident_in"], 16)
            dve.wait_ge(*wk.filled(("vec", 0)))
            v.tensor_copy(vecs[:, 0, 0:NVEC], wk.bank(("vec", 0))[:, 0:NVEC]).then_inc(*wk.frees(("vec", 0)))
            dve.wait_ge(*wk.freed(("vec", 0)))

            def other_vectors():
                for k in (1, 2):
                    dve.wait_ge(*wk.filled(("vec", k)))
                    v.tensor_copy(vecs[:, k, 0:88], wk.bank(("vec", k))[:, 0:88]).then_inc(*wk.frees(("vec", k)))
                dve.wait_ge(*wk.filled(("pe",)))
                b = wk.bank(("pe",))
                v.tensor_copy(peT[:].rearrange("p j k -> p (j k)"), b[0:HD, 0:P]).then_inc(*wk.frees(("pe",)))
                dve.wait_ge(*wk.freed(("pe",)))
                l0, l1 = vecs[:, 0, V_LB:V_LB + 4], vecs[:, 0, V_LB + 4:V_LB + 8]
                tt(lbt[:, 8:12], l0, l1, ALU.max).then_inc(own, 1)
                dve.wait_ge(own, ln.made(own))
                tt(lbt[:, 0:4], l0, lbt[:, 8:12], ALU.subtract).then_inc(own, 1)
                dve.wait_ge(own, ln.made(own))
                tt(lbt[:, 4:8], l1, lbt[:, 8:12], ALU.subtract).then_inc(S["lb_arg"], 1)
                dve.wait_ge(S["lb_arg"], ln.made(S["lb_arg"]))
                dve.wait_ge(S["lb_exp"], ln.next(S["lb_exp"]))
                tt(lbt[:, 12:16], lbt[:, 0:4], lbt[:, 4:8], ALU.add).then_inc(own, 1)
                dve.wait_ge(own, ln.made(own))
                v.reciprocal(lbt[:, 12:16], lbt[:, 12:16]).then_inc(own, 1)
                dve.wait_ge(own, ln.made(own))
                tt(lbt[:, 8:12], lbt[:, 0:4], lbt[:, 12:16], ALU.mult).then_inc(own, 1)
                dve.wait_ge(own, ln.made(own))
                ts(lbt[:, 12:16], lbt[:, 8:12], -0.5, 0.5, ALU.mult, ALU.add).then_inc(own, 1)
                dve.wait_ge(own, ln.made(own))
                tt(lbt[:, 8:12], lbt[:, 8:12], lbt[:, 12:16], ALU.add).then_inc(own, 1)
                dve.wait_ge(own, ln.made(own))


            for l in range(DEPTH):
                into_hT(("mix", l), V_ATTN + KC * l)
                if l == 0:
                    split_low(2)
                    other_vectors()
                split_low(6)
                if l == 0:
                    dve.wait_ge(S["tables_in"], 16 * len(TABLES))
                dve.wait_ge(*acc.freed(("in", l, 5, NT - 1)))
                q3 = proj[:, :, O_NQ:O_KV]
                k4 = proj[:, :, O_KV + 256:O_KV + 768].rearrange("p t (b n) -> p t b n", b=2)[:, :, :, 0:P]
                sq = nsq.rearrange("p (t n) -> p t n", t=NT)
                tt(sq, q3, q3, ALU.mult).then_inc(own, 1)
                dve.wait_ge(own, ln.made(own))
                ssv = ss[:, 4:24].rearrange("p (t n) -> p t n", t=NT)
                v.tensor_reduce(ss[:, 4:16].rearrange("p (t h) -> p t h", t=NT), sq.rearrange("p t (h d) -> p t h d", d=HD), AX_X, ALU.add).then_inc(own, 1)
                dve.wait_ge(own, ln.made(own))
                sk4 = sk.rearrange("p (t b n) -> p t b n", t=NT, b=2)
                for t in range(NT):
                    tt(sk4[:, t], k4[:, t], k4[:, t], ALU.mult).then_inc(own, 1)
                    dve.wait_ge(own, ln.made(own))
                v.tensor_reduce(ss[:, 16:24], sk.rearrange("p (q d) -> p q d", d=HD), AX_X, ALU.add).then_inc(S["head_sums"], 1)
                dve.wait_ge(S["head_sums"], ln.made(S["head_sums"]))
                dve.wait_ge(*wk.freed(("aT", l, 1)))
                for j in range(2):
                    for g in range(2):
                        src = aT[:, j, g, :]
                        win = bass.AP(src.tensor, src.offset, [list(src.ap[0]), [1, CMP_LEN], [CMP_STRIDE, NCMP]])
                        to = S["blocks_ready"] if j and g else own
                        tt(blk[:, j, :, g * NCMP:(g + 1) * NCMP], win, over(peT[:, 2 * l + j, :], NCMP), ALU.add).then_inc(to, 1)
                        dve.wait_ge(to, ln.made(to))
                split_low(1)
                dve.wait_ge(S["head_scale"], ln.next(S["head_scale"]))
                for t in range(NT):
                    qv = qn[:, t, :].rearrange("p (q g d) -> p g q d", q=HPG, g=2)
                    src = proj[:, t, O_NQ:O_KV].rearrange("p (g q d) -> p g q d", q=HPG, g=2)
                    tt(qv, src, over(rs[:, 4 + t * NH:4 + (t + 1) * NH].rearrange("p (g q) -> p g q", g=2), HD), ALU.mult).then_inc(own, 1)
                    dve.wait_ge(own, ln.made(own))
                    stt(qn[:, t, :].rearrange("p (h d) -> p h d", d=HD), qn[:, t, :].rearrange("p (h d) -> p h d", d=HD), HD ** -0.5,
                                across(gains[:, l, 0, :], 1, NH), ALU.mult, ALU.mult).then_inc(own, 1)
                    dve.wait_ge(own, ln.made(own))
                    kv_ = kn[:, t, :].rearrange("p (b g d) -> p b g d", b=2, g=2)
                    tt(kv_, k4[:, t].rearrange("p b (g d) -> p b g d", g=2),
                               over(rs[:, 16 + 4 * t:20 + 4 * t].rearrange("p (b g) -> p b g", b=2), HD), ALU.mult).then_inc(own, 1)
                    dve.wait_ge(own, ln.made(own))
                    to = S["nsa_rows"] if t else own
                    tt(kv_, kv_, across(gains[:, l, 2:4, :], 2, 2), ALU.mult).then_inc(to, 1)
                    dve.wait_ge(to, ln.made(to))
                split_low(1)
                def decay_scores(heads_):
                    for h in heads_:
                        dve.wait_ge(*wk.filled(("rs", l, h)))
                        b = wk.bank(("rs", l, h))
                        if h >= 4:
                            dve.wait_ge(S["ret_mixed"], (NH - 1) * l + h - 3)
                        tt(sT[:, h % 4, 0:T], b[:, 0:T], decay[:, h, :], ALU.mult)
                        tt(sT[:, h % 4, T:T + P], b[:, T:T + P], decay[:, h, 0:P], ALU.mult).then_inc(*wk.frees(("rs", l, h)))


                dve.wait_ge(*acc.freed(("in", l, 1, NT - 1)))
                rotate(proj[:, :, 0:2 * RET_W].rearrange("p t (h d) -> p t h d", d=HD), rope[:, :, 0, :], rope[:, :, 1, :], 2 * NH, rtmp)
                dve.sem_inc(S["rotated"], 1)
                dve.wait_ge(*wk.filled(("kc", l)))
                b = wk.bank(("kc", l))
                v.tensor_copy(kc[0:NCMP, :], b[0:NCMP, 0:256]).then_inc(*wk.frees(("kc", l)))
                dve.wait_ge(*wk.freed(("kc", l)))
                tt(kcn[0:NCMP, :], kc[0:NCMP, 0:P], kc[0:NCMP, 0:P], ALU.mult).then_inc(own, 1)
                dve.wait_ge(own, ln.made(own))
                v.tensor_reduce(ss[0:NCMP, 32:34], kcn[0:NCMP, :].rearrange("p (g d) -> p g d", g=2), AX_X, ALU.add).then_inc(S["head_sums"], 1)
                dve.wait_ge(S["head_sums"], ln.made(S["head_sums"]))
                split_low(2)
                dve.wait_ge(S["head_scale"], ln.next(S["head_scale"]))
                kc3 = kcn[0:NCMP, :].rearrange("p (g d) -> p g d", g=2)
                tt(kc3, kc[0:NCMP, 0:P].rearrange("p (g d) -> p g d", g=2), over(rs[0:NCMP, 32:34], HD), ALU.mult).then_inc(own, 1)
                dve.wait_ge(own, ln.made(own))
                tt(kc3, kc3, across(gains[0:NCMP, l, 1, :], 1, 2), ALU.mult).then_inc(S["kc_rows"], 1)
                dve.wait_ge(S["kc_rows"], ln.made(S["kc_rows"]))
                dve.wait_ge(*wk.filled(("kcT", l)))
                b = wk.bank(("kcT", l))
                v.tensor_copy(kTc[:, 0:NCMP], b[:, 0:NCMP]).then_inc(*wk.frees(("kcT", l)))
                if l == 0:
                    dve.wait_ge(S["bias_in"], 16 * NH)
                for g in range(2):
                    dve.wait_ge(*wk.filled(("sc", l, g)))
                    b = wk.bank(("sc", l, g))[:, 0:NT * HPG * 16].rearrange("p (q n) -> p q n", n=16)
                    for t in range(NT):
                        at = (1 - t) * P + CMP_LEN - 1
                        i = tt(s_c[:, t * NH + g * HPG:t * NH + (g + 1) * HPG], b[:, t * HPG:(t + 1) * HPG, 0:NCMP],
                               bias[:, g * HPG:(g + 1) * HPG, at:at + 14 * CMP_STRIDE + 1:CMP_STRIDE], ALU.add)
                        if t == 0:
                            i.then_inc(own, 1)
                            dve.wait_ge(own, ln.made(own))
                        else:
                            i.then_inc(*wk.frees(("sc", l, g)))
                            dve.wait_ge(*wk.freed(("sc", l, g)))
                v.tensor_reduce(nmax[:, 8:20], s_c, AX_X, ALU.max).then_inc(own, 1)
                dve.wait_ge(own, ln.made(own))
                tt(s_c, s_c, over(nmax[:, 8:20], NCMP), ALU.subtract).then_inc(S["cmp_scores"], 1)
                dve.wait_ge(S["cmp_scores"], ln.made(S["cmp_scores"]))
                decay_scores(range(3))
                dve.wait_ge(S["gelu_ready"], ln.next(S["gelu_ready"]))
                zv = proj[:, :, O_GM + GM_W:IN_W]
                tt(vn, zv, zv, ALU.mult).then_inc(own, 1)
                dve.wait_ge(own, ln.made(own))
                v.tensor_reduce(ss[:, 24:32].rearrange("p (t h) -> p t h", t=NT), vn.rearrange("p t (h d) -> p t h d", d=HD), AX_X, ALU.add).then_inc(S["head_sums"], 1)
                dve.wait_ge(S["head_sums"], ln.made(S["head_sums"]))
                dve.wait_ge(S["cmp_exp"], ln.next(S["cmp_exp"]))
                v.tensor_reduce(lsum[:, :, :, 0], s_c, AX_X, ALU.add).then_inc(own, 1)
                dve.wait_ge(own, ln.made(own))
                sc4 = s_c.rearrange("p (t h) n -> p t h n", t=NT)
                tt(sc4, sc4, across(cmask[:], 2, NH), ALU.mult).then_inc(S["cmp_probs"], 1)
                dve.wait_ge(S["cmp_probs"], ln.made(S["cmp_probs"]))
                decay_scores(range(3, NH))
                split_low(1)
                dve.wait_ge(S["head_scale"], ln.next(S["head_scale"]))
                for t in range(NT):
                    tt(vn[:, t, :].rearrange("p (h d) -> p h d", d=HD), zv[:, t, :].rearrange("p (h d) -> p h d", d=HD),
                               over(rs[:, 24 + 4 * t:28 + 4 * t], HD), ALU.mult).then_inc(own, 1)
                    dve.wait_ge(own, ln.made(own))
                dve.wait_ge(*wk.filled(("wsT", l)))
                b = wk.bank(("wsT", l)).rearrange("p (g n) -> p g n", g=4)
                tt(wsT, b, across(triu[:], 1, 4), ALU.mult).then_inc(*wk.frees(("wsT", l)))
                dve.wait_ge(*wk.freed(("wsT", l)))
                dve.sem_inc(S["gm_rows"], 1)
                dve.wait_ge(*acc.freed(("ro", l, NT - 1)))
                ro = rows[:, :, 0:RET_W]
                tt(rsq, ro, ro, ALU.mult).then_inc(own, 1)
                dve.wait_ge(own, ln.made(own))
                v.tensor_reduce(ss[:, 36:48].rearrange("p (t h) -> p t h", t=NT), rsq.rearrange("p t (h d) -> p t h d", d=HD), AX_X, ALU.add).then_inc(S["head_sums"], 1)
                dve.wait_ge(S["head_sums"], ln.made(S["head_sums"]))
                for n in range(NT * NH):
                    t, h = n // NH, n % NH
                    K = P * (t + 1)
                    dve.wait_ge(*wk.filled(("s", l, n)))
                    b = wk.bank(("s", l, n)).rearrange("p (b n) -> p b n", b=2)[:, :, 0:K]
                    if n >= 4:
                        dve.wait_ge(*wk.filled(("pT", l, n - 4)))
                    s = probs[n % 4].rearrange("p (b n) -> p b n", b=2)[:, :, 0:K]
                    tt(s, b, across(bias[:, h, (1 - t) * P:(1 - t) * P + K], 1, 2), ALU.add).then_inc(*wk.frees(("s", l, n)))
                    dve.wait_ge(*wk.freed(("s", l, n)))
                    v.tensor_reduce(nmax[:, 2 * (n % 4):2 * (n % 4) + 2], s, AX_X, ALU.max, negate=True).then_inc(S["scores_ready"], 1)
                    if n == 1:
                        dve.wait_ge(*acc.filled(("gm", l)))
                        g_ = acc.bank(("gm", l)).rearrange("p (g t n) -> p g t n", g=4, t=NT)
                        for g in range(4):
                            dst = rows[:, :, 2 * RET_W + g * HD:2 * RET_W + (g + 1) * HD]
                            i = stt(dst, g_[:, g], vecs[:, 0, V_GMB + 4 * l + g:V_GMB + 4 * l + g + 1], proj[:, :, O_GM + g * HD:O_GM + (g + 1) * HD], ALU.add, ALU.mult)
                            if g < 3:
                                i.then_inc(own, 1)
                                dve.wait_ge(own, ln.made(own))
                            else:
                                i.then_inc(*acc.frees(("gm", l)))
                                dve.wait_ge(*acc.freed(("gm", l)))
                    if n == 2:
                        dve.wait_ge(S["head_scale"], ln.next(S["head_scale"]))
                        dve.wait_ge(S["silu_ready"], ln.next(S["silu_ready"]))
                        for t_ in range(NT):
                            r3 = ro[:, t_, :].rearrange("p (h d) -> p h d", d=HD)
                            tt(r3, r3, over(rs[:, 36 + NH * t_:36 + NH * (t_ + 1)], HD), ALU.mult).then_inc(own, 1)
                            dve.wait_ge(own, ln.made(own))
                        tt(ro, ro, proj[:, :, O_RG:O_NQ], ALU.mult).then_inc(own, 1)
                        dve.wait_ge(own, ln.made(own))
                    if n == 3:
                        dve.wait_ge(S["gates_ready"], ln.next(S["gates_ready"]))
                        ts(gate, gate, 0.5, 0.5, ALU.mult, ALU.add).then_inc(own, 1)
                        dve.wait_ge(own, ln.made(own))
                    if n == NH + LAG:
                        combine(l, 0)
                    if n in (8, 10):
                        split_low(1)
                combine(l, 1)
                mixed_low(l)
                split_low(2)
                add_mix(l, 0)
                split_low(1)
                add_mix(l, 1)
                ffn(("ffn", l), l, V_FFN + KC * l)
            for r in range(2):
                for key_, dst in (("bbT", bbT), ("cT", cT)):
                    dve.wait_ge(*wk.filled((key_, r)))
                    b = wk.bank((key_, r))
                    if key_ == "cT" and r == 0:
                        ts(cT[:, 2].rearrange("p i n -> p (i n)"), b, -1.0, None, ALU.mult).then_inc(own, 1)
                        dve.wait_ge(own, ln.made(own))
                    v.tensor_copy(dst[:, r].rearrange("p i n -> p (i n)"), b).then_inc(*wk.frees((key_, r)))
                    dve.wait_ge(*wk.freed((key_, r)))

            into_hT(("mix", 2), V_MIX2)
            split_low(3)
            v.memset(ones, 1.0).then_inc(own, 1)
            dve.wait_ge(own, ln.made(own))
            ts(small2[:, 8:12], vecs[:, 0, V_GLU:V_GLU + 4], 0.5, None, ALU.mult).then_inc(own, 1)
            dve.wait_ge(own, ln.made(own))
            dve.wait_ge(*acc.freed(("even", 1, 1)))
            for h in range(HG):
                ts(lf[:, h, :], lf[:, h, :], lbt[:, 12 + h:13 + h], lbt[:, 8 + h:9 + h], ALU.mult, ALU.add).then_inc(own, 1)
                made = ln.made(own)
            dve.wait_ge(own, made)
            ts(key, lf, -1.0, 1.0, ALU.mult, ALU.add).then_inc(S["hg_forget"], 1)
            dve.wait_ge(S["hg_forget"], ln.made(S["hg_forget"]))
            split_low(1)
            dve.wait_ge(S["hg_ln"], ln.next(S["hg_ln"]))
            for h in range(HG):
                for n in range(NCH):
                    c = slice(n * HC, (n + 1) * HC)
                    i = v.tensor_tensor_scan(bcum[:, h, c], ones, lf[:, h, c], 0.0, ALU.mult, ALU.add)
            i.then_inc(S["hg_cum"], 1)
            dve.wait_ge(S["hg_cum"], ln.made(S["hg_cum"]))
            chunks = lambda m: m.rearrange("p h n -> p (h n)").rearrange("p (q c) -> p q c", c=HC)
            tt(chunks(lf), over(chunks(bcum)[:, :, HC - 1], HC), chunks(bcum), ALU.subtract).then_inc(S["hg_cum"], 1)
            dve.wait_ge(S["hg_cum"], ln.made(S["hg_cum"]))
            split_low(3)
            dve.wait_ge(*acc.freed(("even", 0, 1)))
            dve.wait_ge(S["hg_exp"], ln.next(S["hg_exp"]))
            dec = small2[:, 16:32]
            v.tensor_copy(dec, chunks(eb)[:, :, HC - 1]).then_inc(own, 1)
            dve.wait_ge(own, ln.made(own))
            tt(eb, eb, qTe, ALU.mult).then_inc(own, 1)
            dve.wait_ge(own, ln.made(own))
            tt(bcum, bcum, key, ALU.mult).then_inc(S["hg_q"], 1)
            dve.wait_ge(S["hg_q"], ln.made(S["hg_q"]))
            dve.wait_ge(S["hg_exp"], ln.next(S["hg_exp"]))
            tt(key, key, lf, ALU.mult).then_inc(S["hg_kk"], 1)
            dve.wait_ge(S["hg_kk"], ln.made(S["hg_kk"]))
            split_low(2)
            dve.wait_ge(*wk.filled(("att",)))
            b = wk.bank(("att",)).rearrange("p (q n) -> p q n", n=HC)
            tt(att, b, across(tri64[:], 1, NT * HG), ALU.mult).then_inc(*wk.frees(("att",)))
            dve.wait_ge(*wk.freed(("att",)))
            dve.sem_inc(S["hg_att"], 1)
            for n in range(NCH - 1):
                dve.wait_ge(*wk.filled(("ds", n)))
                b = wk.bank(("ds", n)).rearrange("p (h n) -> p h n", h=HG)
                if n == 0:
                    v.tensor_copy(state[:, 0], b).then_inc(*wk.frees(("ds", n)))
                    dve.wait_ge(*wk.freed(("ds", n)))
                else:
                    for h in range(HG):
                        i = stt(state[:, n, h, :], state[:, n - 1, h, :], dec[:, h * NCH + n:h * NCH + n + 1], b[:, h, :], ALU.mult, ALU.add)
                        if h < HG - 1:
                            i.then_inc(own, 1)
                            dve.wait_ge(own, ln.made(own))
                        else:
                            i.then_inc(*wk.frees(("ds", n)))
                            dve.wait_ge(*wk.freed(("ds", n)))
                dve.sem_inc(S["hg_state"], 1)
            dve.wait_ge(S["table_done"], ln.next(S["table_done"]))
            def s5_rows(q):
                dve.wait_ge(*acc.filled(("sy", q)))
                b = acc.bank(("sy", q))
                stt(uT[:, q, :], uT[:, q, :], vecs[:, 0, V_SD + q:V_SD + q + 1], b[:, 0:T], ALU.mult, ALU.add).then_inc(*acc.frees(("sy", q)))

            for q in range(4):
                co, si = cosT[:, 4 * q:4 * q + 4, :], sinT[:, 4 * q:4 * q + 4, :]
                A, B, C, E_ = turns[q % 2]
                if q >= 2:
                    s5_rows(q - 2)
                for j in range(4):
                    dve.wait_ge(*wk.filled(("bu", q, j)))
                re, im = work[:, 0:4, 0:T], work[:, 0:4, T:2 * T]
                tt(A, co, re, ALU.mult).then_inc(own, 1)
                tt(B, si, im, ALU.mult).then_inc(own, 1)
                tt(C, co, im, ALU.mult).then_inc(own, 1)
                made = [ln.made(own) for _ in range(3)]
                for j in range(4):
                    tt(E_[:, j, :], si[:, j, :], work[:, j, 0:T], ALU.mult).then_inc(*wk.frees(("bu", q, j)))
                dve.wait_ge(own, made[1])
                tt(A, A, B, ALU.add).then_inc(own, 1)
                for j in range(4):
                    dve.wait_ge(*wk.freed(("bu", q, j)))
                tt(C, C, E_, ALU.subtract).then_inc(own, 1)
                made = [ln.made(own) for _ in range(2)]
                for m, w, z in ((0, A, B), (1, C, E_)):
                    dve.wait_ge(own, made[m])
                    for j in range(4):
                        f = mag[:, 4 * q + j:4 * q + j + 1].to_broadcast([P, T])
                        i = v.tensor_tensor_scan(z[:, j, :], f, w[:, j, :], 0.0, ALU.mult, ALU.add)
                    i.then_inc(S["scanned"], 1)
                if q == 0:
                    dve.wait_ge(*acc.freed(("eo", NT - 1)))
                    dve.wait_ge(S["silu_ready"], ln.next(S["silu_ready"]))
                    tt(rows[:, :, 0:512], rows[:, :, 0:512], eg[:, :, 512:1024], ALU.mult).then_inc(S["mixed"], 1)
                    dve.wait_ge(S["mixed"], ln.made(S["mixed"]))
                if q == 2:
                    for t in range(NT):
                        dve.wait_ge(*wk.filled(("eT", t)))
                        b = wk.bank(("eT", t)).rearrange("p (k n) -> p k n", k=4)
                        tt(stage[:, t, :].rearrange("p (k n) -> p k n", k=4), b, over(vecs[:, 0, V_HG:V_HG + 4], P), ALU.mult).then_inc(*wk.frees(("eT", t)))
                if q == 3:
                    for t in range(NT):
                        c = (slice(None), slice(0, 4), slice(t * P, (t + 1) * P))
                        dve.wait_ge(S["hT_high"], ln.next(S["hT_high"]))
                        tt(hTl[c], stage[:, t, :].rearrange("p (k n) -> p k n", k=4), hTh[c], ALU.subtract).then_inc(S["hT_ready"], 1)
                        dve.wait_ge(S["hT_ready"], ln.made(S["hT_ready"]))
            dve.wait_ge(S["scanned"], 8)
            tt(C, co, E_, ALU.mult).then_inc(own, 1)
            dve.wait_ge(own, ln.made(own))
            tt(E_, si, E_, ALU.mult).then_inc(S["last_turned"], 1)
            s5_rows(2)
            s5_rows(3)
            dve.wait_ge(*wk.filled(("glu", 3)))
            for q in range(2):
                dve.wait_ge(*wk.freed(("glu", 2 * q + 1)))
                h = slice(2 * q, 2 * q + 2)
                stt(zT[:, h], qTe[:, h], 1.0, zT[:, h], ALU.add, ALU.mult).then_inc(S["z_gated"], 1)
            for q in range(2):
                h, c = slice(2 * q, 2 * q + 2), slice(4 + 2 * q, 6 + 2 * q)
                dve.wait_ge(S["hT_high"], ln.next(S["hT_high"]))
                stt(hTl[:, c, :], zT[:, h], 0.5, hTh[:, c, :], ALU.mult, ALU.subtract).then_inc(S["hT_ready"], 1)
                dve.wait_ge(S["hT_ready"], ln.made(S["hT_ready"]))
            split_low(3)
            add_mix(2, 0)
            split_low(1)
            add_mix(2, 1)
            v.tensor_copy(mst[:, 48:50], posi[:]).then_inc(own, 1)
            dve.wait_ge(own, ln.made(own))
            for t in range(NT):
                ts(mang[:, 0, t, :], freq[:], mst[:, 48 + t:49 + t], None, ALU.mult).then_inc(own, 1)
                dve.wait_ge(own, ln.made(own))
            ts(mang[:, 1], mang[:, 0], 1.0 / TWO_PI, MAGIC, ALU.mult, ALU.add).then_inc(own, 1)
            dve.wait_ge(own, ln.made(own))
            ts(mang[:, 1], mang[:, 1], -MAGIC, None, ALU.add).then_inc(own, 1)
            dve.wait_ge(own, ln.made(own))
            for c in (CW1, CW2, CW3):
                stt(mang[:, 0], mang[:, 1], -c, mang[:, 0], ALU.mult, ALU.add).then_inc(own, 1)
                dve.wait_ge(own, ln.made(own))
            ts(mang[:, 0], mang[:, 0], PI_SAFE, -PI_SAFE, ALU.min, ALU.max).then_inc(S["pos_arg"], 1)
            dve.wait_ge(S["pos_arg"], ln.made(S["pos_arg"]))
            ffn(("ffn", 2), 2, V_FFN2)

            into_hT(("mix", 3), V_MIX2 + KC)
            dve.wait_ge(*acc.freed(("odd", 0, NT - 1)))
            dve.wait_ge(S["lat_scale"], ln.next(S["lat_scale"]))
            for t in range(NT):
                i = ts(oin[:, t, 0:MQ], oin[:, t, 0:MQ], rs[:, 4 + t:5 + t], None, ALU.mult)
            i.then_inc(S["cq_rows"], 1)
            for t in range(NT):
                c = slice(t * P, (t + 1) * P)
                dve.wait_ge(*wk.filled(("oT", t, 0)))
                b = wk.bank(("oT", t, 0))[:, 0:MQ].rearrange("p (c n) -> p c n", c=3)
                tt(cqT[:, :, c], b, over(vecs[:, 0, V_MQ:V_MQ + 3], P), ALU.mult).then_inc(*wk.frees(("oT", t, 0)))
                dve.wait_ge(*wk.freed(("oT", t, 0)))
                dve.sem_inc(S["odd_T"], 1)
            dve.wait_ge(*acc.freed(("odd", 1, NT - 1)))
            dve.wait_ge(S["pos_trig"], ln.next(S["pos_trig"]))
            cos, sin = mang[:, 2], mang[:, 3]
            rotate(oin[:, :, MQ + MKV:].rearrange("p t (h d) -> p t h d", h=1), cos, sin, 1, [mtmp[:, k, 0:NT * 32] for k in range(4)])
            for k in range(2):
                v.tensor_copy(kr[:, :, k * MR:(k + 1) * MR], oin[:, :, MQ + MKV:]).then_inc(own, 1)
                dve.wait_ge(own, ln.made(own))
            dve.wait_ge(S["lat_scale"], ln.next(S["lat_scale"]))
            for t in range(NT):
                i = ts(oin[:, t, MQ:MQ + MKV], oin[:, t, MQ:MQ + MKV], rs[:, 6 + t:7 + t], None, ALU.mult)
            i.then_inc(S["odd_rows"], 1)
            for t in range(NT):
                c = slice(t * P, (t + 1) * P)
                dve.wait_ge(*wk.filled(("oT", t, 1)))
                b = wk.bank(("oT", t, 1))
                tt(ckvT[:, :, c], b[:, 0:MKV].rearrange("p (c n) -> p c n", c=2), over(vecs[:, 0, V_MKV:V_MKV + 2], P), ALU.mult).then_inc(own, 1)
                dve.wait_ge(own, ln.made(own))
                v.tensor_copy(krT[:, c], b[:, MKV:MKV + P]).then_inc(*wk.frees(("oT", t, 1)))
                dve.wait_ge(*wk.freed(("oT", t, 1)))
                dve.sem_inc(S["odd_T"], 1)
            for q in range(4):
                dve.wait_ge(*acc.freed(("qr", q)))
            rotate(qr.rearrange("p t (h d) -> p t h d", h=MH), cos, sin, MH, [mtmp[:, k, :] for k in range(4)])
            dve.sem_inc(S["qrope_rows"], 1)
            for n in range(NT * MH + 1):
                if n < NT * MH:
                    K = P * (n // MH + 1)
                    dve.wait_ge(*wk.filled(("ms", n)))
                    b = wk.bank(("ms", n))[:, 0:K]
                    if n >= 4:
                        dve.wait_ge(S["m_probs"], n - 3)
                    s_ = ms[:, n % 4, 0:K]
                    stt(s_, b, MQK ** -0.5, causal[:, T - K:T], ALU.mult, ALU.add).then_inc(*wk.frees(("ms", n)))
                    dve.wait_ge(*wk.freed(("ms", n)))
                    v.tensor_reduce(mst[:, n:n + 1], s_, AX_X, ALU.max, negate=True).then_inc(S["m_scores"], 1)
                if n >= 1:
                    m = n - 1
                    K = P * (m // MH + 1)
                    dve.wait_ge(S["m_probs"], ln.next(S["m_probs"]))
                    v.reciprocal(mst[:, 32 + m:33 + m], mst[:, 16 + m:17 + m]).then_inc(own, 1)
                    dve.wait_ge(own, ln.made(own))
                    ts(mp[:, m % 4, 0:K], mp[:, m % 4, 0:K], mst[:, 32 + m:33 + m], None, ALU.mult).then_inc(S["m_norm"], 1)
                if n in (8, 10, 12):
                    split_low(1)
            for t in range(NT):
                for q in range(2):
                    c = (slice(None), slice(4 * q, 4 * q + 4), slice(t * P, (t + 1) * P))
                    b = acc.bank(("mo", t, q)).rearrange("p (k n) -> p k n", k=4)
                    dve.wait_ge(S["hT_high"], ln.next(S["hT_high"]))
                    tt(hTl[c], b, hTh[c], ALU.subtract).then_inc(*acc.frees(("mo", t, q)))
            split_low(2)
            add_mix(3, 0)
            split_low(1)
            add_mix(3, 1)
            ffn(("ffn", 3), 3, V_FFN2 + KC)
            dve.wait_ge(S["mla_in"], 16)
            for t in range(NT):
                dve.wait_ge(S["norm_scale"], ln.next(S["norm_scale"]))
                stt(rows[:, t, :], x[:, t, :], rs[:, t:t + 1], fg, ALU.mult, ALU.mult).then_inc(S["out_rows"], 1)

        @block.sync
        def _(sp):
            xv = a["x"].rearrange("b (t p) d -> p (b t) d", p=P)
            sp.dma_start(x[:], xv).then_inc(S["x_in"], 16)
            sp.dma_start(ident[:], a["const_ident"]).then_inc(S["ident_in"], 16)
            for dst, src in VECTORS:
                sp.dma_start(dst, src, allow_slow_non_contiguous=True).then_inc(S["vectors_in"], 16)
            for k, (name, slot, _, _) in enumerate(W.pieces):
                if k == 1:
                    for dst, src in P1:
                        sp.dma_start(dst, src, allow_slow_non_contiguous=True).then_inc(S["params_in"], 16)
                if k == NRAW:
                    for dst, src in TABLES:
                        sp.dma_start(dst, src, allow_slow_non_contiguous=True).then_inc(S["tables_in"], 16)
                if k >= NRAW:
                    sp.wait_ge(*W.pieces[k - NRAW][3])
                n, loads = man[name]
                for dst, src in loads:
                    sp.dma_start(dst(wraw[:, slot, 0:n]), src).then_inc(W.landed[slot], 16)
            ov = out.rearrange("b (t p) d -> p (b t) d", p=P)
            for t in range(NT):
                sp.wait_ge(S["out_rows"], t + 1)
                sp.dma_start(ov[:, t, :], rows[:, t, :]).then_inc(S["stored"], 16)
            sp.wait_ge(S["stored"], 16 * NT)


_INS = """x attn_norm w_in w_out nsa_q_gain nsa_k_gain cmp_pe cmp_w1 cmp_w2 gm_ws gm_b ffn_norm w_gate_up w_down rel_bias
    positions_2 norm_mix_g_2 norm_ffn_g_2 final_norm_g_2 even_w_in_2 hgrn_lb_logits_2 hgrn_norm_g_2 s5_a_re_2 s5_a_im_2
    s5_log_dt_2 s5_b_re_2 s5_b_im_2 s5_c_re_2 s5_c_im_2 s5_d_2 s5_w_glu_2 s5_b_glu_2 even_w_out_2 odd_w_in_2 mla_q_norm_g_2
    mla_w_uq_2 mla_kv_norm_g_2 mla_w_ukv_2 odd_w_out_2 ffn_w_in_2 ffn_conv_w_2 ffn_conv_b_2 ffn_w_out_2""".split()


def kernel(**inputs):
    import concourse.bacc as bacc
    from concourse.bass_utils import run_bass_kernel_spmd

    nc = bacc.Bacc("TRN2", target_bir_lowering=False, num_devices=1)
    arrays, aps = {}, {}
    for name in _INS:
        v = np.ascontiguousarray(inputs[name])
        arrays["in_" + name] = v
        aps[name] = nc.dram_tensor("in_" + name, v.shape, mybir.dt.from_np(v.dtype), kind="ExternalInput").ap()
    for name, v in shape_constants().items():
        v = np.ascontiguousarray(v)
        arrays[name] = v
        aps[name] = nc.dram_tensor(name, v.shape, F32, kind="ExternalInput").ap()
    out = nc.dram_tensor("out", (1, T, D), F32, kind="ExternalOutput").ap()
    build(nc, aps, out)
    r = run_bass_kernel_spmd(nc, [arrays], core_ids=[0])
    return r.results[0]["out"]
```
